# Optimizing a Trainium2 kernel written in Bass

```python
import math
import jax, jax.numpy as jnp
from jax import lax
import numpy as np

D_MODEL = 1024
BATCH = 1
SEQ = 512
DEPTH = 2

GRID_W = 64
NUM_MIXERS = 2
HEAD_DIM = 64
MIX_WIDTH = D_MODEL
A_HEADS = MIX_WIDTH // HEAD_DIM
A_WIN_ROWS = 8
A_WIN_COLS = 16
B_Q_HEADS = MIX_WIDTH // HEAD_DIM
B_KV_HEADS = 4
B_QBLK = 128
ROPE_THETA = 10000.0
ROPE_SECTION = HEAD_DIM // 2
PLE_DIM = 256
NORM_EPS = 1e-6


def rms_norm(x, g):
    xf = x.astype(jnp.float32)
    y = xf * lax.rsqrt(jnp.mean(xf * xf, axis=-1, keepdims=True) + NORM_EPS)
    return (y * g.astype(jnp.float32)).astype(x.dtype)

def _na_indices(rows):
    win_r = min(A_WIN_ROWS, rows)
    win_c = A_WIN_COLS
    r = np.arange(rows)
    c = np.arange(GRID_W)
    rs = np.clip(r - win_r // 2, 0, rows - win_r)
    cs = np.clip(c - win_c // 2, 0, GRID_W - win_c)
    key_r = rs[:, None] + np.arange(win_r)[None, :]
    key_c = cs[:, None] + np.arange(win_c)[None, :]
    idx = key_r[:, None, :, None] * GRID_W + key_c[None, :, None, :]
    idx = idx.reshape(rows, GRID_W, win_r * win_c).astype(np.int32)
    dr = (key_r - r[:, None] + (A_WIN_ROWS - 1)).astype(np.int32)
    dc = (key_c - c[:, None] + (A_WIN_COLS - 1)).astype(np.int32)
    return idx, dr, dc

def mixer_a(h, w_in, rpb, w_out):
    b, s, _ = h.shape
    rows = s // GRID_W
    idx_np, dr, dc = _na_indices(rows)
    nk = idx_np.shape[-1]
    proj = h @ w_in
    q, k, v, gate = jnp.split(proj, 4, axis=-1)
    to_heads = lambda t: t.reshape(b, s, A_HEADS, HEAD_DIM).transpose(0, 2, 1, 3)
    q, k, v = to_heads(q), to_heads(k), to_heads(v)
    bias = rpb[:, dr[:, None, :, None], dc[None, :, None, :]]
    bias = bias.reshape(A_HEADS, rows, GRID_W, nk).transpose(1, 0, 2, 3)
    q_blk = q.reshape(b, A_HEADS, rows, GRID_W, HEAD_DIM).transpose(2, 0, 1, 3, 4)
    idx = jnp.asarray(idx_np)
    scale = 1.0 / math.sqrt(HEAD_DIM)

    def row_block(args):
        qb, ib, bb = args
        flat = ib.reshape(-1)
        kg = jnp.take(k, flat, axis=2).reshape(b, A_HEADS, GRID_W, nk, HEAD_DIM)
        vg = jnp.take(v, flat, axis=2).reshape(b, A_HEADS, GRID_W, nk, HEAD_DIM)
        sc = jnp.einsum('bhqd,bhqnd->bhqn', qb, kg).astype(jnp.float32) * scale
        sc = sc + bb.astype(jnp.float32)[None]
        pr = jax.nn.softmax(sc, axis=-1).astype(vg.dtype)
        return jnp.einsum('bhqn,bhqnd->bhqd', pr, vg)

    o = lax.map(row_block, (q_blk, idx, bias))
    o = o.transpose(1, 0, 3, 2, 4).reshape(b, s, MIX_WIDTH)
    return (o * jax.nn.silu(gate)) @ w_out

def _axial_rope(seq):
    t = jnp.arange(seq)
    row = (t // GRID_W).astype(jnp.float32)
    col = (t % GRID_W).astype(jnp.float32)
    n_freq = ROPE_SECTION // 2
    inv = jnp.power(ROPE_THETA, -jnp.arange(n_freq, dtype=jnp.float32) * 2.0 / ROPE_SECTION)
    ang_r = row[:, None] * inv[None, :]
    ang_c = col[:, None] * inv[None, :]
    return jnp.cos(ang_r), jnp.sin(ang_r), jnp.cos(ang_c), jnp.sin(ang_c)

def _rotate(x, cos, sin):
    x1, x2 = jnp.split(x, 2, axis=-1)
    return jnp.concatenate([x1 * cos - x2 * sin, x2 * cos + x1 * sin], axis=-1)

def _apply_axial_rope(x, tabs):
    cos_r, sin_r, cos_c, sin_c = tabs
    xf = x.astype(jnp.float32)
    xr = _rotate(xf[..., :ROPE_SECTION], cos_r, sin_r)
    xc = _rotate(xf[..., ROPE_SECTION:], cos_c, sin_c)
    return jnp.concatenate([xr, xc], axis=-1).astype(x.dtype)

def mixer_b(h, w_in, q_norm_g, k_norm_g, w_out):
    b, s, _ = h.shape
    group = B_Q_HEADS // B_KV_HEADS
    kv_w = B_KV_HEADS * HEAD_DIM
    proj = h @ w_in
    q, k, v, gate = jnp.split(proj, [MIX_WIDTH, MIX_WIDTH + kv_w, MIX_WIDTH + 2 * kv_w], axis=-1)
    q = rms_norm(q.reshape(b, s, B_Q_HEADS, HEAD_DIM), q_norm_g).transpose(0, 2, 1, 3)
    k = rms_norm(k.reshape(b, s, B_KV_HEADS, HEAD_DIM), k_norm_g).transpose(0, 2, 1, 3)
    v = v.reshape(b, s, B_KV_HEADS, HEAD_DIM).transpose(0, 2, 1, 3)
    tabs = _axial_rope(s)
    q = _apply_axial_rope(q, tabs)
    k = _apply_axial_rope(k, tabs)
    nb = s // B_QBLK
    q_blk = q.reshape(b, B_KV_HEADS, group, nb, B_QBLK, HEAD_DIM).transpose(3, 0, 1, 2, 4, 5)
    scale = 1.0 / math.sqrt(HEAD_DIM)

    def q_block(qb):
        sc = jnp.einsum('bkgqd,bksd->bkgqs', qb, k).astype(jnp.float32) * scale
        pr = jax.nn.softmax(sc, axis=-1).astype(v.dtype)
        return jnp.einsum('bkgqs,bksd->bkgqd', pr, v)

    o = lax.map(q_block, q_blk)
    o = o.transpose(1, 0, 4, 2, 3, 5).reshape(b, s, MIX_WIDTH)
    return (o * jax.nn.silu(gate)) @ w_out

def first_inputs(seed: int = 0) -> dict:
    key = jax.random.key(seed)
    ks = jax.random.split(key, 16)
    n_a = (DEPTH + NUM_MIXERS - 1) // NUM_MIXERS
    n_b = DEPTH // NUM_MIXERS
    kv_w = B_KV_HEADS * HEAD_DIM
    b_in_w = 2 * MIX_WIDTH + 2 * kv_w
    nrm = lambda k, shape, fan: jax.random.normal(k, shape, jnp.float32) * (fan ** -0.5)
    gain = lambda k, shape: 1.0 + 0.05 * jax.random.normal(k, shape, jnp.float32)
    return {
        "x": jax.random.normal(ks[0], (BATCH, SEQ, D_MODEL), jnp.float32),
        "p": jax.random.normal(ks[1], (DEPTH, BATCH, SEQ, PLE_DIM), jnp.float32),
        "norm_g": gain(ks[2], (DEPTH, D_MODEL)),
        "a_w_in": nrm(ks[3], (n_a, D_MODEL, 4 * MIX_WIDTH), D_MODEL),
        "a_rpb": 0.1 * jax.random.normal(ks[4], (n_a, A_HEADS, 2 * A_WIN_ROWS - 1, 2 * A_WIN_COLS - 1), jnp.float32),
        "a_w_out": nrm(ks[5], (n_a, MIX_WIDTH, D_MODEL), MIX_WIDTH),
        "b_w_in": nrm(ks[6], (n_b, D_MODEL, b_in_w), D_MODEL),
        "b_q_norm": gain(ks[7], (n_b, HEAD_DIM)),
        "b_k_norm": gain(ks[8], (n_b, HEAD_DIM)),
        "b_w_out": nrm(ks[9], (n_b, MIX_WIDTH, D_MODEL), MIX_WIDTH),
        "ple_norm_g": gain(ks[10], (DEPTH, D_MODEL)),
        "ple_w_gate": nrm(ks[11], (DEPTH, D_MODEL, D_MODEL), D_MODEL),
        "ple_w_proj": nrm(ks[12], (DEPTH, PLE_DIM, D_MODEL), PLE_DIM),
        "final_norm_g": gain(ks[13], (D_MODEL,)),
    }

def first_block(x, p, norm_g, a_w_in, a_rpb, a_w_out, b_w_in, b_q_norm, b_k_norm,
              b_w_out, ple_norm_g, ple_w_gate, ple_w_proj, final_norm_g):
    for i in range(DEPTH):
        h = rms_norm(x, norm_g[i])
        j = i // NUM_MIXERS
        if i % NUM_MIXERS == 0:
            y = mixer_a(h, a_w_in[j], a_rpb[j], a_w_out[j])
        else:
            y = mixer_b(h, b_w_in[j], b_q_norm[j], b_k_norm[j], b_w_out[j])
        x = x + y
        g = jax.nn.sigmoid(rms_norm(x, ple_norm_g[i]) @ ple_w_gate[i])
        x = x + g * (p[i] @ ple_w_proj[i])
    return rms_norm(x, final_norm_g)


DEPTH_2 = 1

NSA_HEADS = 8
NSA_KV = 2
NSA_REP = NSA_HEADS // NSA_KV
RWKV_HEADS = 8
NSA_WIDTH = NSA_HEADS * HEAD_DIM
RWKV_WIDTH = RWKV_HEADS * HEAD_DIM
MIX_WIDTH_2 = NSA_WIDTH + RWKV_WIDTH
KV_WIDTH = NSA_KV * HEAD_DIM
ROPE_DIM = HEAD_DIM // 4
ROPE_THETA_2 = 500000.0
CMP_BLOCK = 32
CMP_STRIDE = 16
CMP_HIDDEN = 256
SEL_BLOCK = 64
SEL_TOPK = 8
WINDOW = 512
Q_BLOCK = 128
DECAY_RANK = 64
ICLR_RANK = 64
RWKV_SHIFT_WIDTH = 3 * RWKV_WIDTH + DECAY_RANK + ICLR_RANK
IN_SIZES = (NSA_WIDTH, KV_WIDTH, KV_WIDTH, KV_WIDTH, KV_WIDTH, KV_WIDTH, KV_WIDTH,
            3 * NSA_HEADS, NSA_WIDTH, RWKV_SHIFT_WIDTH, RWKV_WIDTH)
IN_WIDTH = sum(IN_SIZES)
SCALE = HEAD_DIM ** -0.5
RMS_EPS = 1e-6
GN_EPS = 64e-5
NEG_INF = -1e30
FORCE_BONUS = 1e3


def _split(h, sizes):
    idx = np.cumsum(sizes)[:-1].tolist()
    return jnp.split(h, idx, axis=-1)

def rms_norm_2(x, g):
    xf = x.astype(jnp.float32)
    y = xf * lax.rsqrt(jnp.mean(xf * xf, axis=-1, keepdims=True) + RMS_EPS)
    return (y * g.astype(jnp.float32)).astype(x.dtype)

def partial_rope(t, pos):
    half = ROPE_DIM // 2
    inv = ROPE_THETA_2 ** (-jnp.arange(half, dtype=jnp.float32) / half)
    ang = pos.astype(jnp.float32)[:, None] * inv[None, :]
    cos, sin = jnp.cos(ang), jnp.sin(ang)
    tr = t[..., :ROPE_DIM].astype(jnp.float32)
    t1, t2 = tr[..., :half], tr[..., half:]
    rot = jnp.concatenate([t1 * cos - t2 * sin, t2 * cos + t1 * sin], axis=-1).astype(t.dtype)
    return jnp.concatenate([rot, t[..., ROPE_DIM:]], axis=-1)

def masked_softmax(s, mask):
    s = jnp.where(mask, s.astype(jnp.float32), NEG_INF)
    p = jax.nn.softmax(s, axis=-1)
    return jnp.where(mask, p, 0.0)

def compress_blocks(kv, pos_emb, w1, w2):
    B, G, S, D = kv.shape
    ch = kv.reshape(B, G, S // CMP_STRIDE, CMP_STRIDE, D)
    blk = jnp.concatenate([ch[:, :, :-1], ch[:, :, 1:]], axis=3) + pos_emb
    flat = blk.reshape(B, G, -1, CMP_BLOCK * D)
    return jax.nn.silu(flat @ w1) @ w2

def cmp_to_sel_matrix(n_cmp, n_sel):
    c0 = np.arange(n_cmp)[:, None] * CMP_STRIDE
    s0 = np.arange(n_sel)[None, :] * SEL_BLOCK
    ov = np.clip(np.minimum(c0 + CMP_BLOCK, s0 + SEL_BLOCK) - np.maximum(c0, s0), 0, None)
    return jnp.asarray(ov / CMP_BLOCK, dtype=jnp.float32)

def nsa_mixer(q, kc, vc, ks, vs, kw, vw, gate_logits,
              pos_k, w1_k, w2_k, pos_v, w1_v, w2_v):
    B, S, _ = q.shape
    n_cmp = S // CMP_STRIDE - 1
    n_sel = S // SEL_BLOCK
    top_n = min(SEL_TOPK, n_sel)
    n_qb = S // Q_BLOCK
    pos = jnp.arange(S)
    f32 = jnp.float32
    qh = q.reshape(B, S, NSA_KV, NSA_REP, HEAD_DIM).transpose(0, 2, 3, 1, 4)

    def kvh(t):
        return t.reshape(B, S, NSA_KV, HEAD_DIM).transpose(0, 2, 1, 3)

    k_cmp = compress_blocks(kvh(kc), pos_k, w1_k, w2_k)
    v_cmp = compress_blocks(kvh(vc), pos_v, w1_v, w2_v)
    s_cmp = jnp.einsum('bgrsd,bgcd->bgrsc', qh, k_cmp) * SCALE
    cmp_end = jnp.arange(n_cmp) * CMP_STRIDE + CMP_BLOCK - 1
    p_cmp = masked_softmax(s_cmp, cmp_end[None, :] <= pos[:, None])
    o_cmp = jnp.einsum('bgrsc,bgcd->bgrsd', p_cmp, v_cmp.astype(f32))

    imp = jnp.einsum('bgrsc,cj->bgsj', p_cmp, cmp_to_sel_matrix(n_cmp, n_sel))
    t_blk = (pos // SEL_BLOCK)[:, None]
    j = jnp.arange(n_sel)[None, :]
    forced = ((j == 0) | (j == t_blk) | (j == t_blk - 1)).astype(f32)
    imp = jnp.where(j <= t_blk, imp + FORCE_BONUS * forced, -1.0)
    _, sel_idx = lax.top_k(imp, top_n)

    q_rot = partial_rope(qh, pos)
    ks_blk = partial_rope(kvh(ks), pos).reshape(B, NSA_KV, n_sel, SEL_BLOCK, HEAD_DIM)
    vs_blk = kvh(vs).reshape(B, NSA_KV, n_sel, SEL_BLOCK, HEAD_DIM)
    pad = ((0, 0), (0, 0), (WINDOW, 0), (0, 0))
    kw_pad = jnp.pad(partial_rope(kvh(kw), pos), pad)
    vw_pad = jnp.pad(kvh(vw), pad)
    bi = jnp.arange(B)[:, None, None, None]
    gi = jnp.arange(NSA_KV)[None, :, None, None]
    n_tok = top_n * SEL_BLOCK

    def block_fn(qb):
        q0 = qb * Q_BLOCK
        tq = q0 + jnp.arange(Q_BLOCK)
        qc = lax.dynamic_slice_in_dim(q_rot, q0, Q_BLOCK, axis=3)
        idx = lax.dynamic_slice_in_dim(sel_idx, q0, Q_BLOCK, axis=2)
        k_g = ks_blk[bi, gi, idx].reshape(B, NSA_KV, Q_BLOCK, n_tok, HEAD_DIM)
        v_g = vs_blk[bi, gi, idx].reshape(B, NSA_KV, Q_BLOCK, n_tok, HEAD_DIM)
        k_pos = (idx[..., None] * SEL_BLOCK + jnp.arange(SEL_BLOCK)).reshape(B, NSA_KV, Q_BLOCK, n_tok)
        s_sel = jnp.einsum('bgrqd,bgqmd->bgrqm', qc, k_g) * SCALE
        p_sel = masked_softmax(s_sel, (k_pos <= tq[:, None])[:, :, None])
        o_sel = jnp.einsum('bgrqm,bgqmd->bgrqd', p_sel, v_g.astype(f32))
        kwc = lax.dynamic_slice_in_dim(kw_pad, q0, WINDOW + Q_BLOCK, axis=2)
        vwc = lax.dynamic_slice_in_dim(vw_pad, q0, WINDOW + Q_BLOCK, axis=2)
        w_pos = q0 - WINDOW + jnp.arange(WINDOW + Q_BLOCK)
        diff = tq[:, None] - w_pos[None, :]
        w_mask = (diff >= 0) & (diff < WINDOW) & (w_pos[None, :] >= 0)
        s_win = jnp.einsum('bgrqd,bgkd->bgrqk', qc, kwc) * SCALE
        p_win = masked_softmax(s_win, w_mask)
        o_win = jnp.einsum('bgrqk,bgkd->bgrqd', p_win, vwc.astype(f32))
        return o_sel, o_win

    o_sel, o_win = lax.map(block_fn, jnp.arange(n_qb))

    def unblock(o):
        return o.transpose(1, 2, 3, 0, 4, 5).reshape(B, NSA_KV, NSA_REP, S, HEAD_DIM)

    g = jax.nn.sigmoid(gate_logits.astype(f32)).reshape(B, S, NSA_KV, NSA_REP, 3).transpose(0, 2, 3, 1, 4)
    o = g[..., 0:1] * o_cmp + g[..., 1:2] * unblock(o_sel) + g[..., 2:3] * unblock(o_win)
    return o.transpose(0, 3, 1, 2, 4).reshape(B, S, NSA_WIDTH)

def rwkv7_step(state, inp):
    r_t, w_t, k_t, v_t, kk_t, a_t = inp
    sa = jnp.einsum('bhvk,bhk->bhv', state, -kk_t)
    state = (state * w_t[:, :, None, :] + sa[..., None] * (kk_t * a_t)[:, :, None, :]
             + v_t[..., None] * k_t[:, :, None, :])
    y = jnp.einsum('bhvk,bhk->bhv', state, r_t)
    return state, y

def rwkv7_mixer(p, shift_mu, w0, w_up, a0, a_up, k_k, k_a, r_k, gn_w, gn_b):
    B, S, _ = p.shape
    f32 = jnp.float32
    prev = jnp.pad(p, ((0, 0), (1, 0), (0, 0)))[:, :-1]
    p = p + shift_mu * (prev - p)
    r, k, v, wd, ad = _split(p, (RWKV_WIDTH, RWKV_WIDTH, RWKV_WIDTH, DECAY_RANK, ICLR_RANK))
    w = (w0 + jnp.tanh(wd) @ w_up).astype(f32)
    decay = jnp.exp(-jnp.exp(-jax.nn.softplus(-w) - 0.5))
    a = jax.nn.sigmoid((a0 + ad @ a_up).astype(f32))

    def heads(t):
        return t.astype(f32).reshape(B, S, RWKV_HEADS, HEAD_DIM)

    kk = heads(k * k_k)
    kk = kk / jnp.maximum(jnp.sqrt(jnp.sum(kk * kk, axis=-1, keepdims=True)), 1e-12)
    k = k.astype(f32) * (1.0 + (a - 1.0) * k_a)
    rh, kh, vh, wh, ah = heads(r), heads(k), heads(v), heads(decay), heads(a)

    def tm(t):
        return t.transpose(1, 0, 2, 3)

    s0 = jnp.zeros((B, RWKV_HEADS, HEAD_DIM, HEAD_DIM), f32)
    _, y = lax.scan(rwkv7_step, s0, (tm(rh), tm(wh), tm(kh), tm(vh), tm(kk), tm(ah)))
    y = y.transpose(1, 0, 2, 3)
    mean = jnp.mean(y, axis=-1, keepdims=True)
    var = jnp.mean(jnp.square(y - mean), axis=-1, keepdims=True)
    y = (y - mean) * lax.rsqrt(var + GN_EPS)
    y = y * gn_w.reshape(RWKV_HEADS, HEAD_DIM) + gn_b.reshape(RWKV_HEADS, HEAD_DIM)
    y = y + jnp.sum(rh * kh * r_k.reshape(RWKV_HEADS, HEAD_DIM), axis=-1, keepdims=True) * vh
    return y.reshape(B, S, RWKV_WIDTH)

def hybrid_layer(x, norm_g, w_in, cmp_pos_k, cmp_w1_k, cmp_w2_k, cmp_pos_v, cmp_w1_v, cmp_w2_v,
                 shift_mu, decay_w0, decay_up, iclr_a0, iclr_up, k_k, k_a, r_k, gn_w, gn_b, w_out):
    h = rms_norm_2(x, norm_g)
    proj = h @ w_in
    (q, kc, vc, ks, vs, kw, vw, gl, g_nsa, rwkv_in, g_rwkv) = _split(proj, IN_SIZES)
    o_nsa = nsa_mixer(q, kc, vc, ks, vs, kw, vw, gl,
                      cmp_pos_k, cmp_w1_k, cmp_w2_k, cmp_pos_v, cmp_w1_v, cmp_w2_v)
    o_nsa = o_nsa * jax.nn.silu(g_nsa.astype(jnp.float32))
    o_rwkv = rwkv7_mixer(rwkv_in, shift_mu, decay_w0, decay_up, iclr_a0, iclr_up,
                         k_k, k_a, r_k, gn_w, gn_b)
    o_rwkv = o_rwkv * jax.nn.silu(g_rwkv.astype(jnp.float32))
    mix = jnp.concatenate([o_nsa, o_rwkv], axis=-1).astype(x.dtype)
    return x + mix @ w_out

def second_inputs(seed: int = 0) -> dict:
    key = jax.random.key(seed)
    ks = jax.random.split(key, 24)
    f32 = jnp.float32

    def nrm(k, shape, scale):
        return jax.random.normal(k, shape, f32) * scale

    L = DEPTH_2
    return {
        "x": nrm(ks[0], (BATCH, SEQ, D_MODEL), 1.0),
        "norm_g": 1.0 + nrm(ks[1], (L, D_MODEL), 0.05),
        "w_in": nrm(ks[2], (L, D_MODEL, IN_WIDTH), D_MODEL ** -0.5),
        "cmp_pos_k": nrm(ks[3], (L, CMP_BLOCK, HEAD_DIM), 0.1),
        "cmp_w1_k": nrm(ks[4], (L, CMP_BLOCK * HEAD_DIM, CMP_HIDDEN), (CMP_BLOCK * HEAD_DIM) ** -0.5),
        "cmp_w2_k": nrm(ks[5], (L, CMP_HIDDEN, HEAD_DIM), CMP_HIDDEN ** -0.5),
        "cmp_pos_v": nrm(ks[6], (L, CMP_BLOCK, HEAD_DIM), 0.1),
        "cmp_w1_v": nrm(ks[7], (L, CMP_BLOCK * HEAD_DIM, CMP_HIDDEN), (CMP_BLOCK * HEAD_DIM) ** -0.5),
        "cmp_w2_v": nrm(ks[8], (L, CMP_HIDDEN, HEAD_DIM), CMP_HIDDEN ** -0.5),
        "shift_mu": jax.random.uniform(ks[9], (L, RWKV_SHIFT_WIDTH), f32),
        "decay_w0": jax.random.uniform(ks[10], (L, RWKV_WIDTH), f32, -4.0, 1.0),
        "decay_up": nrm(ks[11], (L, DECAY_RANK, RWKV_WIDTH), 0.1 * DECAY_RANK ** -0.5),
        "iclr_a0": nrm(ks[12], (L, RWKV_WIDTH), 0.5),
        "iclr_up": nrm(ks[13], (L, ICLR_RANK, RWKV_WIDTH), 0.5 * ICLR_RANK ** -0.5),
        "k_k": 0.85 + nrm(ks[14], (L, RWKV_WIDTH), 0.05),
        "k_a": 1.0 + nrm(ks[15], (L, RWKV_WIDTH), 0.05),
        "r_k": nrm(ks[16], (L, RWKV_WIDTH), 0.1),
        "gn_w": 1.0 + nrm(ks[17], (L, RWKV_WIDTH), 0.05),
        "gn_b": nrm(ks[18], (L, RWKV_WIDTH), 0.02),
        "w_out": nrm(ks[19], (L, MIX_WIDTH_2, D_MODEL), MIX_WIDTH_2 ** -0.5),
        "final_g": 1.0 + nrm(ks[20], (D_MODEL,), 0.05),
    }

def second_block(x, norm_g, w_in, cmp_pos_k, cmp_w1_k, cmp_w2_k, cmp_pos_v, cmp_w1_v, cmp_w2_v,
              shift_mu, decay_w0, decay_up, iclr_a0, iclr_up, k_k, k_a, r_k, gn_w, gn_b,
              w_out, final_g):
    h = x
    for l in range(DEPTH_2):
        h = hybrid_layer(h, norm_g[l], w_in[l], cmp_pos_k[l], cmp_w1_k[l], cmp_w2_k[l],
                         cmp_pos_v[l], cmp_w1_v[l], cmp_w2_v[l], shift_mu[l], decay_w0[l],
                         decay_up[l], iclr_a0[l], iclr_up[l], k_k[l], k_a[l], r_k[l],
                         gn_w[l], gn_b[l], w_out[l])
    return rms_norm_2(h, final_g)


def setup_inputs(seed=0):
    out = dict(first_inputs(seed))
    for name, value in second_inputs(seed + 1).items():
        if name != "x":
            out[name + "_2"] = value
    return out


def reference(
    x, p, norm_g, a_w_in, a_rpb, a_w_out, b_w_in, b_q_norm, b_k_norm, b_w_out, ple_norm_g,
    ple_w_gate, ple_w_proj, final_norm_g, norm_g_2, w_in_2, cmp_pos_k_2, cmp_w1_k_2, cmp_w2_k_2,
    cmp_pos_v_2, cmp_w1_v_2, cmp_w2_v_2, shift_mu_2, decay_w0_2, decay_up_2, iclr_a0_2,
    iclr_up_2, k_k_2, k_a_2, r_k_2, gn_w_2, gn_b_2, w_out_2, final_g_2,
):
    x = first_block(
        x, p, norm_g, a_w_in, a_rpb, a_w_out, b_w_in, b_q_norm, b_k_norm, b_w_out, ple_norm_g,
        ple_w_gate, ple_w_proj, final_norm_g,
    )
    return second_block(
        x, norm_g_2, w_in_2, cmp_pos_k_2, cmp_w1_k_2, cmp_w2_k_2, cmp_pos_v_2, cmp_w1_v_2,
        cmp_w2_v_2, shift_mu_2, decay_w0_2, decay_up_2, iclr_a0_2, iclr_up_2, k_k_2, k_a_2,
        r_k_2, gn_w_2, gn_b_2, w_out_2, final_g_2,
    )


_drawn_inputs = setup_inputs


def setup_inputs(seed=0):
    import zlib

    import numpy as np

    out = dict(_drawn_inputs(seed))
    spreads = {}
    factors = {'norm_g': 5.456,
     'a_rpb': 6.865,
     'b_q_norm': 8.0,
     'b_k_norm': 8.0,
     'ple_norm_g': 12.869,
     'cmp_pos_k_2': 8.0,
     'cmp_w1_k_2': 3.064,
     'cmp_w2_k_2': 2.768,
     'cmp_pos_v_2': 5.071,
     'decay_up_2': 8.0,
     'k_k_2': 21.249,
     'gn_w_2': 2.815,
     'gn_b_2': 7.459}
    for name, (base, spread) in spreads.items():
        noise = np.random.default_rng([zlib.crc32(name.encode()), seed]).standard_normal(out[name].shape)
        drawn = base * np.exp(spread * noise) if base else spread * noise
        out[name] = __import__('jax').numpy.asarray(drawn.astype(out[name].dtype))
    for name, factor in factors.items():
        out[name] = (out[name] * factor).astype(out[name].dtype)
    return out
```

```python
import math
from contextlib import ExitStack

import numpy as np

import concourse.bass as bass
from concourse import mybir

F32 = mybir.dt.float32
BF16 = mybir.dt.bfloat16
I32 = mybir.dt.int32
ALU = mybir.AluOpType
ACT = mybir.ActivationFunctionType
X = mybir.AxisListType.X

P = 128
D = 1024
T = 512
NT = T // P
KB = D // P
HD = 64
GW, GR = 64, 8
CT = GW // NT
NEG = -1e30
EPS = 1e-6
GN_EPS = 64e-5
NBANK = 8
NSLOT = 3
CH = 64
LOGC = math.exp(-0.5)
RSQRT_MAGIC = float(0x5F3759DF)


def constants():
    parts, at, n = [], {}, 0

    def add(name, a):
        nonlocal n
        a = np.asarray(a, np.float64).reshape(P, -1).astype(np.float32)
        at[name] = (n, a.shape[1])
        n += a.shape[1]
        parts.append(a)

    p = np.arange(P)
    cq, r = p // GR, p % GR
    add("ident", np.eye(P))
    j = np.repeat(np.arange(32), GR)
    mid = (j[None] >= cq[:, None]) & (j[None] <= cq[:, None] + 15)
    edge = np.where(cq[:, None] < 8, j[None] >= 16, j[None] < 16)
    add("nbr", np.concatenate([np.where(mid, 0, NEG), np.where(edge, 0, NEG)], 1))
    inv = 10000.0 ** (-np.arange(16) * 2.0 / 32)
    cos, sin = np.zeros((P, NT, 2, 2, 16)), np.zeros((P, NT, 2, 2, 16))
    for i in range(NT):
        for s, pos in ((0, r), (1, CT * i + cq)):
            ang = pos[:, None] * inv[None]
            for hf in range(2):
                cos[:, i, s, hf] = np.cos(ang)
                sin[:, i, s, hf] = np.sin(ang) * (-1 if hf == 0 else 1)
    add("ropeb", np.concatenate([cos.reshape(P, NT * HD), sin.reshape(P, NT * HD)], 1))
    inv2 = 500000.0 ** (-np.arange(8) / 8.0)
    pos = (np.arange(NT)[None] * P + p[:, None])[..., None] * inv2
    add("cos2", np.cos(pos))
    add("sin2", np.sin(pos))
    c = np.arange(32)
    ok = (c[None, None] * 16 + 31 <= (np.arange(NT)[None] * P + p[:, None])[..., None]) & (c < 31)
    add("cmpneg", np.where(ok, 0, NEG))
    add("cmpok", ok)
    add("causal", np.where(p[None] > p[:, None], NEG, 0))
    s, t = p[:, None], p[None]
    same, same16 = s // CH == t // CH, s // 16 == t // 16
    add("a16", (s < t) & same16)
    add("e16", (s < t) & same & ~same16)
    add("gram", np.concatenate([(s <= t) & same, (s < t) & same, (s <= t) & same], 1))
    add("chunk", np.tile((np.arange(T) % CH != 0), (P, 1)))
    add("heads", np.stack([p < HD, p >= HD], 1))
    add("ident64", np.tile(np.eye(HD), (2, 1)))
    return np.concatenate(parts, 1), at


CST, CAT = constants()


def program(nc, A, out, stop=None):
    ctx = ExitStack()
    with ctx:
        def sb(name, shape, dt=F32):
            return ctx.enter_context(nc.sbuf_tensor(name, shape, dt))

        def sem(name):
            return ctx.enter_context(nc.semaphore(name))

        x = sb("x", [P, NT, D])
        hT = sb("hT", [P, KB, T])
        ring = sb("ring", [P, NSLOT, KB * 512])
        cst = sb("cst", [P, CST.shape[1]])
        vrow = sb("vrow", [P, P])
        vec = sb("vec", [P, P])
        stat = sb("stat", [P, 640])
        identb = sb("identb", [P, P], BF16)
        causalb = sb("causalb", [P, P], BF16)
        w2 = sb("w2", [P, 2, 2, HD])
        wa = sb("wa", [P, 512])
        NARENA = 28000
        arena = sb("arena", [P, NARENA])
        bank = [ctx.enter_context(nc.psum_tensor(f"bank{b}", [P, 512], F32)) for b in range(NBANK)]
        scratch = nc.dram_tensor("rpb_rows", [16, 1024], F32, kind="Internal").ap()

        def C(name):
            o, n = CAT[name]
            return cst[:, o:o + n]

        def ap(base, dims, off=0):
            return bass.AP(base.tensor, base.offset + off, [list(base.ap[0])] + [list(d) for d in dims])

        def area(o, n):
            assert o + n <= NARENA
            return arena[:, o:o + n]

        ident = C("ident")

        rows, V0 = [], {}
        for name, src in (("norm0", A["norm_g"][0:1]), ("norm1", A["norm_g"][1:2]),
                          ("ple0", A["ple_norm_g"][0:1]), ("ple1", A["ple_norm_g"][1:2]),
                          ("norm2", A["norm_g_2"]), ("mu", A["shift_mu_2"]), ("w0", A["decay_w0_2"]),
                          ("a0", A["iclr_a0_2"]), ("kk", A["k_k_2"]), ("ka", A["k_a_2"]), ("rk", A["r_k_2"]),
                          ("gnw", A["gn_w_2"]), ("gnb", A["gn_b_2"]),
                          ("posk", A["cmp_pos_k_2"].rearrange("a b c -> a (b c)")),
                          ("posv", A["cmp_pos_v_2"].rearrange("a b c -> a (b c)"))):
            n = src.shape[1] // P
            V0[name] = sum(m for _, m in rows)
            rows.append((src.rearrange("a (j p) -> (a j) p", p=P), n))
        NV = sum(m for _, m in rows)
        assert NV <= P

        def vcol(name, j=0, n=1):
            return vec[:, V0[name] + j:V0[name] + j + n]

        chunks, CI = [], {}

        def chunk(name, src, shape):
            CI[name] = len(chunks)
            chunks.append((src, shape))

        def cols(w, a, b):
            return w.rearrange("(k p) n -> p k n", p=P)[:, :, a:b]

        for n in range(8):
            chunk(("A", n), cols(A["a_w_in"][0], 512 * n, 512 * n + 512), (KB, 512))
        for n in range(2):
            chunk(("AO", n), cols(A["a_w_out"][0], 512 * n, 512 * n + 512), (KB, 512))

        def ple_chunks(l):
            for n in range(2):
                chunk(("PG", l, n), cols(A["ple_w_gate"][l], 512 * n, 512 * n + 512), (KB, 512))
            chunk(("PP", l), cols(A["ple_w_proj"][l], 0, D), (2, D))

        ple_chunks(0)
        for n in range(5):
            chunk(("B", n), cols(A["b_w_in"][0], 512 * n, 512 * n + 512), (KB, 512))
        for n in range(2):
            chunk(("BO", n), cols(A["b_w_out"][0], 512 * n, 512 * n + 512), (KB, 512))
        ple_chunks(1)
        CCOL = [(0, 512), (512, 1024), (1024, 1304), (1304, 1816), (1816, 2328), (2328, 2840), (2840, 3352),
                (3352, 3480), (3480, 3992)]
        for n in range(4):
            chunk(("C", n), cols(A["w_in_2"][0], *CCOL[n]), (KB, CCOL[n][1] - CCOL[n][0]))
        chunk("W1K", cols(A["cmp_w1_k_2"][0], 0, 256), (16, 256))
        chunk("W1V", cols(A["cmp_w1_v_2"][0], 0, 256), (16, 256))
        for n in range(4, 9):
            chunk(("C", n), cols(A["w_in_2"][0], *CCOL[n]), (KB, CCOL[n][1] - CCOL[n][0]))
        for n in range(2):
            chunk(("CO", n), cols(A["w_out_2"][0], 512 * n, 512 * n + 512), (KB, 512))
        wave_slot = CI[("C", 8)] % NSLOT
        assert wave_slot not in (CI[("CO", 0)] % NSLOT, CI[("CO", 1)] % NSLOT)

        def W(name):
            n = CI[name]
            k, m = chunks[n][1]
            return ring[:, n % NSLOT, 0:k * m].rearrange("p (k m) -> p k m", k=k)

        filled = sem("filled")
        drained = {"a": sem("drained_by_scalar"), "v": sem("drained_by_vector")}
        weights = [sem(f"weights{i}") for i in range(NSLOT)]
        s_x = [sem(f"x_loaded{i}") for i in range(NT)]
        s_cst = sem("constants_loaded")
        s_vrow = sem("vectors_loaded")
        s_small = sem("small_weights_loaded")
        s_p = [sem(f"p_loaded{l}") for l in range(2)]
        s_gb = [sem(f"gain_rows_loaded{l}") for l in range(3)]
        s_rpb = sem("rpb_loaded")
        s_rpbr = sem("rpb_reversed")
        s_scr = sem("rpb_scratch_written")
        s_ext = [sem(f"bias_rows_loaded{i}") for i in range(2)]
        s_bias = sem("bias_ready")
        s_v = sem("vector_chain")
        s_out = sem("out_written")
        made = {}

        def S(name):
            if name not in made:
                made[name] = sem(name)
            return made[name]

        order, J, who, nth, count = [], {}, {}, {}, {"a": 0, "v": 0}

        def take(eng, key):
            eng.wait_ge(filled, J[key] + 1)
            return bank[J[key] % NBANK]

        given = {"a": 0, "v": 0}

        def give(ins, key):
            given[who[key]] += 1
            assert nth[key] == given[who[key]], (key, nth[key], given)
            ins.then_inc(drained[who[key]], 1)

        def evacuated(eng, key):
            eng.wait_ge(drained[who[key]], nth[key])

        qT = area(0, 4096).rearrange("p (j t) -> p j t", j=8)
        kT = area(4096, 4096).rearrange("p (j t) -> p j t", j=8)
        va = area(8192, 4096).rearrange("p (i n) -> p i n", i=NT)
        G = area(12288, 4096).rearrange("p (j t) -> p j t", j=8)
        xn = area(16384, 2048).rearrange("p (b d) -> p b d", b=2)
        th = area(18432, 1024).rearrange("p (b d) -> p b d", b=2)
        ext = area(19456, 1024).rearrange("p (b d) -> p b d", b=2)
        bias = area(20480, 1024).rearrange("p (b d) -> p b d", b=2)
        sA = area(21504, 2048).rearrange("p (b d) -> p b d", b=2)
        pA = area(23552, 2048).rearrange("p (b d) -> p b d", b=2)
        ptA = area(16384, 3072).rearrange("p (b h d) -> p b h d", b=3, h=2)
        rpb_in = area(24576, 480)
        rrev = area(19456, 1024)[0:16, :]
        junk = area(25976, 1024)
        p_tm = area(20480, 1024).rearrange("p (i n) -> p i n", i=NT)
        p_T = area(21504, 1024).rearrange("p (k t) -> p k t", k=2)
        thp = area(22528, 2048).rearrange("p (b d) -> p b d", b=4)
        tp = area(24576, 1024).rearrange("p (b d) -> p b d", b=2)
        kTB = area(4096, 2048).rearrange("p (g t) -> p g t", g=4)
        vB = area(6144, 1024).rearrange("p (i n) -> p i n", i=NT)
        tabq = area(7168, 512).rearrange("p (s n) -> p s n", s=2)
        tabk = area(7680, 512).rearrange("p (s n) -> p s n", s=2)
        gqk = area(8192, 128)
        kB = area(8320, 1024).rearrange("p (i n) -> p i n", i=NT)
        qB = area(19456, 4096).rearrange("p (i n) -> p i n", i=NT)
        t1B = area(23552, 1024)
        t2B = area(24576, 1024)
        sqB = area(25600, 1024).rearrange("p (b d) -> p b d", b=2)
        tkB = area(9344, 512)
        kD = area(9856, 2048).rearrange("p (i n) -> p i n", i=NT)
        ptB = area(19456, 4096).rearrange("p (b k t) -> p b k t", b=2, k=4)
        pB = area(23552, 1536).rearrange("p (b d) -> p b d", b=3)
        gb = area(0, 1024)
        xo = area(0, 4096).rearrange("p (i d) -> p i d", i=NT)
        gb2 = area(4096, 1024)
        q2 = area(0, 2048).rearrange("p (i n) -> p i n", i=NT)
        q2r = area(2048, 2048).rearrange("p (i n) -> p i n", i=NT)
        qTp = area(4096, 2048).rearrange("p (j t) -> p j t", j=4)
        qTr = area(6144, 2048).rearrange("p (j t) -> p j t", j=4)
        kz = area(8192, 4096).rearrange("p (b g e t) -> p b g e t", b=2, g=2, e=2)
        vS = area(12288, 1024).rearrange("p (i b n) -> p i b n", i=NT, b=2)
        gt = area(14432, 96).rearrange("p (i n) -> p i n", i=NT)
        pTc = area(14528, 1024).rearrange("p (g t) -> p g t", g=2)
        fl = area(15552, 2048).rearrange("p (b n) -> p b n", b=2)
        hid = area(17600, 256).rearrange("p (b n) -> p b n", b=2)
        thh = area(17856, 128)
        kcz = area(17984, 128).rearrange("p (g e c) -> p g e c", g=2, e=2)
        vcz = area(18112, 512).rearrange("p (g r d) -> p g r d", g=2, r=4)
        pN = area(18624, 1536).rearrange("p (b n) -> p b n", b=3)
        ptN = [area(20160, 4096).rearrange("p (b k t) -> p b k t", b=2, k=4),
               area(0, 4096).rearrange("p (b k t) -> p b k t", b=2, k=4)]
        rt = area(20160, 1024).rearrange("p (b n) -> p b n", b=4)
        kd = area(21184, 2048).rearrange("p (i b n) -> p i b n", i=NT, b=2)
        smC = area(24256, 512).rearrange("p (b n) -> p b n", b=2)
        Gn = area(24768, 2048).rearrange("p (j t) -> p j t", j=4)
        thC = area(26816, 1024).rearrange("p (b n) -> p b n", b=2)
        mixA = area(15552, 2048).rearrange("p (j t) -> p j t", j=4)
        def four(o):
            return area(o, 2048).rearrange("p (j t) -> p j t", j=4)

        rF, kF, vF, Gr = four(0), four(2048), four(4096), four(6144)
        raw = area(8192, 1539).rearrange("p (b n) -> p b n", b=3)
        wdad = area(9732, 512)
        dif = area(10244, 1024).rearrange("p (b n) -> p b n", b=2)
        yF = four(11268)
        lw, cum, iP, aF, kk = four(13316), four(17600), four(19648), four(21696), four(23744)
        sq = four(8192)
        bx = area(8192, 2048)
        AR = hT[:, :, :].rearrange("p (j i) t -> p (j i t)", j=4).rearrange("p (j i a t) -> p j i a t", j=4, i=4, a=2)
        wslot = ring[:, wave_slot, :]
        B3 = wslot[:, 0:3072].rearrange("p (h m t) -> p h m t", h=8, m=3)
        Dm = wslot[:, 3072:4096].rearrange("p (h t) -> p h t", h=8)
        AE = area(2048, 2048).rearrange("p (h m t) -> p h m t", h=8, m=2)
        A2 = area(13316, 1024).rearrange("p (h t) -> p h t", h=8)
        D2 = area(14340, 1024).rearrange("p (h t) -> p h t", h=8)
        Qa = area(17600, 1024).rearrange("p (h t) -> p h t", h=8)
        Qb = area(18624, 1024).rearrange("p (h t) -> p h t", h=8)
        XG = area(23744, 1024).rearrange("p (h t) -> p h t", h=8)
        HG = area(24768, 1024).rearrange("p (h t) -> p h t", h=8)
        btm, ktm, vtm = area(8192, 512), area(8704, 512), area(9216, 512)
        MT = area(9728, 512).rearrange("p (c j k) -> p c j k", c=2, j=4)
        Bm = area(10240, 512).rearrange("p (c n) -> p c n", c=2)
        RHO = area(10752, 512)
        Sst = area(25792, 1024).rearrange("p (b n) -> p b n", b=4)
        mixB = four(13316)
        PC = stat[:, 544:576].rearrange("p (j c) -> p j c", j=4)

        UN = [(h, br, i) for h in range(8) for br in range(2) for i in range(NT)]

        block = ctx.enter_context(nc.Block())
        chunk_last = {}

        @block.tensor
        def _(pe):
            def begin(key, consumer):
                n = len(order)
                if n >= NBANK:
                    evacuated(pe, order[n - NBANK])
                order.append(key)
                J[key], who[key] = n, consumer
                count[consumer] += 1
                nth[key] = count[consumer]
                return bank[n % NBANK]

            def end(ins):
                ins.then_inc(filled, 1)

            def mm(o, l, r, start, stop):
                return nc.tensor.matmul(o, l, r, start=start, stop=stop)

            def need(name):
                n = CI[name]
                pe.wait_ge(weights[n % NSLOT], 16 * (n // NSLOT + 1))

            def used(name):
                chunk_last[CI[name]] = len(order) - 1

            def norm(tag):
                for i in range(NT):
                    pe.wait_ge(S("xn_" + tag), i + 1)
                    for hf in range(2):
                        b = begin((tag, i, hf), "v")
                        for q in range(4):
                            o = (4 * hf + q) * P
                            ins = nc.tensor.transpose(b[:, q * P:(q + 1) * P], xn[:, i % 2, o:o + P], ident)
                        end(ins)
                evacuated(pe, (tag, NT - 1, 1))

            def fm(key, consumer, name, c0, m=P):
                b = begin(key, consumer)
                w = W(name)
                for k in range(KB):
                    ins = mm(b[0:m, :], w[:, k, c0:c0 + m], hT[:, k, :], k == 0, k == KB - 1)
                end(ins)

            def tm(key, consumer, name, i, c0, n, src=None, nk=KB):
                b = begin(key, consumer)
                w, src = W(name), hT if src is None else src
                for k in range(nk):
                    ins = mm(b[:, 0:n], src[:, k, i * P:(i + 1) * P], w[:, k, c0:c0 + n], k == 0, k == nk - 1)
                end(ins)

            def out_proj(tag):
                for n in range(2):
                    need((tag, n))
                    for i in range(NT):
                        tm((tag, n, i), "v", (tag, n), i, 0, 512)
                    used((tag, n))

            def ple(l):
                pe.wait_ge(s_p[l], 16 * NT)
                for k in range(2):
                    b = begin(("pT", l, k), "a")
                    for i in range(NT):
                        ins = nc.tensor.transpose(b[:, i * P:(i + 1) * P], p_tm[:, i, k * P:(k + 1) * P], ident)
                    end(ins)
                norm(f"ple{l}")
                for n in range(2):
                    need(("PG", l, n))
                    if n == 0:
                        need(("PP", l))
                        evacuated(pe, ("pT", l, 1))
                    for i in range(NT):
                        tm(("PG", l, n, i), "a", ("PG", l, n), i, 0, 512)
                        tm(("PP", l, n, i), "v", ("PP", l), i, 512 * n, 512, src=p_T, nk=2)
                    used(("PG", l, n))
                used(("PP", l))

            pe.wait_ge(s_cst, 16)
            pe.wait_ge(S("vrow_zero"), 1)
            pe.wait_ge(s_vrow, 16 * len(rows))
            b = begin("vec", "a")
            end(nc.tensor.transpose(b[:, 0:P], vrow[:, :], ident))

            norm("norm0")
            for n in range(8):
                need(("A", n))
                if n in (4, 5):
                    for i in range(NT):
                        tm(("Av", n, i), "a", ("A", n), i, 0, 512)
                else:
                    for s in range(4):
                        fm(("A", n, s), "a" if n < 4 else "v", ("A", n), s * P)
                used(("A", n))

            def scoresA(h):
                e, j = 64 * (h % 2), h // 2
                q = qT[e:e + 64, j, :]
                k = kT[e:e + 64, j, :]
                for hf in range(2):
                    b = begin(("AS", h, hf), "v")
                    for m in range(2):
                        t = 2 * hf + m
                        l = q[:, P * t:P * t + P]
                        r = k[:, P * t:P * t + 256] if t < 3 else ap(k, [(384, 2), (1, P)])
                        ins = mm(b[:, m * 256:(m + 1) * 256], l, r, True, True)
                    end(ins)

            def transA(h):
                for hf in range(2):
                    pe.wait_ge(S("A_probs"), 2 * h + hf + 1)
                    b = begin(("AT", h, hf), "a")
                    for m in range(2):
                        for c in range(2):
                            o = (2 * m + c) * P
                            ins = nc.tensor.transpose(b[:, o:o + P], pA[:, h % 2, 512 * hf + o:512 * hf + o + P], ident)
                    end(ins)

            def pvA(h):
                e = 64 * (h % 2)
                evacuated(pe, ("AT", h, 1))
                b = begin(("AO_", h), "v")
                for t in range(4):
                    for c in range(2):
                        kt = (t + c) if t < 3 else 3 * c
                        o = (2 * (t % 2) + c) * P
                        ins = mm(b[e:e + 64, t * P:(t + 1) * P], va[:, kt, h * 64:h * 64 + 64],
                                 ptA[:, h % 3, t // 2, o:o + P], c == 0, c == 1)
                end(ins)

            evacuated(pe, ("A", 3, 3))
            evacuated(pe, ("Av", 5, 3))
            for h in range(16 + 3):
                if h < 16:
                    scoresA(h)
                if h >= 3:
                    pvA(h - 3)
                if 1 <= h < 17:
                    transA(h - 1)
            evacuated(pe, ("AO_", 15))
            pe.wait_ge(S("A_o_mid"), 16)
            out_proj("AO")
            ple(0)

            norm("norm1")
            for n in range(3):
                need(("B", n))
                for i in range(NT):
                    tm(("B", n, i), "a", ("B", n), i, 0, 512)
                used(("B", n))
            for n in (3, 4):
                need(("B", n))
                for s in range(4):
                    fm(("B", n, s), "v", ("B", n), s * P)
                used(("B", n))
            for i in range(NT):
                pe.wait_ge(S("B_rope"), i + 1)
                pe.wait_ge(S("B_rope_k"), i + 1)
                for hf in range(2):
                    b = begin(("BqT", i, hf), "a")
                    for q in range(4):
                        o = (4 * hf + q) * P
                        ins = nc.tensor.transpose(b[:, q * P:(q + 1) * P], qB[:, i, o:o + P], ident)
                    end(ins)
                b = begin(("BkT", i), "a")
                for g in range(4):
                    ins = nc.tensor.transpose(b[:, g * P:(g + 1) * P], kD[:, i, g * P:(g + 1) * P], ident)
                end(ins)
            evacuated(pe, ("BkT", NT - 1))

            NB_ = 16 * NT

            def scoresB(u):
                h, i = divmod(u, NT)
                e = 64 * (h % 2)
                b = begin(("BS", u), "a")
                end(mm(b[:, :], qT[e:e + 64, h // 2, i * P:(i + 1) * P], kTB[e:e + 64, h // 4, :], True, True))

            def transB(u):
                pe.wait_ge(S("B_probs"), u + 1)
                b = begin(("BT", u), "a")
                for k in range(4):
                    ins = nc.tensor.transpose(b[:, k * P:(k + 1) * P], pB[:, u % 3, k * P:(k + 1) * P], ident)
                end(ins)

            def pvB(h):
                e = 64 * (h % 2)
                evacuated(pe, ("BT", NT * h + 3))
                b = begin(("BO_", h), "v")
                for k in range(4):
                    ins = mm(b[e:e + 64, :], vB[:, k, (h // 4) * 64:(h // 4) * 64 + 64], ptB[:, h % 2, k, :],
                             k == 0, k == 3)
                end(ins)

            for u in range(NB_ + 4):
                if u < NB_:
                    scoresB(u)
                if 2 <= u < NB_ + 2:
                    transB(u - 2)
                if u >= 6 and (u - 6) % 4 == 0:
                    pvB((u - 6) // 4)
            evacuated(pe, ("BO_", 15))
            out_proj("BO")
            ple(1)

            if stop:
                return
            norm("norm2")
            need(("C", 0))
            for i in range(NT):
                tm(("C", 0, i), "a", ("C", 0), i, 0, 512)
            used(("C", 0))
            need(("C", 1))
            for n in range(2):
                fm(("kvc", n), "v", ("C", 1), n * P)
            for i in range(NT):
                tm(("C", 1, i), "a", ("C", 1), i, 256, 256)
            used(("C", 1))
            need(("C", 2))
            for i in range(NT):
                tm(("C", 2, i), "a", ("C", 2), i, 0, 280)
            used(("C", 2))
            need(("C", 3))
            for s in range(4):
                fm(("C", 3, s), "v", ("C", 3), s * P)
            used(("C", 3))

            for n, name in enumerate(("W1K", "W1V")):
                need(name)
                pe.wait_ge(S("C_flat"), n + 1)
                b = begin(("hid", n), "v")
                for blk in range(2):
                    for ii in range(16):
                        ins = mm(b[:, blk * 64:blk * 64 + 64], W(name)[:, ii, blk * P:blk * P + P],
                                 fl[:, n, ii * 64:ii * 64 + 64], ii == 0, ii == 15)
                end(ins)
                used(name)
            pe.wait_ge(s_small, 64)
            evacuated(pe, ("hid", 1))
            b = begin("kcmp", "v")
            for blk in range(2):
                ins = mm(b[0:64, 0:64], w2[:, 0, blk, :], hid[:, 0, blk * 64:blk * 64 + 64], blk == 0, blk == 1)
            end(ins)
            b = begin("vcmp", "v")
            for g in range(2):
                for blk in range(2):
                    ins = mm(b[0:32, g * 64:g * 64 + 64], hid[:, 1, blk * 64 + g * 32:blk * 64 + g * 32 + 32],
                             w2[:, 1, blk, :], blk == 0, blk == 1)
            end(ins)
            pe.wait_ge(S("C_rope"), 4)
            for i in range(NT):
                for name, src in (("qp", q2), ("qr", q2r)):
                    b = begin((name, i), "a")
                    for j in range(4):
                        ins = nc.tensor.transpose(b[:, j * P:(j + 1) * P], src[:, i, j * P:(j + 1) * P], ident)
                    end(ins)
                b = begin(("kz", i), "a")
                for m in range(4):
                    ins = nc.tensor.transpose(b[:, m * P:(m + 1) * P], kd[:, i, m // 2, (m % 2) * P:(m % 2) * P + P], ident)
                end(ins)
            evacuated(pe, ("kz", NT - 1))
            pe.wait_ge(S("C_cmp"), 12)
            for i in range(NT):
                b = begin(("cs", i), "v")
                for h in range(8):
                    ins = mm(b[:, h * 32:h * 32 + 32], qTp[:, h // 2, i * P:(i + 1) * P], kcz[:, h // 4, h % 2, :],
                             True, True)
                end(ins)
            for i in range(NT):
                pe.wait_ge(S("C_pc"), i + 1)
                b = begin(("ct", i), "a")
                for g in range(2):
                    ins = nc.tensor.transpose(b[:, g * P:(g + 1) * P], smC[:, i % 2, g * P:(g + 1) * P], ident)
                end(ins)

            def scoresN(u):
                h, br, i = UN[u]
                q = qTr[:, h // 2, i * P:(i + 1) * P]
                k = kz[:, br, h // 4, h % 2, :]
                b = begin(("NS", u), "a")
                if i:
                    mm(b[:, 0:i * P], q, k[:, 0:i * P], True, True)
                d = b[:, i * P:(i + 1) * P]
                mm(d, q, k[:, i * P:(i + 1) * P], True, False)
                end(mm(d, identb[:, :], causalb[:, :], False, True))

            def transN(u):
                h, br, i = UN[u]
                pe.wait_ge(S("N_probs"), u + 1)
                b = begin(("NT", u), "a")
                for k in range(i + 1):
                    ins = nc.tensor.transpose(b[:, k * P:(k + 1) * P], pN[:, u % 3, k * P:(k + 1) * P], ident)
                end(ins)

            def pvN(h):
                e, g = 64 * (h % 2), h // 4
                evacuated(pe, ("NT", 8 * h + 7))
                b = begin(("NO", h), "v")
                mm(b[e:e + 64, :], vcz[:, g, h % 4, :], pTc[:, g, :], True, False)
                for br in range(2):
                    for k in (3, 2, 1, 0):
                        ins = mm(b[e:e + 64, k * P:T], vS[:, k, br, g * 64:g * 64 + 64],
                                 ptN[h % 2][:, br, k, k * P:T], False, br == 1 and k == 0)
                end(ins)

            pe.wait_ge(S("bf16_constants"), 2)
            for u in range(len(UN) + 4):
                if u < len(UN):
                    scoresN(u)
                if 2 <= u < len(UN) + 2:
                    transN(u - 2)
                if u >= 11 and (u - 11) % 8 == 0:
                    pvN((u - 11) // 8)

            for s in range(13):
                n = 4 + s // 4
                if s % 4 == 0:
                    need(("C", n))
                fm(("R", s), "a", ("C", n), (s % 4) * P)
                if s % 4 == 3 or s == 12:
                    used(("C", n))
            need(("C", 8))
            for s in range(4):
                fm(("C", 8, s), "v", ("C", 8), s * P)
            used(("C", 8))
            pe.wait_ge(S("R_twd"), 1)
            for j in range(4):
                b = begin(("W", j), "a")
                end(mm(b[:, :], wa[0:64, j * P:(j + 1) * P], wdad[0:64, :], True, True))
            for j in range(4):
                b = begin(("A_", j), "a")
                end(mm(b[:, :], wa[64:128, j * P:(j + 1) * P], wdad[64:128, :], True, True))

            def head_sums(key, src):
                b = begin(key, "v")
                for i in range(NT):
                    for j in range(4):
                        c = (4 * i + j) * 2
                        ins = mm(b[:, c:c + 2], src[:, j, i * P:(i + 1) * P], C("heads"), True, True)
                end(ins)

            def spread(key, j):
                b = begin((key, j), "v")
                for i in range(NT):
                    o = (4 * i + j) * P
                    ins = nc.tensor.transpose(b[:, i * P:(i + 1) * P], bx[:, o:o + P], ident)
                end(ins)

            pe.wait_ge(S("R_sq"), 4)
            head_sums("ks", sq)
            pe.wait_ge(S("R_kx"), 1)
            for j in range(4):
                spread("kb", j)
            pe.wait_ge(S("R_rk"), 4)
            head_sums("bs", sq)
            pe.wait_ge(S("R_bx"), 1)
            for j in range(4):
                spread("bb", j)

            def four_heads(key, consumer, left, right):
                for bt in range(2):
                    b = begin(key + (bt,), consumer)
                    for q in range(4):
                        h = 4 * bt + q
                        ins = mm(b[:, q * P:(q + 1) * P], left(h), right(h), True, True)
                    end(ins)

            def turned(key, consumer, src):
                for bt in range(2):
                    b = begin(key + (bt,), consumer)
                    for q in range(4):
                        ins = nc.tensor.transpose(b[:, q * P:(q + 1) * P], src(4 * bt + q), ident)
                    end(ins)

            mA, mE, mD = (lambda h: AE[:, h, 0, :]), (lambda h: AE[:, h, 1, :]), (lambda h: Dm[:, h, :])
            mA2, mD2 = (lambda h: A2[:, h, :]), (lambda h: D2[:, h, :])
            mQa, mQb = (lambda h: Qa[:, h, :]), (lambda h: Qb[:, h, :])
            pe.wait_ge(S("R_ops"), 4)
            for i in range(NT):
                ti = slice(i * P, (i + 1) * P)
                for h in range(8):
                    e, j = 64 * (h % 2), h // 2
                    b = begin(("gr", i, h), "v")
                    mm(b[:, 0:256], aF[e:e + 64, j, ti], AR[e:e + 64, j, i, :, :], True, True)
                    end(mm(b[:, 256:512], iP[e:e + 64, j, ti], AR[e:e + 64, j, i, :, :], True, True))
                for n, src in enumerate((lambda j: AR[:, j, i, 0, :], lambda j: aF[:, j, ti], lambda j: iP[:, j, ti],
                                         lambda j: vF[:, j, ti])):
                    b = begin(("tm", i, n), "a")
                    for j in range(4):
                        ins = nc.tensor.transpose(b[:, j * P:(j + 1) * P], src(j), ident)
                    end(ins)
                evacuated(pe, ("gr", i, 7))
                turned(("D", i), "a", mA)
                b = begin(("X", i), "a")
                evacuated(pe, ("tm", i, 3))
                for h in range(8):
                    ins = mm(b[:, h * 64:h * 64 + 64], B3[:, h, 1, :], vtm[:, h * 64:h * 64 + 64], True, True)
                end(ins)
                evacuated(pe, ("D", i, 1))
                four_heads(("A2", i), "a", mD, mA)
                four_heads(("D2", i), "v", mA, mD)
                evacuated(pe, ("A2", i, 1))
                evacuated(pe, ("D2", i, 1))
                four_heads(("Q2", i), "v", mD2, mQa)
                four_heads(("A4", i), "a", mD2, mA2)
                four_heads(("D4", i), "a", mA2, mD2)
                evacuated(pe, ("D4", i, 1))
                evacuated(pe, ("Q2", i, 1))
                four_heads(("Q3", i), "v", mD, mQb)
                four_heads(("D8", i), "a", mA, mD)
                evacuated(pe, ("D8", i, 1))
                evacuated(pe, ("Q3", i, 1))
                four_heads(("Q4", i), "v", mD2, mQa)
                evacuated(pe, ("Q4", i, 1))
                turned(("QT", i), "a", mQb)
                evacuated(pe, ("QT", i, 1))
                four_heads(("KT", i), "a", mE, mA2)
                four_heads(("K", i), "v", mA2, mE)
                evacuated(pe, ("KT", i, 1))
                evacuated(pe, ("K", i, 1))
                four_heads(("K2", i), "a", mA, mD)
                evacuated(pe, ("K2", i, 1))
                four_heads(("Q5", i), "v", mD2, mQb)
                evacuated(pe, ("Q5", i, 1))
                four_heads(("RR", i), "v", mD, mQa)
                evacuated(pe, ("RR", i, 1))
                evacuated(pe, ("X", i))
                four_heads(("HG", i), "a", mQb, lambda h: XG[:, h, :])
                evacuated(pe, ("HG", i, 1))
                b = begin(("rho", i), "v")
                for h in range(8):
                    e, j = 64 * (h % 2), h // 2
                    ins = mm(b[e:e + 64, j * P:(j + 1) * P], HG[:, h, 64:128], B3[:, h, 0, :], True, True)
                end(ins)
                for c in range(2):
                    cs = slice(64 * c, 64 * c + 64)
                    b = begin(("M", i, c), "v")
                    for h in range(8):
                        e, j = 64 * (h % 2), h // 2
                        ins = mm(b[e:e + 64, j * 64:j * 64 + 64], HG[cs, h, 64:128], btm[cs, h * 64:h * 64 + 64], True, True)
                    end(ins)
                for c in range(2):
                    cs = slice(64 * c, 64 * c + 64)
                    b = begin(("Bm", i, c), "a")
                    for h in range(8):
                        e, j = 64 * (h % 2), h // 2
                        o = b[e:e + 64, j * 64:j * 64 + 64]
                        mm(o, btm[cs, h * 64:h * 64 + 64], HG[cs, h, 0:64], True, False)
                        ins = mm(o, ktm[cs, h * 64:h * 64 + 64], vtm[cs, h * 64:h * 64 + 64], False, True)
                    end(ins)
                b = begin(("Y1", i), "a")
                for h in range(8):
                    e, j = 64 * (h % 2), h // 2
                    o = b[e:e + 64, j * P:(j + 1) * P]
                    mm(o, HG[:, h, 0:64], B3[:, h, 0, :], True, False)
                    ins = mm(o, vtm[:, h * 64:h * 64 + 64], B3[:, h, 2, :], False, True)
                end(ins)
                for c in range(2):
                    k = 2 * i + c
                    evacuated(pe, ("M", i, c))
                    pe.wait_ge(S("R_state"), k + 1)
                    b = begin(("St", k), "v")
                    for h in range(8):
                        e, j = 64 * (h % 2), h // 2
                        ins = mm(b[e:e + 64, j * 64:j * 64 + 64], MT[e:e + 64, c, j, :],
                                 Sst[e:e + 64, k % 4, j * 64:j * 64 + 64], True, True)
                    end(ins)
                evacuated(pe, ("rho", i))
                b = begin(("Y2", i), "v")
                for c in range(2):
                    for h in range(8):
                        e, j = 64 * (h % 2), h // 2
                        o = j * P + 64 * c
                        ins = mm(b[e:e + 64, o:o + 64], Sst[e:e + 64, (2 * i + c) % 4, j * 64:j * 64 + 64],
                                 RHO[e:e + 64, o:o + 64], True, True)
                end(ins)

            evacuated(pe, ("Y2", NT - 1))
            head_sums("gn1", yF)
            pe.wait_ge(S("R_gx"), 1)
            for j in range(4):
                spread("gb1", j)
            pe.wait_ge(S("R_gsq"), 4)
            head_sums("gn2", sq)
            pe.wait_ge(S("R_gx"), 2)
            for j in range(4):
                spread("gb2", j)
            pe.wait_ge(S("R_done"), 4)
            for n in range(2):
                need(("CO", n))
                for i in range(NT):
                    b = begin(("CO", n, i), "v")
                    w = W(("CO", n))
                    for k in range(KB):
                        src = mixA[:, k, :] if k < 4 else mixB[:, k - 4, :]
                        ins = mm(b[:, :], src[:, i * P:(i + 1) * P], w[:, k, :], k == 0, k == KB - 1)
                    end(ins)
                used(("CO", n))

        @block.scalar
        def _(act):
            for l in range(NT):
                act.dma_start(x[:, l, :], A["x"][0].rearrange("(r c) d -> c r d", r=GR)[CT * l:CT * l + CT])\
                   .then_inc(s_x[l], 16)

            def copy(o, i, scale=1.0):
                return nc.scalar.activation(o, i, ACT.Copy, scale=scale)

            def squares(tag, ready, col):
                for i in range(NT):
                    ready(i)
                    if i >= 1:
                        act.wait_ge(S("ss_" + tag), i)
                    nc.scalar.activation(junk, x[:, i, :], ACT.Square, accum_out=stat[:, col + i:col + i + 1])\
                      .then_inc(S("ss_" + tag), 1)

            def loaded(i):
                act.wait_ge(s_x[i], 16)

            key = "vec"
            b = take(act, key)
            give(copy(vec[:, :], b[:, 0:P]), key)
            squares("norm0", loaded, 0)
            for n in range(8):
                if n in (4, 5):
                    for i in range(NT):
                        key = ("Av", n, i)
                        b = take(act, key)
                        give(copy(va[:, i, 512 * (n - 4):512 * (n - 3)], b[:, :]), key)
                elif n < 4:
                    for s in range(4):
                        key = ("A", n, s)
                        b = take(act, key)
                        j = (4 * n + s) % 8
                        if n < 2:
                            copy(qT[:, j, 0:448], b[:, 64:512], 0.125)
                            give(copy(qT[:, j, 448:512], b[:, 0:64], 0.125), key)
                        else:
                            give(copy(kT[:, j, :], b[:, :]), key)
                else:
                    for s in range(4):
                        k = 4 * (n - 6) + s
                        b = take(act, ("A", n, s))
                        if k >= 2:
                            act.wait_ge(drained["v"], nth[("A", 6 + (k - 2) // 4, (k - 2) % 4)])
                        nc.scalar.activation(th[:, k % 2, :], b[:, :], ACT.Tanh, scale=0.5).then_inc(S("A_tanh"), 1)

            def expA(h):
                for hf in range(2):
                    act.wait_ge(S("A_max"), 2 * h + hf + 1)
                    if h >= 2:
                        act.wait_ge(filled, J[("AT", h - 2, hf)] + 1)
                    for m in range(2):
                        c = 64 + 8 * (h % 2) + 2 * hf + m
                        o = 512 * hf + 256 * m
                        ins = nc.scalar.activation(pA[:, h % 2, o:o + 256], sA[:, h % 2, o:o + 256], ACT.Exp,
                                                   bias=stat[:, c:c + 1], accum_out=stat[:, c + 16:c + 17])
                    ins.then_inc(S("A_exp"), 1)

            def ptA_copy(h):
                for hf in range(2):
                    key = ("AT", h, hf)
                    b = take(act, key)
                    if h >= 3:
                        act.wait_ge(filled, J[("AO_", h - 3)] + 1)
                    give(copy(ptA[:, h % 3, hf, :], b[:, :]), key)

            for h in range(16 + 1):
                if h < 16:
                    expA(h)
                if h >= 1:
                    ptA_copy(h - 1)

            def ple(l, tag, col, ready):
                for k in range(2):
                    key = ("pT", l, k)
                    b = take(act, key)
                    give(copy(p_T[:, k, :], b[:, :]), key)
                squares(f"ple{l}", ready, col)
                for n in range(2):
                    for i in range(NT):
                        key = ("PG", l, n, i)
                        u = 4 * n + i
                        b = take(act, key)
                        if u >= 4:
                            act.wait_ge(drained["v"], nth[("PP", l, (u - 4) // 4, (u - 4) % 4)])
                        give(nc.scalar.activation(thp[:, u % 4, :], b[:, :], ACT.Tanh, scale=0.5), key)

            ple(0, "AO", 4, lambda i: evacuated(act, ("AO", 1, i)))
            squares("norm1", lambda i: act.wait_ge(S("x_ple"), 4 + i + 1), 8)
            for n in range(3):
                for i in range(NT):
                    key = ("B", n, i)
                    u = 4 * n + i
                    b = take(act, key)
                    if u >= 2:
                        act.wait_ge(S("B_sq_read"), u - 1)
                    w = 512 if n < 2 else 256
                    nc.scalar.activation(sqB[:, u % 2, 0:w], b[:, 0:w], ACT.Square).then_inc(S("B_sq"), 1)
                    if n < 2:
                        give(copy(qB[:, i, 512 * n:512 * n + 512], b[:, :]), key)
                    else:
                        copy(kB[:, i, :], b[:, 0:256])
                        give(copy(vB[:, i, :], b[:, 256:512]), key)
            for n in (3, 4):
                for s in range(4):
                    k = 4 * (n - 3) + s
                    b = take(act, ("B", n, s))
                    if k >= 2:
                        act.wait_ge(drained["v"], nth[("B", 3 + (k - 2) // 4, (k - 2) % 4)])
                    nc.scalar.activation(th[:, k % 2, :], b[:, :], ACT.Tanh, scale=0.5).then_inc(S("B_tanh"), 1)
            for i in range(NT):
                for hf in range(2):
                    key = ("BqT", i, hf)
                    b = take(act, key)
                    give(copy(qT[:, 4 * hf:4 * hf + 4, i * P:(i + 1) * P], b[:, :].rearrange("p (j t) -> p j t", j=4)), key)
                key = ("BkT", i)
                b = take(act, key)
                give(copy(kTB[:, :, i * P:(i + 1) * P], b[:, :].rearrange("p (j t) -> p j t", j=4)), key)

            NB_ = 16 * NT
            for u in range(NB_ + 2):
                if u < NB_:
                    key = ("BS", u)
                    b = take(act, key)
                    act.wait_ge(S("B_max"), u + 1)
                    if u >= 3:
                        act.wait_ge(filled, J[("BT", u - 3)] + 1)
                    c = 128 + u % 4
                    give(nc.scalar.activation(pB[:, u % 3, :], b[:, :], ACT.Exp, bias=stat[:, c:c + 1],
                                              accum_out=stat[:, c + 4:c + 5]), key)
                if u >= 2:
                    v = u - 2
                    h, i = divmod(v, NT)
                    key = ("BT", v)
                    b = take(act, key)
                    if h >= 2:
                        act.wait_ge(filled, J[("BO_", h - 2)] + 1)
                    give(copy(ptB[:, h % 2, :, i * P:(i + 1) * P], b[:, :].rearrange("p (k t) -> p k t", k=4)), key)
            ple(1, "BO", 12, lambda i: evacuated(act, ("BO", 1, i)))
            squares("fin", lambda i: act.wait_ge(S("x_ple"), 8 + 4 + i + 1), 16)
            if stop:
                return
            squares("norm2", lambda i: act.wait_ge(S("x_fin"), i + 1), 20)
            for i in range(NT):
                key = ("C", 0, i)
                b = take(act, key)
                copy(q2[:, i, :], b[:, :])
                give(copy(q2r[:, i, :], b[:, :]), key)
            for n in (1, 2):
                for i in range(NT):
                    key = ("C", n, i)
                    b = take(act, key)
                    if n == 2:
                        nc.scalar.activation(gt[:, i, :], b[:, 256:280], ACT.Tanh, scale=0.5).then_inc(S("C_gates"), 1)
                    copy(ap(kd[:, i, n - 1, :], [(P, 2), (64, 2), (1, 64)]), ap(b[:, 0:P], [(64, 2), (0, 2), (1, 64)]))
                    give(copy(vS[:, i, n - 1, :], b[:, P:256]), key)

            def tanhs(keys, name):
                for k, key in enumerate(keys):
                    b = take(act, key)
                    if k >= 2:
                        evacuated(act, keys[k - 2])
                    nc.scalar.activation(thC[:, k % 2, :], b[:, :], ACT.Tanh, scale=0.5).then_inc(S(name), 1)

            tanhs([("C", 3, s) for s in range(4)], "C_tanh")
            for n in range(2):
                b = take(act, ("hid", n))
                if n:
                    evacuated(act, ("hid", 0))
                nc.scalar.activation(thh, b[:, 0:128], ACT.Tanh, scale=0.5).then_inc(S("C_thh"), 1)
            act.wait_ge(S("C_clear"), 3)
            for i in range(NT):
                for name, dst in (("qp", qTp), ("qr", qTr)):
                    key = (name, i)
                    b = take(act, key)
                    give(copy(dst[:, :, i * P:(i + 1) * P], b[:, :].rearrange("p (j t) -> p j t", j=4), 0.125), key)
                key = ("kz", i)
                b = take(act, key)
                for e in range(2):
                    es = slice(64 * e, 64 * e + 64)
                    ins = copy(ap(kz[es, 0, 0, e, :], [(1024, 4), (1, P)], i * P), b[es, :].rearrange("p (j t) -> p j t", j=4))
                give(ins, key)
            for i in range(NT):
                act.wait_ge(S("C_cs"), i + 1)
                nc.scalar.activation(smC[:, i % 2, :], smC[:, i % 2, :], ACT.Exp).then_inc(S("C_ce"), 1)
                if i >= 1:
                    key = ("ct", i - 1)
                    b = take(act, key)
                    give(copy(pTc[:, :, (i - 1) * P:i * P], b[:, 0:256].rearrange("p (g t) -> p g t", g=2)), key)
            key = ("ct", NT - 1)
            b = take(act, key)
            give(copy(pTc[:, :, (NT - 1) * P:T], b[:, 0:256].rearrange("p (g t) -> p g t", g=2)), key)

            for u in range(len(UN) + 2):
                if u < len(UN):
                    nk = (UN[u][2] + 1) * P
                    key = ("NS", u)
                    b = take(act, key)
                    act.wait_ge(S("N_max"), u + 1)
                    if u >= 3:
                        act.wait_ge(filled, J[("NT", u - 3)] + 1)
                    c = 400 + u % 4
                    give(nc.scalar.activation(pN[:, u % 3, 0:nk], b[:, 0:nk], ACT.Exp, bias=stat[:, c:c + 1],
                                              accum_out=stat[:, c + 4:c + 5]), key)
                if u >= 2:
                    h, br, i = UN[u - 2]
                    key = ("NT", u - 2)
                    b = take(act, key)
                    if h >= 2:
                        act.wait_ge(filled, J[("NO", h - 2)] + 1)
                    give(copy(ptN[h % 2][:, br, 0:i + 1, i * P:(i + 1) * P],
                              b[:, 0:(i + 1) * P].rearrange("p (k t) -> p k t", k=i + 1)), key)

            evacuated(act, ("NO", 7))
            act.wait_ge(S("R_rawzero"), 1)
            for s in range(13):
                key = ("R", s)
                b = take(act, key)
                if s >= 3:
                    act.wait_ge(S("R_mix"), s - 2)
                give(copy(raw[:, s % 3, 1:513], b[:, :]), key)
            tanhs([("C", 8, s) for s in range(4)], "R_tanh")
            act.wait_ge(S("R_mix"), 13)
            nc.scalar.activation(wdad[0:64, :], wdad[0:64, :], ACT.Tanh).then_inc(S("R_twd"), 1)
            act.wait_ge(S("R_half"), 1)
            for j in range(4):
                key = ("W", j)
                b = take(act, key)
                give(nc.scalar.activation(lw[:, j, :], b[:, :], ACT.Tanh, bias=stat[:, 576 + j:577 + j], scale=0.5), key)
            for j in range(4):
                key = ("A_", j)
                b = take(act, key)
                give(nc.scalar.activation(aF[:, j, :], b[:, :], ACT.Tanh, bias=stat[:, 580 + j:581 + j], scale=0.5), key)
            for j in range(4):
                act.wait_ge(S("R_kkraw"), j + 1)
                nc.scalar.activation(sq[:, j, :], kk[:, j, :], ACT.Square).then_inc(S("R_sq"), 1)
            for j in range(4):
                act.wait_ge(S("R_cum"), j + 1)
                nc.scalar.activation(iP[:, j, :], cum[:, j, :], ACT.Exp, scale=-1.0).then_inc(S("R_P"), 1)
                nc.scalar.activation(lw[:, j, :], lw[:, j, :], ACT.Exp).then_inc(S("R_P"), 1)
                nc.scalar.activation(cum[:, j, :], cum[:, j, :], ACT.Exp).then_inc(S("R_P"), 1)

            def move(key, dst):
                b = take(act, key)
                give(copy(dst, b[:, :].rearrange("p (h t) -> p h t", h=4)), key)

            def moves(key, dst):
                for bt in range(2):
                    move(key + (bt,), dst[:, 4 * bt:4 * bt + 4, :])

            def As():
                return AE[:, :, 0, :]

            act.wait_ge(S("R_ops"), 4)
            for i in range(NT):
                key = ("tm", i, 0)
                b = take(act, key)
                give(copy(XG[:, :, 64:128], b[:, :].rearrange("p (h k) -> p h k", h=8)), key)
                for n, dst in ((1, btm), (2, ktm), (3, vtm)):
                    key = ("tm", i, n)
                    b = take(act, key)
                    give(copy(dst, b[:, :]), key)
                moves(("D", i), Dm)
                key = ("X", i)
                b = take(act, key)
                give(copy(XG[:, :, 0:64], b[:, :].rearrange("p (h k) -> p h k", h=8)), key)
                moves(("A2", i), A2)
                moves(("A4", i), As())
                moves(("D4", i), Dm)
                moves(("D8", i), D2)
                moves(("QT", i), A2)
                moves(("KT", i), Dm)
                moves(("K2", i), D2)
                moves(("HG", i), HG)
                for c in range(2):
                    key = ("Bm", i, c)
                    b = take(act, key)
                    if i >= 1:
                        act.wait_ge(S("R_state"), 2 * i + 1)
                    give(copy(Bm[:, c, :], b[:, 0:256]), key)
                key = ("Y1", i)
                b = take(act, key)
                give(copy(yF[:, :, i * P:(i + 1) * P], b[:, :].rearrange("p (j t) -> p j t", j=4)), key)
            for j in range(4):
                act.wait_ge(S("R_centred"), j + 1)
                nc.scalar.activation(sq[:, j, :], yF[:, j, :], ACT.Square).then_inc(S("R_gsq"), 1)
            squares("out", lambda i: evacuated(act, ("CO", 1, i)), 24)

        @block.vector
        def _(dve):
            chain = [0]

            def link(ins):
                chain[0] += 1
                ins.then_inc(s_v, 1)
                dve.wait_ge(s_v, chain[0])

            TT, TS, STT = nc.vector.tensor_tensor, nc.vector.tensor_scalar, nc.vector.scalar_tensor_tensor

            def rsqrt(y, v, t):
                link(TS(y.bitcast(I32), v.bitcast(I32), 1, None, ALU.arith_shift_right))
                link(TS(y.bitcast(I32), y.bitcast(I32), -1.0, RSQRT_MAGIC, ALU.mult, ALU.add))
                for _ in range(3):
                    link(STT(t, y, -0.5, y, ALU.mult, ALU.mult))
                    link(TT(t, t, v, ALU.mult))
                    link(STT(y, t, 1.5, y, ALU.add, ALU.mult))

            def rstd(tag, col, width=D, eps=EPS):
                dve.wait_ge(S("ss_" + tag), NT)
                v = stat[:, col:col + NT]
                link(TS(v, v, 1.0 / width, eps, ALU.mult, ALU.add))
                y = stat[:, 32:32 + NT]
                rsqrt(y, v, stat[:, 36:36 + NT])
                return y

            def norm(tag, col, natural=False):
                y = rstd(tag, col)
                g = vcol(tag, 0, 8)

                def evac(i):
                    for hf in range(2):
                        key = (tag, i, hf)
                        b = take(dve, key)
                        if natural:
                            o = ap(hT[:, 4 * hf, :], [(T, 4), (1, CT), (GW, GR)], CT * i)
                            s = b[:, :].rearrange("p (k c r) -> p k c r", k=4, r=GR)
                            w = ap(g, [(1, 4), (0, CT), (0, GR)], 4 * hf)
                        else:
                            o = hT[:, 4 * hf:4 * hf + 4, i * P:(i + 1) * P]
                            s = b[:, :].rearrange("p (k t) -> p k t", k=4)
                            w = ap(g, [(1, 4), (0, P)], 4 * hf)
                        give(TT(o, s, w, ALU.mult), key)

                for i in range(NT):
                    if i >= 2:
                        dve.wait_ge(filled, J[(tag, i - 2, 1)] + 1)
                    TS(xn[:, i % 2, :], x[:, i, :], y[:, i:i + 1], None, ALU.mult).then_inc(S("xn_" + tag), 1)
                    if i >= 1:
                        evac(i - 1)
                evac(NT - 1)

            nc.vector.memset(vrow[64:P, :], 0.0).then_inc(S("vrow_zero"), 1)
            nc.vector.memset(rrev, 0.0).then_inc(s_rpbr, 1)
            dve.wait_ge(s_rpb, 16)
            dve.wait_ge(s_rpbr, 1)
            nc.vector.tensor_copy(ap(rrev, [(-64, 15), (-1, 31)], 1007), rpb_in[0:16, 0:465].rearrange(
                "p (a b) -> p a b", a=15)).then_inc(s_rpbr, 1)
            dve.wait_ge(s_cst, 16)
            nc.vector.tensor_copy(identb[:, :], ident).then_inc(S("bf16_constants"), 1)
            nc.vector.tensor_copy(causalb[:, :], C("causal")).then_inc(S("bf16_constants"), 1)
            evacuated(dve, "vec")
            norm("norm0", 0)

            def gates(keys, name, dst):
                for k, key in enumerate(keys):
                    b = take(dve, key)
                    dve.wait_ge(S(name), k + 1)
                    give(STT(dst[:, k, :], th[:, k % 2, :], 1.0, b[:, :], ALU.add, ALU.mult), key)

            gates([("A", 6 + k // 4, k % 4) for k in range(8)], "A_tanh", G)

            dve.wait_ge(S("bias_edge"), 2)

            def frontA(h):
                dve.wait_ge(s_bias, 3 * h + 3)
                for hf in range(2):
                    key = ("AS", h, hf)
                    b = take(dve, key)
                    if h >= 2:
                        dve.wait_ge(S("A_exp"), 2 * (h - 2) + hf + 1)
                    s = sA[:, h % 2, 512 * hf:512 * hf + 512]
                    w = ap(bias[:, h % 2, :], [(0, 2), (1, 256)]) if hf == 0 else \
                        bias[:, h % 2, :].rearrange("p (m n) -> p m n", m=2)
                    ins = TT(s.rearrange("p (m n) -> p m n", m=2), b[:, :].rearrange("p (m n) -> p m n", m=2), w, ALU.add)
                    give(ins, key)
                    evacuated(dve, key)
                    c = 64 + 8 * (h % 2) + 2 * hf
                    ins = nc.vector.tensor_reduce(stat[:, c:c + 2], s.rearrange("p (m n) -> p m n", m=2), X,
                                                  ALU.max, negate=True)
                    ins.then_inc(S("A_max"), 1)

            def probsA(h):
                for hf in range(2):
                    dve.wait_ge(S("A_exp"), 2 * h + hf + 1)
                    c = 64 + 8 * (h % 2) + 2 * hf
                    link(nc.vector.reciprocal(stat[:, c + 32:c + 34], stat[:, c + 16:c + 18]))
                    for m in range(2):
                        o = 512 * hf + 256 * m
                        ins = TS(pA[:, h % 2, o:o + 256], pA[:, h % 2, o:o + 256], stat[:, c + 32 + m:c + 33 + m],
                                 None, ALU.mult)
                    ins.then_inc(S("A_probs"), 1)

            def outA(h):
                e, j = 64 * (h % 2), h // 2
                key = ("AO_", h)
                b = take(dve, key)
                g = G[e:e + 64, j, :]
                o = hT[e:e + 64, j, :]
                s = b[e:e + 64, :]
                STT(o[:, 64:512], s[:, 0:448], 0.5, g[:, 64:512], ALU.mult, ALU.mult).then_inc(S("A_o_mid"), 1)
                give(STT(o[:, 0:64], s[:, 448:512], 0.5, g[:, 0:64], ALU.mult, ALU.mult), key)

            for h in range(16 + 3):
                if h < 16:
                    frontA(h)
                if 1 <= h < 17:
                    probsA(h - 1)
                if h >= 3:
                    outA(h - 3)
            evacuated(dve, ("AO_", 15))

            def out_proj(tag):
                for n in range(2):
                    for i in range(NT):
                        key = (tag, n, i)
                        b = take(dve, key)
                        give(TT(x[:, i, 512 * n:512 * n + 512], x[:, i, 512 * n:512 * n + 512], b[:, :], ALU.add), key)
                        evacuated(dve, key)

            def ple(l, col):
                norm(f"ple{l}", col)
                for n in range(2):
                    for i in range(NT):
                        key = ("PP", l, n, i)
                        u = 4 * n + i
                        b = take(dve, key)
                        evacuated(dve, ("PG", l, n, i))
                        give(STT(tp[:, u % 2, :], thp[:, u % 4, :], 1.0, b[:, :], ALU.add, ALU.mult), key)
                        evacuated(dve, key)
                        xs = x[:, i, 512 * n:512 * n + 512]
                        STT(xs, tp[:, u % 2, :], 0.5, xs, ALU.mult, ALU.add).then_inc(S("x_ple"), 1)

            out_proj("AO")
            ple(0, 4)

            dve.wait_ge(S("gqk_loaded"), 32)
            cb, sbn = CAT["ropeb"][0], CAT["ropeb"][0] + NT * HD
            tab = cst[:, cb:cb + 2 * NT * HD]
            for n, (dst, sc) in enumerate(((tabq, 0.125), (tabk, 1.0))):
                g = gqk[:, 64 * n:64 * n + 64]
                o = ap(dst[:, 0, :], [(64, 4), (1, 64)])
                STT(o, ap(tab, [(64, 4), (1, 64)]), sc, ap(g, [(0, 4), (1, 64)]), ALU.mult, ALU.mult)
                for hf in range(2):
                    for s in range(2):
                        a = 32 * s + 16 * hf
                        STT(ap(dst[:, 1, :], [(64, 4), (1, 16)], a), ap(tab, [(64, 4), (1, 16)], NT * HD + a), sc,
                            ap(g, [(0, 4), (1, 16)], 32 * s + 16 * (1 - hf)), ALU.mult, ALU.mult)\
                            .then_inc(S("B_tab"), 1)
            dve.wait_ge(S("B_tab"), 8)
            norm("norm1", 8)
            ssq = stat[:, 160:240].rearrange("p (i h) -> p i h", i=NT)
            for n in range(3):
                for i in range(NT):
                    u = 4 * n + i
                    dve.wait_ge(S("B_sq"), u + 1)
                    w = 8 if n < 2 else 4
                    nc.vector.tensor_reduce(ssq[:, i, 8 * n:8 * n + w],
                                            sqB[:, u % 2, 0:64 * w].rearrange("p (h d) -> p h d", d=64), X, ALU.add)\
                        .then_inc(S("B_sq_read"), 1)
            dve.wait_ge(S("B_sq_read"), 12)
            link(TS(stat[:, 160:240], stat[:, 160:240], 1.0 / HD, EPS, ALU.mult, ALU.add))
            rsqrt(stat[:, 240:320], stat[:, 160:240], stat[:, 320:400])
            gates([("B", 3 + k // 4, k % 4) for k in range(8)], "B_tanh", G)
            evacuated(dve, ("B", 2, 3))

            def rope(src, nh, col, tabs, i, a, b, last):
                v = ap(src, [(64, nh), (1, 64)])
                link(TT(v, v, ap(stat[:, col:col + nh], [(1, nh), (0, 64)]), ALU.mult))
                TT(ap(a, [(64, nh), (1, 64)]), v, ap(tabs[:, 0, :], [(0, nh), (1, 64)], 64 * i), ALU.mult)\
                    .then_inc(S("B_rope_t"), 1)
                for hf in range(2):
                    TT(ap(b, [(64, nh), (32, 2), (1, 16)], 16 * hf), ap(src, [(64, nh), (32, 2), (1, 16)], 16 * (1 - hf)),
                       ap(tabs[:, 1, :], [(0, nh), (32, 2), (1, 16)], 64 * i + 16 * hf), ALU.mult)\
                        .then_inc(S("B_rope_t"), 1)
                rope_n[0] += 3
                dve.wait_ge(S("B_rope_t"), rope_n[0])
                if last:
                    TT(src, a[:, 0:64 * nh], b[:, 0:64 * nh], ALU.add).then_inc(S("B_rope"), 1)
                else:
                    TT(ap(kD[:, i, :], [(128, nh), (64, 2), (1, 64)]), ap(a, [(64, nh), (0, 2), (1, 64)]),
                       ap(b, [(64, nh), (0, 2), (1, 64)]), ALU.add).then_inc(S("B_rope_k"), 1)

            rope_n = [0]
            for i in range(NT):
                rope(kB[:, i, :], 4, 240 + 20 * i + 16, tabk, i, tkB[:, 0:256], tkB[:, 256:512], False)
                rope(qB[:, i, :], 16, 240 + 20 * i, tabq, i, t1B, t2B, True)
                dve.wait_ge(S("B_rope"), i + 1)

            NB_ = 16 * NT

            def outB(h):
                e = 64 * (h % 2)
                key = ("BO_", h)
                b = take(dve, key)
                give(STT(hT[e:e + 64, h // 2, :], b[e:e + 64, :], 0.5, G[e:e + 64, h // 2, :], ALU.mult, ALU.mult), key)

            for u in range(NB_ + 1):
                if u < NB_:
                    b = take(dve, ("BS", u))
                    if u >= 4:
                        evacuated(dve, ("BS", u - 4))
                    nc.vector.tensor_reduce(stat[:, 128 + u % 4:129 + u % 4], b[:, :], X, ALU.max, negate=True)\
                        .then_inc(S("B_max"), 1)
                if u >= 1:
                    v = u - 1
                    evacuated(dve, ("BS", v))
                    c = 136 + v % 4
                    link(nc.vector.reciprocal(stat[:, c:c + 1], stat[:, c - 4:c - 3]))
                    TS(pB[:, v % 3, :], pB[:, v % 3, :], stat[:, c:c + 1], None, ALU.mult).then_inc(S("B_probs"), 1)
                if u >= 8 and u % 4 == 0:
                    outB(u // 4 - 2)
            outB(15)
            evacuated(dve, ("BO_", 15))
            out_proj("BO")
            ple(1, 12)

            y = rstd("fin", 16)
            dve.wait_ge(s_gb[0], 16)
            for i in range(NT):
                STT(x[:, i, :], x[:, i, :], y[:, i:i + 1], gb[:, :], ALU.mult, ALU.mult).then_inc(S("x_fin"), 1)
            if stop:
                return
            dve.wait_ge(S("x_fin"), NT)
            norm("norm2", 20, natural=True)
            nc.vector.memset(fl[:, :, :], 0.0).then_inc(S("C_flz"), 1)
            dve.wait_ge(S("C_flz"), 1)
            for n in range(2):
                key = ("kvc", n)
                b = take(dve, key)
                m = 0
                for g in range(2):
                    for par in range(2):
                        for hi in range(2):
                            src = ap(b[64 * g:64 * g + 64, :], [(2, 8), (16, 31)], 16 * hi + par)
                            dst = ap(fl[64 * par:64 * par + 64, n, :], [(64, 8), (1, 31)], 8 * hi * 64 + 32 * g)
                            ins = nc.vector.tensor_copy(dst, src)
                            m += 1
                            if m < 8:
                                ins.then_inc(S("C_flcopy"), 1)
                give(ins, key)
                dve.wait_ge(S("C_flcopy"), 7 * (n + 1))
                evacuated(dve, key)
                pos = vcol("posk" if n == 0 else "posv", 0, 16)
                f = ap(fl[:, n, :], [(64, 16), (1, 64)])
                TT(f, f, ap(pos, [(1, 16), (0, 64)]), ALU.add).then_inc(S("C_flat"), 1)

            def gatesC(keys, name, dst):
                for k, key in enumerate(keys):
                    b = take(dve, key)
                    dve.wait_ge(S(name), k + 1)
                    give(STT(dst[:, k, :], thC[:, k % 2, :], 1.0, b[:, :], ALU.add, ALU.mult), key)

            gatesC([("C", 3, s) for s in range(4)], "C_tanh", Gn)
            dve.wait_ge(S("C_gates"), NT)
            link(TS(gt[:, :, :], gt[:, :, :], 0.5, 0.5, ALU.mult, ALU.add))
            evacuated(dve, ("C", 2, NT - 1))
            evacuated(dve, ("C", 0, NT - 1))
            for n, (src, dst) in enumerate(((q2, q2r), (kd, kd))):
                src, dst = src[:, 0], dst[:, 0]

                def part(v, o):
                    return ap(v, [(512, NT), (64, 8), (1, 8)], o)

                def tabs(name):
                    return ap(C(name), [(8, NT), (0, 8), (1, 8)])

                r4 = [ap(rt[:, k, :], [(64, NT), (8, 8), (1, 8)]) for k in range(4)]
                TT(r4[0], part(src, 0), tabs("cos2"), ALU.mult).then_inc(S("C_rt"), 1)
                TT(r4[1], part(src, 8), tabs("sin2"), ALU.mult).then_inc(S("C_rt"), 1)
                TT(r4[2], part(src, 8), tabs("cos2"), ALU.mult).then_inc(S("C_rt"), 1)
                TT(r4[3], part(src, 0), tabs("sin2"), ALU.mult).then_inc(S("C_rt"), 1)
                dve.wait_ge(S("C_rt"), 4 * n + 4)
                TT(part(dst, 0), r4[0], r4[1], ALU.subtract).then_inc(S("C_rope"), 1)
                TT(part(dst, 8), r4[2], r4[3], ALU.add).then_inc(S("C_rope"), 1)
                dve.wait_ge(S("C_rope"), 2 * n + 2)
            for n in range(2):
                key = ("hid", n)
                b = take(dve, key)
                dve.wait_ge(S("C_thh"), n + 1)
                give(STT(hid[:, n, :], thh, 1.0, b[:, 0:128], ALU.add, ALU.mult), key)
            dve.wait_ge(S("C_clear"), 3)
            b = take(dve, "kcmp")
            for e in range(2):
                ins = TS(kcz[64 * e:64 * e + 64, :, e, :], b[0:64, 0:64].rearrange("p (g c) -> p g c", g=2), 0.5, None,
                         ALU.mult)
                if e == 0:
                    ins.then_inc(S("C_cmp"), 1)
            give(ins, "kcmp")
            evacuated(dve, "kcmp")
            b = take(dve, "vcmp")
            for g in range(2):
                for r in range(4):
                    ins = TS(vcz[32 * r:32 * r + 32, g, r, :], b[0:32, g * 64:g * 64 + 64], 0.5, None, ALU.mult)
                    if (g, r) != (1, 3):
                        ins.then_inc(S("C_cmp"), 1)
            give(ins, "vcmp")
            evacuated(dve, "vcmp")
            dve.sem_inc(S("C_cmp"), 4)

            def heads8(i):
                return smC[:, i % 2, :].rearrange("p (h c) -> p h c", h=8)

            for i in range(NT):
                if i >= 2:
                    dve.wait_ge(filled, J[("ct", i - 2)] + 1)
                s = heads8(i)
                key = ("cs", i)
                b = take(dve, key)
                give(TT(s, b[:, 0:256].rearrange("p (h c) -> p h c", h=8),
                        ap(C("cmpneg"), [(0, 8), (1, 32)], 32 * i), ALU.add), key)
                evacuated(dve, key)
                mx, sm, sc = stat[:, 416:424], stat[:, 424:432], stat[:, 432:440]
                link(nc.vector.tensor_reduce(mx, s, X, ALU.max))
                TT(s, s, ap(mx, [(1, 8), (0, 32)]), ALU.subtract).then_inc(S("C_cs"), 1)
                dve.wait_ge(S("C_ce"), i + 1)
                link(nc.vector.tensor_reduce(sm, s, X, ALU.add))
                link(nc.vector.reciprocal(sm, sm))
                link(TT(sc, sm, ap(gt[:, i, :], [(3, 8)]), ALU.mult))
                link(TT(s, s, ap(C("cmpok"), [(0, 8), (1, 32)], 32 * i), ALU.mult))
                TT(s, s, ap(sc, [(1, 8), (0, 32)]), ALU.mult).then_inc(S("C_pc"), 1)

            def outN(h):
                e, j = 64 * (h % 2), h // 2
                key = ("NO", h)
                b = take(dve, key)
                give(STT(ap(mixA[e:e + 64, j, :], [(1, GR), (GR, GW)]), b[e:e + 64, :].rearrange("p (r c) -> p r c", r=GR),
                         0.5, Gn[e:e + 64, j, :].rearrange("p (r c) -> p r c", r=GR), ALU.mult, ALU.mult), key)

            for u in range(len(UN) + 4):
                if u < len(UN):
                    nk = (UN[u][2] + 1) * P
                    b = take(dve, ("NS", u))
                    if u >= 4:
                        evacuated(dve, ("NS", u - 4))
                    nc.vector.tensor_reduce(stat[:, 400 + u % 4:401 + u % 4], b[:, 0:nk], X, ALU.max, negate=True)\
                        .then_inc(S("N_max"), 1)
                if 1 <= u < len(UN) + 1:
                    v = u - 1
                    h, br, i = UN[v]
                    nk = (i + 1) * P
                    evacuated(dve, ("NS", v))
                    c = 408 + v % 4
                    link(nc.vector.reciprocal(stat[:, c:c + 1], stat[:, c - 4:c - 3]))
                    TS(pN[:, v % 3, 0:nk], pN[:, v % 3, 0:nk], stat[:, c:c + 1], gt[:, i, 3 * h + 1 + br:3 * h + 2 + br],
                       ALU.mult, ALU.mult).then_inc(S("N_probs"), 1)
                if u >= 12 and (u - 12) % 8 == 0:
                    outN((u - 12) // 8)
            outN(7)

            nc.vector.memset(ap(raw[:, 0, :], [(513, 3)]), 0.0).then_inc(S("R_rawzero"), 1)
            dsts = [rF[:, j, :] for j in range(4)] + [kF[:, j, :] for j in range(4)] + [vF[:, j, :] for j in range(4)] + [wdad]
            for s in range(13):
                dve.wait_ge(S("R_dif"), s + 1)
                STT(dsts[s], dif[:, s % 2, :], vcol("mu", s), raw[:, s % 3, 1:513], ALU.mult, ALU.add).then_inc(S("R_mix"), 1)
            TS(stat[:, 576:584], vec[:, V0["w0"]:V0["w0"] + 8], 0.5, None, ALU.mult).then_inc(S("R_half"), 1)
            gatesC([("C", 8, s) for s in range(4)], "R_tanh", Gr)
            dve.wait_ge(S("R_mix"), 13)
            for j in range(4):
                TS(kk[:, j, :], kF[:, j, :], vcol("kk", j), None, ALU.mult).then_inc(S("R_kkraw"), 1)
            for j in range(4):
                evacuated(dve, ("W", j))
                link(TS(lw[:, j, :], lw[:, j, :], -LOGC / 2, -LOGC / 2, ALU.mult, ALU.add))
                link(nc.vector.tensor_tensor_scan(cum[:, j, :], C("chunk"), lw[:, j, :], 0.0, ALU.mult, ALU.add))
                TT(lw[:, j, :], cum[:, j, :], lw[:, j, :], ALU.subtract).then_inc(S("R_cum"), 1)
            for j in range(4):
                evacuated(dve, ("A_", j))
                link(TS(aF[:, j, :], aF[:, j, :], 0.5, 0.5, ALU.mult, ALU.add))
                link(TS(dif[:, 0, :], aF[:, j, :], -1.0, vcol("ka", j), ALU.add, ALU.mult))
                link(STT(kF[:, j, :], dif[:, 0, :], 1.0, kF[:, j, :], ALU.add, ALU.mult))
            b = take(dve, "ks")
            give(TS(stat[:, 448:480], b[:, 0:32], 1e-24, None, ALU.max), "ks")
            evacuated(dve, "ks")
            rsqrt(stat[:, 480:512], stat[:, 448:480], stat[:, 512:544])
            bx3 = bx.rearrange("p (s d) -> p s d", d=64)
            nc.vector.tensor_copy(bx3, ap(stat[:, 480:512], [(1, 32), (0, 64)])).then_inc(S("R_kx"), 1)
            for j in range(4):
                key = ("kb", j)
                b = take(dve, key)
                give(TT(kk[:, j, :], kk[:, j, :], b[:, :], ALU.mult), key)
            evacuated(dve, ("kb", 3))
            dve.wait_ge(S("R_P"), 12)
            for j in range(4):
                def tiles(v):
                    return v.rearrange("p (i t) -> p i t", i=NT)

                STT(AR[:, j, :, 0, :], tiles(kk[:, j, :]), -1.0, tiles(lw[:, j, :]), ALU.mult, ALU.mult).then_inc(S("R_ar"), 1)
                link(TT(aF[:, j, :], aF[:, j, :], kk[:, j, :], ALU.mult))
                link(TT(aF[:, j, :], aF[:, j, :], iP[:, j, :], ALU.mult))
                TT(AR[:, j, :, 1, :], tiles(rF[:, j, :]), tiles(cum[:, j, :]), ALU.mult).then_inc(S("R_ar"), 1)
                STT(sq[:, j, :], rF[:, j, :], vcol("rk", j), kF[:, j, :], ALU.mult, ALU.mult).then_inc(S("R_rk"), 1)
                nc.vector.tensor_copy(PC[:, j, :], ap(cum[:, j, :], [(CH, 8)], CH - 1)).then_inc(S("R_ar"), 1)
                TT(iP[:, j, :], kF[:, j, :], iP[:, j, :], ALU.mult).then_inc(S("R_kap"), 1)
                dve.wait_ge(S("R_kap"), j + 1)
                dve.wait_ge(S("R_ar"), 3 * j + 3)
                dve.sem_inc(S("R_ops"), 1)
            b = take(dve, "bs")
            give(nc.vector.tensor_copy(bx3, ap(b[:, 0:32], [(1, 32), (0, 64)])), "bs")
            evacuated(dve, "bs")
            dve.sem_inc(S("R_bx"), 1)
            for j in range(4):
                key = ("bb", j)
                b = take(dve, key)
                give(TT(rF[:, j, :], vF[:, j, :], b[:, :], ALU.mult), key)
            nc.vector.memset(Sst[:, 0, :], 0.0).then_inc(S("R_state"), 1)

            def plus(key, dst, src):
                for bt in range(2):
                    b = take(dve, key + (bt,))
                    hs = slice(4 * bt, 4 * bt + 4)
                    give(TT(dst[:, hs, :], b[:, :].rearrange("p (h t) -> p h t", h=4), src[:, hs, :], ALU.add), key + (bt,))
                evacuated(dve, key + (1,))

            def moves(key, dst):
                for bt in range(2):
                    b = take(dve, key + (bt,))
                    give(nc.vector.tensor_copy(dst[:, 4 * bt:4 * bt + 4, :], b[:, :].rearrange("p (h t) -> p h t", h=4)),
                         key + (bt,))

            for i in range(NT):
                for h in range(8):
                    key = ("gr", i, h)
                    b = take(dve, key)
                    TT(AE[:, h, :, :], ap(b[:, 0:P], [(0, 2), (1, P)]), ap(C("a16"), [(P, 2), (1, P)]), ALU.mult)\
                        .then_inc(S("R_gram"), 1)
                    give(TT(B3[:, h, :, :].rearrange("p m t -> p (m t)"), b[:, P:512], C("gram"), ALU.mult), key)
                dve.wait_ge(S("R_gram"), 8 * i + 8)
                TT(Qa[:, :, :], AE[:, :, 0, :], ap(ident, [(0, 8), (1, P)]), ALU.add).then_inc(S("R_q1"), 1)
                moves(("D2", i), D2)
                dve.wait_ge(S("R_q1"), i + 1)
                plus(("Q2", i), Qb, Qa)
                plus(("Q3", i), Qa, Qb)
                plus(("Q4", i), Qb, Qa)
                moves(("K", i), AE[:, :, 0, :])
                plus(("Q5", i), Qa, Qb)
                plus(("RR", i), Qb, Qa)
                key = ("rho", i)
                b = take(dve, key)
                give(TT(RHO.rearrange("p (j t) -> p j t", j=4), b[:, :].rearrange("p (j t) -> p j t", j=4),
                        AR[:, :, i, 1, :], ALU.add), key)
                for c in range(2):
                    key = ("M", i, c)
                    b = take(dve, key)
                    give(TT(MT[:, c, :, :], b[:, 0:256].rearrange("p (j k) -> p j k", j=4),
                            ap(C("ident64"), [(0, 4), (1, 64)]), ALU.add), key)
                for c in range(2):
                    k = 2 * i + c
                    key = ("St", k)
                    b = take(dve, key)
                    evacuated(dve, ("Bm", i, c))
                    nx = Sst[:, (k + 1) % 4, :]
                    give(TT(nx, b[:, 0:256], Bm[:, c, :], ALU.add), key)
                    evacuated(dve, key)
                    nv = nx.rearrange("p (j v) -> p j v", j=4)
                    TT(nv, nv, ap(PC[:, :, k], [(8, 4), (0, 64)]), ALU.mult).then_inc(S("R_state"), 1)
                    dve.wait_ge(S("R_state"), k + 2)
                key = ("Y2", i)
                b = take(dve, key)
                evacuated(dve, ("Y1", i))
                yi = yF[:, :, i * P:(i + 1) * P]
                give(TT(yi, yi, b[:, :].rearrange("p (j t) -> p j t", j=4), ALU.add), key)

            b = take(dve, "gn1")
            give(TS(bx3, ap(b[:, 0:32], [(1, 32), (0, 64)]), 1.0 / HD, None, ALU.mult), "gn1")
            evacuated(dve, "gn1")
            dve.sem_inc(S("R_gx"), 1)
            for j in range(4):
                key = ("gb1", j)
                b = take(dve, key)
                give(TT(yF[:, j, :], yF[:, j, :], b[:, :], ALU.subtract), key)
                evacuated(dve, key)
                if j == 3:
                    dve.sem_inc(S("R_centred"), 4)
            b = take(dve, "gn2")
            give(TS(stat[:, 448:480], b[:, 0:32], 1.0 / HD, GN_EPS, ALU.mult, ALU.add), "gn2")
            evacuated(dve, "gn2")
            rsqrt(stat[:, 480:512], stat[:, 448:480], stat[:, 512:544])
            nc.vector.tensor_copy(bx3, ap(stat[:, 480:512], [(1, 32), (0, 64)])).then_inc(S("R_gx"), 1)
            for j in range(4):
                key = ("gb2", j)
                b = take(dve, key)
                y = yF[:, j, :]
                give(TT(y, y, b[:, :], ALU.mult), key)
                evacuated(dve, key)
                link(TS(y, y, vcol("gnw", j), vcol("gnb", j), ALU.mult, ALU.add))
                link(TT(y, y, rF[:, j, :], ALU.add))
                STT(ap(mixB[:, j, :], [(1, GR), (GR, GW)]), y.rearrange("p (r c) -> p r c", r=GR), 0.5,
                    Gr[:, j, :].rearrange("p (r c) -> p r c", r=GR), ALU.mult, ALU.mult).then_inc(S("R_done"), 1)
            out_proj("CO")

            y = rstd("out", 24)
            dve.wait_ge(s_gb[1], 16)
            for i in range(NT):
                STT(xo[:, i, :], x[:, i, :], y[:, i:i + 1], gb2[:, :], ALU.mult, ALU.mult).then_inc(S("out_ready"), 1)

        @block.gpsimd
        def _(pool):
            pool.dma_start(cst[:, :], A["cst"]).then_inc(s_cst, 16)
            pool.dma_start(rpb_in[0:16, 0:465], A["a_rpb"][0].rearrange("h a b -> h (a b)")).then_inc(s_rpb, 16)
            pool.wait_ge(S("vrow_zero"), 1)
            c = 0
            for src, n in rows:
                pool.dma_start(vrow[c:c + n, :], src).then_inc(s_vrow, 16)
                c += n
            pool.wait_ge(s_rpbr, 2)
            pool.dma_start(scratch, rrev).then_inc(s_scr, 16)
            pool.wait_ge(s_scr, 16)
            pool.dma_start(w2[:, 0, :, :], A["cmp_w2_k_2"][0].rearrange("(b p) d -> p b d", p=P)).then_inc(s_small, 16)
            pool.dma_start(w2[:, 1, :, :], A["cmp_w2_v_2"][0].rearrange("(b p) d -> p b d", p=P)).then_inc(s_small, 16)
            pool.dma_start(wa[0:64, :], A["decay_up_2"][0]).then_inc(s_small, 16)
            pool.dma_start(wa[64:128, :], A["iclr_up_2"][0]).then_inc(s_small, 16)

            def load_bias(h):
                src = bass.AP(scratch.tensor, h * 1024 + 49, [[1, 16], [64, 8], [1, 512]])
                pool.dma_start(ext[:, h % 2, :], src).then_inc(s_ext[h % 2], 16)

            for i in range(2):
                nc.gpsimd.memset(bias[0:64, i, 256:384], NEG).then_inc(S("bias_edge"), 1)
            load_bias(0)
            load_bias(1)
            pool.wait_ge(s_cst, 16)
            mask = C("nbr")
            for h in range(16):
                pool.wait_ge(s_ext[h % 2], 16 * (h // 2 + 1))
                if h >= 2:
                    evacuated(pool, ("AS", h - 2, 1))
                e_ = ext[:, h % 2, :]
                o = bias[:, h % 2, :]

                def rev(lo, hi, jj):
                    return ap(ext[lo:hi, h % 2, :], [(-1, 32), (-64, 8)], 511 - jj)

                def jk(v, c):
                    return v[:, c:c + 256].rearrange("p (j k) -> p j k", k=8)

                nc.gpsimd.tensor_tensor(jk(o, 0), rev(0, 128, 8), jk(mask, 0), ALU.add).then_inc(s_bias, 1)
                pool.wait_ge(s_bias, 3 * h + 1)
                nc.gpsimd.tensor_tensor(o[0:64, 384:512].rearrange("p (j k) -> p j k", k=8),
                                        ap(ext[0:64, h % 2, :], [(-1, 16), (-64, 8)], 511 - 8),
                                        mask[0:64, 384:512].rearrange("p (j k) -> p j k", k=8), ALU.add).then_inc(s_bias, 1)
                pool.wait_ge(s_bias, 3 * h + 2)
                nc.gpsimd.tensor_tensor(jk(o[64:128], 256), rev(64, 128, 24), jk(mask[64:128], 256), ALU.add)\
                    .then_inc(s_bias, 1)
                pool.wait_ge(s_bias, 3 * h + 3)
                if h + 2 < 16:
                    load_bias(h + 2)
            for l in range(2):
                evacuated(pool, ("AO_" if l == 0 else "BO_", 15))
                src = A["p"][l, 0].rearrange("(r c) d -> c r d", r=GR)
                for i in range(NT):
                    pool.dma_start(p_tm[:, i, :], src[CT * i:CT * i + CT]).then_inc(s_p[l], 16)
                if l == 0:
                    for n, name in enumerate(("b_q_norm", "b_k_norm")):
                        pool.dma_start(gqk[:, 64 * n:64 * n + 64], bass.AP(A[name].tensor, 0, [[0, P], [1, 64]]))\
                            .then_inc(S("gqk_loaded"), 16)
                else:
                    pool.dma_start(gb[:, :], bass.AP(A["final_norm_g"].tensor, 0, [[0, P], [1, D]]))\
                        .then_inc(s_gb[0], 16)
            if stop:
                return
            evacuated(pool, ("norm2", NT - 1, 1))
            nc.gpsimd.memset(kcz[:, :, :, :], 0.0).then_inc(S("C_clear"), 1)
            nc.gpsimd.memset(vcz[:, :, :, :], 0.0).then_inc(S("C_clear"), 1)
            nc.gpsimd.memset(kz[:, :, :, :, :], 0.0).then_inc(S("C_clear"), 1)
            for s in range(13):
                evacuated(pool, ("R", s))
                if s >= 2:
                    pool.wait_ge(S("R_mix"), s - 1)
                nc.gpsimd.tensor_tensor(dif[:, s % 2, :], raw[:, s % 3, 0:512], raw[:, s % 3, 1:513], ALU.subtract)\
                    .then_inc(S("R_dif"), 1)
            pool.wait_ge(S("R_done"), 4)
            pool.dma_start(gb2[:, :], bass.AP(A["final_g_2"].tensor, 0, [[0, P], [1, D]])).then_inc(s_gb[1], 16)

        @block.sync
        def _(sp):
            for n, (src, (k, m)) in enumerate(chunks):
                if stop and n > CI[("PP", 1)]:
                    break
                if n >= NSLOT:
                    sp.wait_ge(filled, chunk_last[n - NSLOT] + 1)
                dst = ring[:, n % NSLOT, 0:k * m].rearrange("p (k m) -> p k m", k=k)
                sp.dma_start(dst, src).then_inc(weights[n % NSLOT], 16)
            o = out[0].rearrange("(r c) d -> c r d", r=GR)
            for i in range(NT):
                if stop:
                    sp.wait_ge(S("x_fin"), i + 1)
                    src = x[:, i, :]
                else:
                    sp.wait_ge(S("out_ready"), i + 1)
                    src = xo[:, i, :]
                sp.dma_start(o[CT * i:CT * i + CT], src).then_inc(s_out, 16)
            sp.wait_ge(s_out, 16 * NT)


NAMES = ("x p norm_g a_w_in a_rpb a_w_out b_w_in b_q_norm b_k_norm b_w_out ple_norm_g ple_w_gate ple_w_proj "
         "final_norm_g norm_g_2 w_in_2 cmp_pos_k_2 cmp_w1_k_2 cmp_w2_k_2 cmp_pos_v_2 cmp_w1_v_2 cmp_w2_v_2 "
         "shift_mu_2 decay_w0_2 decay_up_2 iclr_a0_2 iclr_up_2 k_k_2 k_a_2 r_k_2 gn_w_2 gn_b_2 w_out_2 "
         "final_g_2").split()
STOP = None


def kernel(**inputs):
    import numpy as _np
    import concourse.bacc as _bacc
    from concourse import mybir as _mybir
    from concourse.bass_utils import run_bass_kernel_spmd as _run

    nc = _bacc.Bacc("TRN2", target_bir_lowering=False, num_devices=1)
    arrays, aps = {}, {}
    for name in NAMES:
        a = _np.ascontiguousarray(inputs[name])
        arrays[f"in_{name}"] = a
        aps[name] = nc.dram_tensor(f"in_{name}", a.shape, _mybir.dt.from_np(a.dtype), kind="ExternalInput").ap()
    arrays["in_cst"] = CST
    aps["cst"] = nc.dram_tensor("in_cst", CST.shape, _mybir.dt.float32, kind="ExternalInput").ap()
    out = nc.dram_tensor("out_0", (1, T, D), _mybir.dt.float32, kind="ExternalOutput").ap()
    program(nc, aps, out, STOP)
    r = _run(nc, [arrays], core_ids=[0])
    return r.results[0]["out_0"]
```

```python
import math
from contextlib import ExitStack

import numpy as np

import concourse.bass as bass
from concourse import mybir

F32 = mybir.dt.float32
F32R = mybir.dt.float32r
BF16 = mybir.dt.bfloat16
I32 = mybir.dt.int32
ALU = mybir.AluOpType
ACT = mybir.ActivationFunctionType
X = mybir.AxisListType.X

P = 128
D = 1024
T = 512
NT = T // P
KB = D // P
HD = 64
GW, GR = 64, 8
CT = GW // NT
NEG = -1e30
EPS = 1e-6
GN_EPS = 64e-5
NBANK = 8
NSLOT = 3
HALF = 2048
NRAW, NHI = 4, 2
CH = 64
LOGC = math.exp(-0.5)
RSQRT_MAGIC = float(0x5F3759DF)


def constants():
    parts, at, n = [], {}, 0

    def add(name, a):
        nonlocal n
        a = np.asarray(a, np.float64).reshape(P, -1).astype(np.float32)
        at[name] = (n, a.shape[1])
        n += a.shape[1]
        parts.append(a)

    p = np.arange(P)
    cq, r = p // GR, p % GR
    add("ident", np.eye(P))
    j = np.repeat(np.arange(32), GR)
    mid = (j[None] >= cq[:, None]) & (j[None] <= cq[:, None] + 15)
    edge = np.where(cq[:, None] < 8, j[None] >= 16, j[None] < 16)
    add("nbr", np.concatenate([np.where(mid, 0, NEG), np.where(edge, 0, NEG)], 1))
    inv = 10000.0 ** (-np.arange(16) * 2.0 / 32)
    cos, sin = np.zeros((P, NT, 2, 2, 16)), np.zeros((P, NT, 2, 2, 16))
    for i in range(NT):
        for s, pos in ((0, r), (1, CT * i + cq)):
            ang = pos[:, None] * inv[None]
            for hf in range(2):
                cos[:, i, s, hf] = np.cos(ang)
                sin[:, i, s, hf] = np.sin(ang) * (-1 if hf == 0 else 1)
    add("ropeb", np.concatenate([cos.reshape(P, NT * HD), sin.reshape(P, NT * HD)], 1))
    inv2 = 500000.0 ** (-np.arange(8) / 8.0)
    pos = (np.arange(NT)[None] * P + p[:, None])[..., None] * inv2
    add("cos2", np.cos(pos))
    add("sin2", np.sin(pos))
    c = np.arange(32)
    ok = (c[None, None] * 16 + 31 <= (np.arange(NT)[None] * P + p[:, None])[..., None]) & (c < 31)
    add("cmpneg", np.where(ok, 0, NEG))
    add("cmpok", ok)
    add("causal", np.where(p[None] > p[:, None], NEG, 0))
    s, t = p[:, None], p[None]
    same, same16 = s // CH == t // CH, s // 16 == t // 16
    add("a16", (s < t) & same16)
    add("e16", (s < t) & same & ~same16)
    add("gram", np.concatenate([(s <= t) & same, (s < t) & same, (s <= t) & same], 1))
    add("chunk", np.tile((np.arange(T) % CH != 0), (P, 1)))
    add("heads", np.stack([p < HD, p >= HD], 1))
    add("ident64", np.tile(np.eye(HD), (2, 1)))
    return np.concatenate(parts, 1), at


CST, CAT = constants()


def program(nc, A, out):
    ctx = ExitStack()
    with ctx:
        def sb(name, shape, dt=F32):
            return ctx.enter_context(nc.sbuf_tensor(name, shape, dt))

        second = {}

        def sb2(name, shape, *spans):
            at = nc.sbuf_base
            plain = sb(name, shape)
            second[name] = [(o, n, nc.alloc_sbuf_tensor_at(f"{name}_parts{o}", [P, n], F32R, offset=at + 4 * o))
                            for o, n in spans]
            return plain

        def sem(name):
            return ctx.enter_context(nc.semaphore(name))

        x = sb("x", [P, NT, D])
        hT = sb2("hT", [P, KB, T], (0, KB * T))
        ring = sb2("ring", [P, NSLOT * KB * 512], (0, NSLOT * KB * 512))
        cst = sb("cst", [P, CST.shape[1]])
        vrow = sb("vrow", [P, P])
        vec = sb("vec", [P, P])
        stat = sb("stat", [P, 640])
        identb = sb("identb", [P, P], BF16)
        causalb = sb("causalb", [P, P], BF16)
        w2 = sb("w2", [P, 2, 2, HD])
        wa = sb("wa", [P, 512])
        NARENA = 28000
        arena = sb2("arena", [P, NARENA], (0, 12288), (19456, 6144))
        bank = [ctx.enter_context(nc.psum_tensor(f"bank{b}", [P, 512], F32)) for b in range(NBANK)]
        scratch = nc.dram_tensor("rpb_rows", [16, 1024], F32, kind="Internal").ap()

        def C(name):
            o, n = CAT[name]
            return cst[:, o:o + n]

        def ap(base, dims, off=0):
            return bass.AP(base.tensor, base.offset + off, [list(base.ap[0])] + [list(d) for d in dims])

        def area(o, n):
            assert o + n <= NARENA
            return arena[:, o:o + n]

        ident = C("ident")

        rows, V0 = [], {}
        for name, src in (("norm0", A["norm_g"][0:1]), ("norm1", A["norm_g"][1:2]),
                          ("ple0", A["ple_norm_g"][0:1]), ("ple1", A["ple_norm_g"][1:2]),
                          ("norm2", A["norm_g_2"]), ("mu", A["shift_mu_2"]), ("w0", A["decay_w0_2"]),
                          ("a0", A["iclr_a0_2"]), ("kk", A["k_k_2"]), ("ka", A["k_a_2"]), ("rk", A["r_k_2"]),
                          ("gnw", A["gn_w_2"]), ("gnb", A["gn_b_2"]),
                          ("posk", A["cmp_pos_k_2"].rearrange("a b c -> a (b c)")),
                          ("posv", A["cmp_pos_v_2"].rearrange("a b c -> a (b c)"))):
            n = src.shape[1] // P
            V0[name] = sum(m for _, m in rows)
            rows.append((src.rearrange("a (j p) -> (a j) p", p=P), n))
        NV = sum(m for _, m in rows)
        assert NV <= P

        def vcol(name, j=0, n=1):
            return vec[:, V0[name] + j:V0[name] + j + n]

        halves, HI = [], {}

        def cols(w, a, b):
            return w.rearrange("(k p) n -> p k n", p=P)[:, :, a:b]

        def half(name, w, n):
            HI[name] = len(halves)
            halves.append(cols(w, 256 * n, 256 * n + 256))

        AORD = list(range(8, 12)) + list(range(8)) + list(range(12, 16))
        for n in AORD:
            half(("A", n), A["a_w_in"][0], n)
        for n in range(4):
            half(("AO", n), A["a_w_out"][0], n)
        for n in range(4):
            half(("PG", 0, n), A["ple_w_gate"][0], n)
        for n in range(10):
            half(("B", n), A["b_w_in"][0], n)
        for n in range(4):
            half(("BO", n), A["b_w_out"][0], n)
        for n in range(4):
            half(("PG", 1, n), A["ple_w_gate"][1], n)

        def raw_slot(n):
            return ring[:, HALF * (n % NRAW):HALF * (n % NRAW) + HALF]

        def high_slot(n):
            o = HALF * (NRAW + n % NHI)
            return ring[:, o:o + HALF]

        chunks, CI = [], {}

        def chunk(name, src, shape):
            CI[name] = len(chunks)
            chunks.append((src, shape))

        CCOL = [(0, 512), (512, 1024), (1024, 1304), (1304, 1816), (1816, 2328), (2328, 2840), (2840, 3352),
                (3352, 3480), (3480, 3992)]
        for n in range(4):
            chunk(("C", n), cols(A["w_in_2"][0], *CCOL[n]), (KB, CCOL[n][1] - CCOL[n][0]))
        chunk("W1K", cols(A["cmp_w1_k_2"][0], 0, 256), (16, 256))
        chunk("W1V", cols(A["cmp_w1_v_2"][0], 0, 256), (16, 256))
        for n in range(4, 9):
            chunk(("C", n), cols(A["w_in_2"][0], *CCOL[n]), (KB, CCOL[n][1] - CCOL[n][0]))
        for n in range(2):
            chunk(("CO", n), cols(A["w_out_2"][0], 512 * n, 512 * n + 512), (KB, 512))

        def slot(n):
            o = 2 * HALF * (1, 0, 2)[n % NSLOT]
            return ring[:, o:o + 2 * HALF]

        wave_slot = CI[("C", 8)]
        assert wave_slot % NSLOT not in (CI[("CO", 0)] % NSLOT, CI[("CO", 1)] % NSLOT)

        def W(name):
            n = CI[name]
            k, m = chunks[n][1]
            return slot(n)[:, 0:k * m].rearrange("p (k m) -> p k m", k=k)


        def rounded(v):
            last = v.offset + sum(step * (count - 1) for step, count in list(v.ap)[1:])
            for o, n, t in second[v.tensor.name]:
                if o <= v.offset and last < o + n:
                    return bass.AP(t, v.offset - o, [[n, P]] + [list(d) for d in list(v.ap)[1:]])
            raise ValueError("no rounded parts here")

        def read_back(v):
            return rounded(v).bitcast(F32)

        def parts(high, low, k):
            return tuple(rounded(v.rearrange("p (k m) -> p k m", k=k)) for v in (high, low))

        def W3(name):
            n = HI[name]
            return parts(high_slot(n), raw_slot(n), KB)

        filled = sem("filled")
        drained = {"a": sem("drained_by_scalar"), "v": sem("drained_by_vector")}
        raw_loaded = [sem(f"raw_loaded{i}") for i in range(NRAW)]
        s_whi = sem("weight_high_parts")
        s_wlo = sem("weight_low_parts")
        s_pp = [sem(f"embedding_weights_loaded{l}") for l in range(2)]
        weights = [sem(f"weights{i}") for i in range(NSLOT)]
        s_x = [sem(f"x_loaded{i}") for i in range(NT)]
        s_cst = sem("constants_loaded")
        s_vrow = sem("vectors_loaded")
        s_small = sem("small_weights_loaded")
        s_p = [sem(f"p_loaded{l}") for l in range(2)]
        s_gb = [sem(f"gain_rows_loaded{l}") for l in range(3)]
        s_rpb = sem("rpb_loaded")
        s_rpbr = sem("rpb_reversed")
        s_scr = sem("rpb_scratch_written")
        s_ext = [sem(f"bias_rows_loaded{i}") for i in range(2)]
        s_bias = sem("bias_ready")
        s_v = sem("vector_chain")
        s_out = sem("out_written")
        made = {}

        def S(name):
            if name not in made:
                made[name] = sem(name)
            return made[name]

        order, J, who, nth, count = [], {}, {}, {}, {"a": 0, "v": 0}

        def take(eng, key):
            eng.wait_ge(filled, J[key] + 1)
            return bank[J[key] % NBANK]

        given = {"a": 0, "v": 0}

        def give(ins, key):
            given[who[key]] += 1
            assert nth[key] == given[who[key]], (key, nth[key], given)
            ins.then_inc(drained[who[key]], 1)

        def evacuated(eng, key):
            eng.wait_ge(drained[who[key]], nth[key])

        qT = area(0, 4096).rearrange("p (j t) -> p j t", j=8)
        kT = area(4096, 4096).rearrange("p (j t) -> p j t", j=8)
        va = area(8192, 4096).rearrange("p (i n) -> p i n", i=NT)
        G = area(12288, 4096).rearrange("p (j t) -> p j t", j=8)
        xn = area(16384, 2048).rearrange("p (b d) -> p b d", b=2)
        th = area(18432, 1024).rearrange("p (b d) -> p b d", b=2)
        ext = area(19456, 1024).rearrange("p (b d) -> p b d", b=2)
        bias = area(20480, 1024).rearrange("p (b d) -> p b d", b=2)
        sA = area(21504, 2048).rearrange("p (b d) -> p b d", b=2)
        pA = area(23552, 2048).rearrange("p (b d) -> p b d", b=2)
        ptA = area(16384, 3072).rearrange("p (b h d) -> p b h d", b=3, h=2)
        rpb_in = area(27136, 480)
        rrev = area(19456, 1024)[0:16, :]
        junk = area(26112, 1024)
        hTf = hT[:, :, :].rearrange("p k t -> p (k t)")
        low = {"norm0": area(21504, 4096), "ple0": area(4096, 4096), "norm1": area(0, 4096), "ple1": area(4096, 4096)}
        o_high = area(0, 4096)
        p_tm = area(20480, 1024).rearrange("p (i n) -> p i n", i=NT)
        p_T = area(21504, 1024).rearrange("p (k t) -> p k t", k=2)
        p_lo = area(19456, 1024).rearrange("p (k t) -> p k t", k=2)
        thp = area(22528, 1024).rearrange("p (b d) -> p b d", b=4)
        tp = area(24576, 512).rearrange("p (b d) -> p b d", b=2)
        pw_lo, pw_hi = area(8192, 2048), area(10240, 2048)
        kTB = area(4096, 2048).rearrange("p (g t) -> p g t", g=4)
        vB = area(6144, 1024).rearrange("p (i n) -> p i n", i=NT)
        tabq = area(7168, 512).rearrange("p (s n) -> p s n", s=2)
        tabk = area(7680, 512).rearrange("p (s n) -> p s n", s=2)
        gqk = area(27616, 128)
        kB = area(8320, 1024).rearrange("p (i n) -> p i n", i=NT)
        qB = area(19456, 4096).rearrange("p (i n) -> p i n", i=NT)
        t1B = area(23552, 1024)
        t2B = area(24576, 1024)
        sqB = area(25600, 512).rearrange("p (b d) -> p b d", b=2)
        tkB = area(9344, 512)
        kD = area(9856, 2048).rearrange("p (i n) -> p i n", i=NT)
        ptB = area(19456, 4096).rearrange("p (b k t) -> p b k t", b=2, k=4)
        pB = area(23552, 1536).rearrange("p (b d) -> p b d", b=3)
        gb = area(12288, 1024)
        xo = area(0, 4096).rearrange("p (i d) -> p i d", i=NT)
        gb2 = area(4096, 1024)
        q2 = area(0, 2048).rearrange("p (i n) -> p i n", i=NT)
        q2r = area(2048, 2048).rearrange("p (i n) -> p i n", i=NT)
        qTp = area(4096, 2048).rearrange("p (j t) -> p j t", j=4)
        qTr = area(6144, 2048).rearrange("p (j t) -> p j t", j=4)
        kz = area(8192, 4096).rearrange("p (b g e t) -> p b g e t", b=2, g=2, e=2)
        vS = area(12288, 1024).rearrange("p (i b n) -> p i b n", i=NT, b=2)
        gt = area(14432, 96).rearrange("p (i n) -> p i n", i=NT)
        pTc = area(14528, 1024).rearrange("p (g t) -> p g t", g=2)
        fl = area(15552, 2048).rearrange("p (b n) -> p b n", b=2)
        hid = area(17600, 256).rearrange("p (b n) -> p b n", b=2)
        thh = area(17856, 128)
        kcz = area(17984, 128).rearrange("p (g e c) -> p g e c", g=2, e=2)
        vcz = area(18112, 512).rearrange("p (g r d) -> p g r d", g=2, r=4)
        pN = area(18624, 1536).rearrange("p (b n) -> p b n", b=3)
        ptN = [area(20160, 4096).rearrange("p (b k t) -> p b k t", b=2, k=4),
               area(0, 4096).rearrange("p (b k t) -> p b k t", b=2, k=4)]
        rt = area(20160, 1024).rearrange("p (b n) -> p b n", b=4)
        kd = area(21184, 2048).rearrange("p (i b n) -> p i b n", i=NT, b=2)
        smC = area(24256, 512).rearrange("p (b n) -> p b n", b=2)
        Gn = area(24768, 2048).rearrange("p (j t) -> p j t", j=4)
        thC = area(26816, 1024).rearrange("p (b n) -> p b n", b=2)
        mixA = area(15552, 2048).rearrange("p (j t) -> p j t", j=4)
        def four(o):
            return area(o, 2048).rearrange("p (j t) -> p j t", j=4)

        rF, kF, vF, Gr = four(0), four(2048), four(4096), four(6144)
        raw = area(8192, 1539).rearrange("p (b n) -> p b n", b=3)
        wdad = area(9732, 512)
        dif = area(10244, 1024).rearrange("p (b n) -> p b n", b=2)
        yF = four(11268)
        lw, cum, iP, aF, kk = four(13316), four(17600), four(19648), four(21696), four(23744)
        sq = four(8192)
        bx = area(8192, 2048)
        AR = hT[:, :, :].rearrange("p (j i) t -> p (j i t)", j=4).rearrange("p (j i a t) -> p j i a t", j=4, i=4, a=2)
        wslot = slot(wave_slot)
        B3 = wslot[:, 0:3072].rearrange("p (h m t) -> p h m t", h=8, m=3)
        Dm = wslot[:, 3072:4096].rearrange("p (h t) -> p h t", h=8)
        AE = area(2048, 2048).rearrange("p (h m t) -> p h m t", h=8, m=2)
        A2 = area(13316, 1024).rearrange("p (h t) -> p h t", h=8)
        D2 = area(14340, 1024).rearrange("p (h t) -> p h t", h=8)
        Qa = area(17600, 1024).rearrange("p (h t) -> p h t", h=8)
        Qb = area(18624, 1024).rearrange("p (h t) -> p h t", h=8)
        XG = area(23744, 1024).rearrange("p (h t) -> p h t", h=8)
        HG = area(24768, 1024).rearrange("p (h t) -> p h t", h=8)
        btm, ktm, vtm = area(8192, 512), area(8704, 512), area(9216, 512)
        MT = area(9728, 512).rearrange("p (c j k) -> p c j k", c=2, j=4)
        Bm = area(10240, 512).rearrange("p (c n) -> p c n", c=2)
        RHO = area(10752, 512)
        Sst = area(25792, 1024).rearrange("p (b n) -> p b n", b=4)
        mixB = four(13316)
        PC = stat[:, 544:576].rearrange("p (j c) -> p j c", j=4)

        UN = [(h, br, i) for h in range(8) for br in range(2) for i in range(NT)]

        block = ctx.enter_context(nc.Block())
        chunk_last, half_last = {}, {}

        @block.tensor
        def _(pe):
            def begin(key, consumer):
                n = len(order)
                if n >= NBANK:
                    evacuated(pe, order[n - NBANK])
                order.append(key)
                J[key], who[key] = n, consumer
                count[consumer] += 1
                nth[key] = count[consumer]
                return bank[n % NBANK]

            def end(ins):
                ins.then_inc(filled, 1)

            def mm(o, l, r, start, stop):
                return nc.tensor.matmul(o, l, r, start=start, stop=stop)

            def need(name):
                n = CI[name]
                pe.wait_ge(weights[n % NSLOT], 16 * (n // NSLOT + 1))

            def used(name):
                chunk_last[CI[name]] = len(order) - 1

            def turn(tag, i):
                pe.wait_ge(S("xn_" + tag), i + 1)
                for hf in range(2):
                    b = begin((tag, i, hf), "v")
                    for q in range(4):
                        o = (4 * hf + q) * P
                        ins = nc.tensor.transpose(b[:, q * P:(q + 1) * P], xn[:, i % 2, o:o + P], ident)
                    end(ins)

            def norm(tag):
                for i in range(NT):
                    turn(tag, i)
                evacuated(pe, (tag, NT - 1, 1))

            def need3(name):
                pe.wait_ge(s_wlo, HI[name] + 1)

            def used3(name):
                half_last[HI[name]] = len(order) - 1

            def three(o, left, right, start, stop):
                mm(o, left[0], right[0], start, False)
                mm(o, left[0], right[1], False, False)
                return mm(o, left[1], right[0], False, stop)

            def fm3(key, consumer, name, c0, act):
                b = begin(key, consumer)
                w = W3(name)
                for k in range(KB):
                    ins = three(b[:, :], [v[:, k, c0:c0 + P] for v in w], [v[:, k, :] for v in act], k == 0, k == KB - 1)
                end(ins)

            def tm3(key, consumer, w, i, c0, act, nk=KB, ready=None):
                b = begin(key, consumer)
                for k in range(nk):
                    if ready:
                        ready(k)
                    ins = three(b[:, 0:256], [v[:, k, i * P:(i + 1) * P] for v in act], [v[:, k, c0:c0 + 256] for v in w],
                                k == 0, k == nk - 1)
                end(ins)

            def tail(jobs, tag):
                for i in range(3):
                    jobs(i)
                turn(tag, 0)
                jobs(3)
                turn(tag, 1)

            def head(tag, jobs):
                for i in range(NT):
                    if i < 3:
                        pe.wait_ge(S("lo_" + tag), 2 * i + 2)
                    else:
                        pe.wait_ge(S("lo3_" + tag), 2)
                    jobs(i)
                    if i < 2:
                        turn(tag, i + 2)

            def act3(tag):
                return parts(hTf, low[tag], KB)

            def fm(key, consumer, name, c0, m=P):
                b = begin(key, consumer)
                w = W(name)
                for k in range(KB):
                    ins = mm(b[0:m, :], w[:, k, c0:c0 + m], hT[:, k, :], k == 0, k == KB - 1)
                end(ins)

            def tm(key, consumer, name, i, c0, n, src=None, nk=KB):
                b = begin(key, consumer)
                w, src = W(name), hT if src is None else src
                for k in range(nk):
                    ins = mm(b[:, 0:n], src[:, k, i * P:(i + 1) * P], w[:, k, c0:c0 + n], k == 0, k == nk - 1)
                end(ins)

            def out_proj(tag, l):
                act = parts(o_high, hTf, KB)

                def ready(k):
                    pe.wait_ge(S("o_low"), 8 * l + k + 1)

                for n in range(4):
                    need3((tag, n))

                    def jobs(i):
                        tm3((tag, n, i), "v", W3((tag, n)), i, 0, act, ready=ready if (n, i) == (0, 0) else None)

                    if n < 3:
                        for i in range(NT):
                            jobs(i)
                    else:
                        tail(jobs, f"ple{l}")
                    used3((tag, n))
                    if n == 0:
                        pe.wait_ge(s_p[l], 16 * NT)
                        for k in range(2):
                            b = begin(("pT", l, k), "v")
                            for i in range(NT):
                                ins = nc.tensor.transpose(b[:, i * P:(i + 1) * P], p_tm[:, i, k * P:(k + 1) * P], ident)
                            end(ins)

            def ple(l, after):
                act = act3(f"ple{l}")
                pw = parts(pw_hi, pw_lo, 2)
                pT = tuple(rounded(v[:, :, :]) for v in (p_T, p_lo))
                for n in range(4):
                    need3(("PG", l, n))
                    if n == 0:
                        evacuated(pe, ("pT", l, 1))
                        pe.wait_ge(S("pw_low"), l + 1)

                    def jobs(i):
                        tm3(("PG", l, n, i), "a", W3(("PG", l, n)), i, 0, act)
                        tm3(("PP", l, n, i), "v", pw, i, 256 * n, pT, nk=2)

                    if n == 0:
                        head(f"ple{l}", jobs)
                    elif n == 3 and after:
                        tail(jobs, after)
                    else:
                        for i in range(NT):
                            jobs(i)
                    used3(("PG", l, n))

            pe.wait_ge(s_cst, 16)
            pe.wait_ge(S("vrow_zero"), 1)
            pe.wait_ge(s_vrow, 16 * len(rows))
            b = begin("vec", "a")
            end(nc.tensor.transpose(b[:, 0:P], vrow[:, :], ident))

            turn("norm0", 0)
            turn("norm0", 1)
            act = act3("norm0")
            for n in AORD:
                need3(("A", n))
                if n == AORD[0]:
                    head("norm0", lambda i: tm3(("Av", n, i), "a", W3(("A", n)), i, 0, act))
                elif n in range(8, 12):
                    for i in range(NT):
                        tm3(("Av", n, i), "a", W3(("A", n)), i, 0, act)
                else:
                    for s in range(2):
                        fm3(("A", n, s), "a" if n < 8 else "v", ("A", n), s * P, act)
                used3(("A", n))

            def scoresA(h):
                e, j = 64 * (h % 2), h // 2
                q = qT[e:e + 64, j, :]
                k = kT[e:e + 64, j, :]
                for hf in range(2):
                    b = begin(("AS", h, hf), "v")
                    for m in range(2):
                        t = 2 * hf + m
                        l = q[:, P * t:P * t + P]
                        r = k[:, P * t:P * t + 256] if t < 3 else ap(k, [(384, 2), (1, P)])
                        ins = mm(b[:, m * 256:(m + 1) * 256], l, r, True, True)
                    end(ins)

            def transA(h):
                for hf in range(2):
                    pe.wait_ge(S("A_probs"), 2 * h + hf + 1)
                    b = begin(("AT", h, hf), "a")
                    for m in range(2):
                        for c in range(2):
                            o = (2 * m + c) * P
                            ins = nc.tensor.transpose(b[:, o:o + P], pA[:, h % 2, 512 * hf + o:512 * hf + o + P], ident)
                    end(ins)

            def pvA(h):
                e = 64 * (h % 2)
                evacuated(pe, ("AT", h, 1))
                b = begin(("AO_", h), "v")
                for t in range(4):
                    for c in range(2):
                        kt = (t + c) if t < 3 else 3 * c
                        o = (2 * (t % 2) + c) * P
                        ins = mm(b[e:e + 64, t * P:(t + 1) * P], va[:, kt, h * 64:h * 64 + 64],
                                 ptA[:, h % 3, t // 2, o:o + P], c == 0, c == 1)
                end(ins)

            evacuated(pe, ("A", 7, 1))
            evacuated(pe, ("Av", 11, 3))
            for h in range(16 + 3):
                if h < 16:
                    scoresA(h)
                if h >= 3:
                    pvA(h - 3)
                if 1 <= h < 17:
                    transA(h - 1)
            out_proj("AO", 0)
            ple(0, "norm1")

            act = act3("norm1")
            for n in range(10):
                need3(("B", n))
                if n == 0:
                    head("norm1", lambda i: tm3(("B", 0, i), "a", W3(("B", 0)), i, 0, act))
                elif n < 6:
                    for i in range(NT):
                        tm3(("B", n, i), "a", W3(("B", n)), i, 0, act)
                else:
                    for s in range(2):
                        fm3(("B", n, s), "v", ("B", n), s * P, act)
                used3(("B", n))
            for i in range(NT):
                pe.wait_ge(S("B_rope"), i + 1)
                pe.wait_ge(S("B_rope_k"), i + 1)
                for hf in range(2):
                    b = begin(("BqT", i, hf), "a")
                    for q in range(4):
                        o = (4 * hf + q) * P
                        ins = nc.tensor.transpose(b[:, q * P:(q + 1) * P], qB[:, i, o:o + P], ident)
                    end(ins)
                b = begin(("BkT", i), "a")
                for g in range(4):
                    ins = nc.tensor.transpose(b[:, g * P:(g + 1) * P], kD[:, i, g * P:(g + 1) * P], ident)
                end(ins)
            evacuated(pe, ("BkT", NT - 1))

            NB_ = 16 * NT

            def scoresB(u):
                h, i = divmod(u, NT)
                e = 64 * (h % 2)
                b = begin(("BS", u), "a")
                end(mm(b[:, :], qT[e:e + 64, h // 2, i * P:(i + 1) * P], kTB[e:e + 64, h // 4, :], True, True))

            def transB(u):
                pe.wait_ge(S("B_probs"), u + 1)
                b = begin(("BT", u), "a")
                for k in range(4):
                    ins = nc.tensor.transpose(b[:, k * P:(k + 1) * P], pB[:, u % 3, k * P:(k + 1) * P], ident)
                end(ins)

            def pvB(h):
                e = 64 * (h % 2)
                evacuated(pe, ("BT", NT * h + 3))
                b = begin(("BO_", h), "v")
                for k in range(4):
                    ins = mm(b[e:e + 64, :], vB[:, k, (h // 4) * 64:(h // 4) * 64 + 64], ptB[:, h % 2, k, :],
                             k == 0, k == 3)
                end(ins)

            for u in range(NB_ + 4):
                if u < NB_:
                    scoresB(u)
                if 2 <= u < NB_ + 2:
                    transB(u - 2)
                if u >= 6 and (u - 6) % 4 == 0:
                    pvB((u - 6) // 4)
            out_proj("BO", 1)
            ple(1, None)

            norm("norm2")
            need(("C", 0))
            for i in range(NT):
                tm(("C", 0, i), "a", ("C", 0), i, 0, 512)
            used(("C", 0))
            need(("C", 1))
            for n in range(2):
                fm(("kvc", n), "v", ("C", 1), n * P)
            for i in range(NT):
                tm(("C", 1, i), "a", ("C", 1), i, 256, 256)
            used(("C", 1))
            need(("C", 2))
            for i in range(NT):
                tm(("C", 2, i), "a", ("C", 2), i, 0, 280)
            used(("C", 2))
            need(("C", 3))
            for s in range(4):
                fm(("C", 3, s), "v", ("C", 3), s * P)
            used(("C", 3))

            for n, name in enumerate(("W1K", "W1V")):
                need(name)
                pe.wait_ge(S("C_flat"), n + 1)
                b = begin(("hid", n), "v")
                for blk in range(2):
                    for ii in range(16):
                        ins = mm(b[:, blk * 64:blk * 64 + 64], W(name)[:, ii, blk * P:blk * P + P],
                                 fl[:, n, ii * 64:ii * 64 + 64], ii == 0, ii == 15)
                end(ins)
                used(name)
            pe.wait_ge(s_small, 64)
            evacuated(pe, ("hid", 1))
            b = begin("kcmp", "v")
            for blk in range(2):
                ins = mm(b[0:64, 0:64], w2[:, 0, blk, :], hid[:, 0, blk * 64:blk * 64 + 64], blk == 0, blk == 1)
            end(ins)
            b = begin("vcmp", "v")
            for g in range(2):
                for blk in range(2):
                    ins = mm(b[0:32, g * 64:g * 64 + 64], hid[:, 1, blk * 64 + g * 32:blk * 64 + g * 32 + 32],
                             w2[:, 1, blk, :], blk == 0, blk == 1)
            end(ins)
            pe.wait_ge(S("C_rope"), 4)
            for i in range(NT):
                for name, src in (("qp", q2), ("qr", q2r)):
                    b = begin((name, i), "a")
                    for j in range(4):
                        ins = nc.tensor.transpose(b[:, j * P:(j + 1) * P], src[:, i, j * P:(j + 1) * P], ident)
                    end(ins)
                b = begin(("kz", i), "a")
                for m in range(4):
                    ins = nc.tensor.transpose(b[:, m * P:(m + 1) * P], kd[:, i, m // 2, (m % 2) * P:(m % 2) * P + P], ident)
                end(ins)
            evacuated(pe, ("kz", NT - 1))
            pe.wait_ge(S("C_cmp"), 12)
            for i in range(NT):
                b = begin(("cs", i), "v")
                for h in range(8):
                    ins = mm(b[:, h * 32:h * 32 + 32], qTp[:, h // 2, i * P:(i + 1) * P], kcz[:, h // 4, h % 2, :],
                             True, True)
                end(ins)
            for i in range(NT):
                pe.wait_ge(S("C_pc"), i + 1)
                b = begin(("ct", i), "a")
                for g in range(2):
                    ins = nc.tensor.transpose(b[:, g * P:(g + 1) * P], smC[:, i % 2, g * P:(g + 1) * P], ident)
                end(ins)

            def scoresN(u):
                h, br, i = UN[u]
                q = qTr[:, h // 2, i * P:(i + 1) * P]
                k = kz[:, br, h // 4, h % 2, :]
                b = begin(("NS", u), "a")
                if i:
                    mm(b[:, 0:i * P], q, k[:, 0:i * P], True, True)
                d = b[:, i * P:(i + 1) * P]
                mm(d, q, k[:, i * P:(i + 1) * P], True, False)
                end(mm(d, identb[:, :], causalb[:, :], False, True))

            def transN(u):
                h, br, i = UN[u]
                pe.wait_ge(S("N_probs"), u + 1)
                b = begin(("NT", u), "a")
                for k in range(i + 1):
                    ins = nc.tensor.transpose(b[:, k * P:(k + 1) * P], pN[:, u % 3, k * P:(k + 1) * P], ident)
                end(ins)

            def pvN(h):
                e, g = 64 * (h % 2), h // 4
                evacuated(pe, ("NT", 8 * h + 7))
                b = begin(("NO", h), "v")
                mm(b[e:e + 64, :], vcz[:, g, h % 4, :], pTc[:, g, :], True, False)
                for br in range(2):
                    for k in (3, 2, 1, 0):
                        ins = mm(b[e:e + 64, k * P:T], vS[:, k, br, g * 64:g * 64 + 64],
                                 ptN[h % 2][:, br, k, k * P:T], False, br == 1 and k == 0)
                end(ins)

            pe.wait_ge(S("bf16_constants"), 2)
            for u in range(len(UN) + 4):
                if u < len(UN):
                    scoresN(u)
                if 2 <= u < len(UN) + 2:
                    transN(u - 2)
                if u >= 11 and (u - 11) % 8 == 0:
                    pvN((u - 11) // 8)

            for s in range(13):
                n = 4 + s // 4
                if s % 4 == 0:
                    need(("C", n))
                fm(("R", s), "a", ("C", n), (s % 4) * P)
                if s % 4 == 3 or s == 12:
                    used(("C", n))
            need(("C", 8))
            for s in range(4):
                fm(("C", 8, s), "v", ("C", 8), s * P)
            used(("C", 8))
            pe.wait_ge(S("R_twd"), 1)
            for j in range(4):
                b = begin(("W", j), "a")
                end(mm(b[:, :], wa[0:64, j * P:(j + 1) * P], wdad[0:64, :], True, True))
            for j in range(4):
                b = begin(("A_", j), "a")
                end(mm(b[:, :], wa[64:128, j * P:(j + 1) * P], wdad[64:128, :], True, True))

            def head_sums(key, src):
                b = begin(key, "v")
                for i in range(NT):
                    for j in range(4):
                        c = (4 * i + j) * 2
                        ins = mm(b[:, c:c + 2], src[:, j, i * P:(i + 1) * P], C("heads"), True, True)
                end(ins)

            def spread(key, j):
                b = begin((key, j), "v")
                for i in range(NT):
                    o = (4 * i + j) * P
                    ins = nc.tensor.transpose(b[:, i * P:(i + 1) * P], bx[:, o:o + P], ident)
                end(ins)

            pe.wait_ge(S("R_sq"), 4)
            head_sums("ks", sq)
            pe.wait_ge(S("R_kx"), 1)
            for j in range(4):
                spread("kb", j)
            pe.wait_ge(S("R_rk"), 4)
            head_sums("bs", sq)
            pe.wait_ge(S("R_bx"), 1)
            for j in range(4):
                spread("bb", j)

            def four_heads(key, consumer, left, right):
                for bt in range(2):
                    b = begin(key + (bt,), consumer)
                    for q in range(4):
                        h = 4 * bt + q
                        ins = mm(b[:, q * P:(q + 1) * P], left(h), right(h), True, True)
                    end(ins)

            def turned(key, consumer, src):
                for bt in range(2):
                    b = begin(key + (bt,), consumer)
                    for q in range(4):
                        ins = nc.tensor.transpose(b[:, q * P:(q + 1) * P], src(4 * bt + q), ident)
                    end(ins)

            mA, mE, mD = (lambda h: AE[:, h, 0, :]), (lambda h: AE[:, h, 1, :]), (lambda h: Dm[:, h, :])
            mA2, mD2 = (lambda h: A2[:, h, :]), (lambda h: D2[:, h, :])
            mQa, mQb = (lambda h: Qa[:, h, :]), (lambda h: Qb[:, h, :])
            pe.wait_ge(S("R_ops"), 4)
            for i in range(NT):
                ti = slice(i * P, (i + 1) * P)
                for h in range(8):
                    e, j = 64 * (h % 2), h // 2
                    b = begin(("gr", i, h), "v")
                    mm(b[:, 0:256], aF[e:e + 64, j, ti], AR[e:e + 64, j, i, :, :], True, True)
                    end(mm(b[:, 256:512], iP[e:e + 64, j, ti], AR[e:e + 64, j, i, :, :], True, True))
                for n, src in enumerate((lambda j: AR[:, j, i, 0, :], lambda j: aF[:, j, ti], lambda j: iP[:, j, ti],
                                         lambda j: vF[:, j, ti])):
                    b = begin(("tm", i, n), "a")
                    for j in range(4):
                        ins = nc.tensor.transpose(b[:, j * P:(j + 1) * P], src(j), ident)
                    end(ins)
                evacuated(pe, ("gr", i, 7))
                turned(("D", i), "a", mA)
                b = begin(("X", i), "a")
                evacuated(pe, ("tm", i, 3))
                for h in range(8):
                    ins = mm(b[:, h * 64:h * 64 + 64], B3[:, h, 1, :], vtm[:, h * 64:h * 64 + 64], True, True)
                end(ins)
                evacuated(pe, ("D", i, 1))
                four_heads(("A2", i), "a", mD, mA)
                four_heads(("D2", i), "v", mA, mD)
                evacuated(pe, ("A2", i, 1))
                evacuated(pe, ("D2", i, 1))
                four_heads(("Q2", i), "v", mD2, mQa)
                four_heads(("A4", i), "a", mD2, mA2)
                four_heads(("D4", i), "a", mA2, mD2)
                evacuated(pe, ("D4", i, 1))
                evacuated(pe, ("Q2", i, 1))
                four_heads(("Q3", i), "v", mD, mQb)
                four_heads(("D8", i), "a", mA, mD)
                evacuated(pe, ("D8", i, 1))
                evacuated(pe, ("Q3", i, 1))
                four_heads(("Q4", i), "v", mD2, mQa)
                evacuated(pe, ("Q4", i, 1))
                turned(("QT", i), "a", mQb)
                evacuated(pe, ("QT", i, 1))
                four_heads(("KT", i), "a", mE, mA2)
                four_heads(("K", i), "v", mA2, mE)
                evacuated(pe, ("KT", i, 1))
                evacuated(pe, ("K", i, 1))
                four_heads(("K2", i), "a", mA, mD)
                evacuated(pe, ("K2", i, 1))
                four_heads(("Q5", i), "v", mD2, mQb)
                evacuated(pe, ("Q5", i, 1))
                four_heads(("RR", i), "v", mD, mQa)
                evacuated(pe, ("RR", i, 1))
                evacuated(pe, ("X", i))
                four_heads(("HG", i), "a", mQb, lambda h: XG[:, h, :])
                evacuated(pe, ("HG", i, 1))
                b = begin(("rho", i), "v")
                for h in range(8):
                    e, j = 64 * (h % 2), h // 2
                    ins = mm(b[e:e + 64, j * P:(j + 1) * P], HG[:, h, 64:128], B3[:, h, 0, :], True, True)
                end(ins)
                for c in range(2):
                    cs = slice(64 * c, 64 * c + 64)
                    b = begin(("M", i, c), "v")
                    for h in range(8):
                        e, j = 64 * (h % 2), h // 2
                        ins = mm(b[e:e + 64, j * 64:j * 64 + 64], HG[cs, h, 64:128], btm[cs, h * 64:h * 64 + 64], True, True)
                    end(ins)
                for c in range(2):
                    cs = slice(64 * c, 64 * c + 64)
                    b = begin(("Bm", i, c), "a")
                    for h in range(8):
                        e, j = 64 * (h % 2), h // 2
                        o = b[e:e + 64, j * 64:j * 64 + 64]
                        mm(o, btm[cs, h * 64:h * 64 + 64], HG[cs, h, 0:64], True, False)
                        ins = mm(o, ktm[cs, h * 64:h * 64 + 64], vtm[cs, h * 64:h * 64 + 64], False, True)
                    end(ins)
                b = begin(("Y1", i), "a")
                for h in range(8):
                    e, j = 64 * (h % 2), h // 2
                    o = b[e:e + 64, j * P:(j + 1) * P]
                    mm(o, HG[:, h, 0:64], B3[:, h, 0, :], True, False)
                    ins = mm(o, vtm[:, h * 64:h * 64 + 64], B3[:, h, 2, :], False, True)
                end(ins)
                for c in range(2):
                    k = 2 * i + c
                    evacuated(pe, ("M", i, c))
                    pe.wait_ge(S("R_state"), k + 1)
                    b = begin(("St", k), "v")
                    for h in range(8):
                        e, j = 64 * (h % 2), h // 2
                        ins = mm(b[e:e + 64, j * 64:j * 64 + 64], MT[e:e + 64, c, j, :],
                                 Sst[e:e + 64, k % 4, j * 64:j * 64 + 64], True, True)
                    end(ins)
                evacuated(pe, ("rho", i))
                b = begin(("Y2", i), "v")
                for c in range(2):
                    for h in range(8):
                        e, j = 64 * (h % 2), h // 2
                        o = j * P + 64 * c
                        ins = mm(b[e:e + 64, o:o + 64], Sst[e:e + 64, (2 * i + c) % 4, j * 64:j * 64 + 64],
                                 RHO[e:e + 64, o:o + 64], True, True)
                end(ins)

            evacuated(pe, ("Y2", NT - 1))
            head_sums("gn1", yF)
            pe.wait_ge(S("R_gx"), 1)
            for j in range(4):
                spread("gb1", j)
            pe.wait_ge(S("R_gsq"), 4)
            head_sums("gn2", sq)
            pe.wait_ge(S("R_gx"), 2)
            for j in range(4):
                spread("gb2", j)
            pe.wait_ge(S("R_done"), 4)
            for n in range(2):
                need(("CO", n))
                for i in range(NT):
                    b = begin(("CO", n, i), "v")
                    w = W(("CO", n))
                    for k in range(KB):
                        src = mixA[:, k, :] if k < 4 else mixB[:, k - 4, :]
                        ins = mm(b[:, :], src[:, i * P:(i + 1) * P], w[:, k, :], k == 0, k == KB - 1)
                    end(ins)
                used(("CO", n))

        @block.scalar
        def _(act):
            for l in range(NT):
                act.dma_start(x[:, l, :], A["x"][0].rearrange("(r c) d -> c r d", r=GR)[CT * l:CT * l + CT])\
                   .then_inc(s_x[l], 16)

            def copy(o, i, scale=1.0):
                return nc.scalar.activation(o, i, ACT.Copy, scale=scale)

            nsq = [0]

            def square(tag, i, col):
                if nsq[0]:
                    act.wait_ge(S("squares_done"), nsq[0])
                nsq[0] += 1
                nc.scalar.activation(junk, x[:, i, :], ACT.Square, accum_out=stat[:, col + i:col + i + 1])\
                  .then_inc(S("squares_done"), 1)
                act.wait_ge(S("squares_done"), nsq[0])
                act.sem_inc(S("ss_" + tag), 1)

            def squares(tag, ready, col):
                for i in range(NT):
                    ready(i)
                    square(tag, i, col)

            split = [0]

            def high(upto):
                while split[0] <= min(upto, len(halves) - 1):
                    n = split[0]
                    act.wait_ge(raw_loaded[n % NRAW], 16 * (n // NRAW + 1))
                    if n >= NHI:
                        act.wait_ge(filled, half_last[n - NHI] + 1)
                    nc.scalar.activation(rounded(high_slot(n)), raw_slot(n), ACT.Copy).then_inc(s_whi, 1)
                    split[0] += 1

            def high_tile(tag, i):
                for hf in range(2):
                    evacuated(act, (tag, i, hf))
                    ks = slice(4 * hf, 4 * hf + 4)
                    src = low[tag].rearrange("p (k t) -> p k t", k=KB)
                    nc.scalar.activation(rounded(hT[:, ks, i * P:(i + 1) * P]), src[:, ks, i * P:(i + 1) * P],
                                         ACT.Copy).then_inc(S("hi_" + tag), 1)

            def head(tag, first, drain):
                high_tile(tag, 0)
                high_tile(tag, 1)
                drain(0)
                high_tile(tag, 2)
                high(first + 1)
                drain(1)
                high_tile(tag, 3)
                drain(2)
                drain(3)

            def high_pair(j):
                nc.scalar.activation(rounded(o_high[:, T * j:T * j + T]), hT[:, j, :], ACT.Copy)\
                    .then_inc(S("o_high"), 1)

            def loaded(i):
                act.wait_ge(s_x[i], 16)

            key = "vec"
            b = take(act, key)
            give(copy(vec[:, :], b[:, 0:P]), key)
            for i in range(NT):
                loaded(i)
                square("norm0", i, 0)
                if i == 0:
                    high(0)

            def drain_v(n, i):
                key = ("Av", n, i)
                b = take(act, key)
                give(copy(va[:, i, 256 * (n - 8):256 * (n - 7)], b[:, 0:256]), key)

            head("norm0", 0, lambda i: drain_v(AORD[0], i))
            for n in AORD[1:]:
                high(HI[("A", n)] + 1)
                if n in range(8, 12):
                    for i in range(NT):
                        drain_v(n, i)
                elif n < 8:
                    for s in range(2):
                        key = ("A", n, s)
                        b = take(act, key)
                        j = (2 * n + s) % 8
                        if n < 4:
                            copy(qT[:, j, 0:448], b[:, 64:512], 0.125)
                            give(copy(qT[:, j, 448:512], b[:, 0:64], 0.125), key)
                        else:
                            give(copy(kT[:, j, :], b[:, :]), key)
                else:
                    for s in range(2):
                        k = 2 * (n - 12) + s
                        b = take(act, ("A", n, s))
                        if k >= 2:
                            act.wait_ge(drained["v"], nth[("A", 12 + (k - 2) // 2, (k - 2) % 2)])
                        nc.scalar.activation(th[:, k % 2, :], b[:, :], ACT.Tanh, scale=0.5).then_inc(S("A_tanh"), 1)
            high(HI[("AO", 1)])

            def expA(h):
                for hf in range(2):
                    act.wait_ge(S("A_max"), 2 * h + hf + 1)
                    if h >= 2:
                        act.wait_ge(filled, J[("AT", h - 2, hf)] + 1)
                    for m in range(2):
                        c = 64 + 8 * (h % 2) + 2 * hf + m
                        o = 512 * hf + 256 * m
                        ins = nc.scalar.activation(pA[:, h % 2, o:o + 256], sA[:, h % 2, o:o + 256], ACT.Exp,
                                                   bias=stat[:, c:c + 1], accum_out=stat[:, c + 16:c + 17])
                    ins.then_inc(S("A_exp"), 1)

            def ptA_copy(h):
                for hf in range(2):
                    key = ("AT", h, hf)
                    b = take(act, key)
                    if h >= 3:
                        act.wait_ge(filled, J[("AO_", h - 3)] + 1)
                    give(copy(ptA[:, h % 3, hf, :], b[:, :]), key)

            for h in range(16 + 1):
                if h < 16:
                    expA(h)
                if h >= 1:
                    ptA_copy(h - 1)
                if h >= 5 and h % 2:
                    evacuated(act, ("AO_", h - 4))
                    act.wait_ge(S("A_o_mid"), h - 3)
                    high_pair((h - 5) // 2)
            for h in (13, 15):
                evacuated(act, ("AO_", h))
                act.wait_ge(S("A_o_mid"), h + 1)
                high_pair(h // 2)

            def ple(l, tag, col, after):
                act.wait_ge(s_pp[l], 16)
                nc.scalar.activation(rounded(pw_hi), pw_lo, ACT.Copy).then_inc(S("pw_high"), 1)
                for k in range(2):
                    b = take(act, ("pT", l, k))
                    nc.scalar.activation(rounded(p_T[:, k, :]), b[:, :], ACT.Copy).then_inc(S("p_high"), 1)
                for n in (1, 2, 3):
                    high(HI[(tag, n)] + 1)
                for i in range(NT):
                    evacuated(act, (tag, 3, i))
                    square(f"ple{l}", i, col)

                def drain(n, i):
                    key = ("PG", l, n, i)
                    u = 4 * n + i
                    b = take(act, key)
                    if u >= 4:
                        act.wait_ge(drained["v"], nth[("PP", l, (u - 4) // 4, (u - 4) % 4)])
                    give(nc.scalar.activation(thp[:, u % 4, :], b[:, 0:256], ACT.Tanh, scale=0.5), key)

                head(f"ple{l}", HI[("PG", l, 0)], lambda i: drain(0, i))
                for n in (1, 2, 3):
                    high(HI[("PG", l, n)] + 1)
                    for i in range(NT):
                        drain(n, i)
                        if n == 3 and i >= 1:
                            after(i - 1)
                after(NT - 1)

            def finished(l, i):
                act.wait_ge(S("x_ple"), 16 * l + 12 + i + 1)

            def square1(i):
                finished(0, i)
                square("norm1", i, 8)

            ple(0, "AO", 4, square1)

            def drain_B(n, i):
                key = ("B", n, i)
                b = take(act, key)
                u = 4 * n + i
                if n < 5:
                    if u >= 2:
                        act.wait_ge(S("B_sq_read"), u - 1)
                    nc.scalar.activation(sqB[:, u % 2, :], b[:, 0:256], ACT.Square).then_inc(S("B_sq"), 1)
                if n < 4:
                    give(copy(qB[:, i, 256 * n:256 * n + 256], b[:, 0:256]), key)
                else:
                    give(copy((kB if n == 4 else vB)[:, i, :], b[:, 0:256]), key)

            head("norm1", HI[("B", 0)], lambda i: drain_B(0, i))
            for n in range(1, 10):
                high(HI[("B", n)] + 1)
                if n < 6:
                    for i in range(NT):
                        drain_B(n, i)
                else:
                    for s in range(2):
                        k = 2 * (n - 6) + s
                        b = take(act, ("B", n, s))
                        if k >= 2:
                            act.wait_ge(drained["v"], nth[("B", 6 + (k - 2) // 2, (k - 2) % 2)])
                        nc.scalar.activation(th[:, k % 2, :], b[:, :], ACT.Tanh, scale=0.5).then_inc(S("B_tanh"), 1)
            high(HI[("BO", 1)])
            for i in range(NT):
                for hf in range(2):
                    key = ("BqT", i, hf)
                    b = take(act, key)
                    give(copy(qT[:, 4 * hf:4 * hf + 4, i * P:(i + 1) * P], b[:, :].rearrange("p (j t) -> p j t", j=4)), key)
                key = ("BkT", i)
                b = take(act, key)
                give(copy(kTB[:, :, i * P:(i + 1) * P], b[:, :].rearrange("p (j t) -> p j t", j=4)), key)

            NB_ = 16 * NT
            for u in range(NB_ + 2):
                if u < NB_:
                    key = ("BS", u)
                    b = take(act, key)
                    act.wait_ge(S("B_max"), u + 1)
                    if u >= 3:
                        act.wait_ge(filled, J[("BT", u - 3)] + 1)
                    c = 128 + u % 4
                    give(nc.scalar.activation(pB[:, u % 3, :], b[:, :], ACT.Exp, bias=stat[:, c:c + 1],
                                              accum_out=stat[:, c + 4:c + 5]), key)
                if u >= 2:
                    v = u - 2
                    h, i = divmod(v, NT)
                    key = ("BT", v)
                    b = take(act, key)
                    if h >= 2:
                        act.wait_ge(filled, J[("BO_", h - 2)] + 1)
                    give(copy(ptB[:, h % 2, :, i * P:(i + 1) * P], b[:, :].rearrange("p (k t) -> p k t", k=4)), key)
                if u >= 16 and u % 8 == 0:
                    j = u // 8 - 2
                    evacuated(act, ("BO_", 2 * j + 1))
                    high_pair(j)
            evacuated(act, ("BO_", 15))
            high_pair(7)

            def square2(i):
                finished(1, i)
                square("fin", i, 16)

            ple(1, "BO", 12, square2)
            squares("norm2", lambda i: act.wait_ge(S("x_fin"), i + 1), 20)
            for i in range(NT):
                key = ("C", 0, i)
                b = take(act, key)
                copy(q2[:, i, :], b[:, :])
                give(copy(q2r[:, i, :], b[:, :]), key)
            for n in (1, 2):
                for i in range(NT):
                    key = ("C", n, i)
                    b = take(act, key)
                    if n == 2:
                        nc.scalar.activation(gt[:, i, :], b[:, 256:280], ACT.Tanh, scale=0.5).then_inc(S("C_gates"), 1)
                    copy(ap(kd[:, i, n - 1, :], [(P, 2), (64, 2), (1, 64)]), ap(b[:, 0:P], [(64, 2), (0, 2), (1, 64)]))
                    give(copy(vS[:, i, n - 1, :], b[:, P:256]), key)

            def tanhs(keys, name):
                for k, key in enumerate(keys):
                    b = take(act, key)
                    if k >= 2:
                        evacuated(act, keys[k - 2])
                    nc.scalar.activation(thC[:, k % 2, :], b[:, :], ACT.Tanh, scale=0.5).then_inc(S(name), 1)

            tanhs([("C", 3, s) for s in range(4)], "C_tanh")
            for n in range(2):
                b = take(act, ("hid", n))
                if n:
                    evacuated(act, ("hid", 0))
                nc.scalar.activation(thh, b[:, 0:128], ACT.Tanh, scale=0.5).then_inc(S("C_thh"), 1)
            act.wait_ge(S("C_clear"), 3)
            for i in range(NT):
                for name, dst in (("qp", qTp), ("qr", qTr)):
                    key = (name, i)
                    b = take(act, key)
                    give(copy(dst[:, :, i * P:(i + 1) * P], b[:, :].rearrange("p (j t) -> p j t", j=4), 0.125), key)
                key = ("kz", i)
                b = take(act, key)
                for e in range(2):
                    es = slice(64 * e, 64 * e + 64)
                    ins = copy(ap(kz[es, 0, 0, e, :], [(1024, 4), (1, P)], i * P), b[es, :].rearrange("p (j t) -> p j t", j=4))
                give(ins, key)
            for i in range(NT):
                act.wait_ge(S("C_cs"), i + 1)
                nc.scalar.activation(smC[:, i % 2, :], smC[:, i % 2, :], ACT.Exp).then_inc(S("C_ce"), 1)
                if i >= 1:
                    key = ("ct", i - 1)
                    b = take(act, key)
                    give(copy(pTc[:, :, (i - 1) * P:i * P], b[:, 0:256].rearrange("p (g t) -> p g t", g=2)), key)
            key = ("ct", NT - 1)
            b = take(act, key)
            give(copy(pTc[:, :, (NT - 1) * P:T], b[:, 0:256].rearrange("p (g t) -> p g t", g=2)), key)

            for u in range(len(UN) + 2):
                if u < len(UN):
                    nk = (UN[u][2] + 1) * P
                    key = ("NS", u)
                    b = take(act, key)
                    act.wait_ge(S("N_max"), u + 1)
                    if u >= 3:
                        act.wait_ge(filled, J[("NT", u - 3)] + 1)
                    c = 400 + u % 4
                    give(nc.scalar.activation(pN[:, u % 3, 0:nk], b[:, 0:nk], ACT.Exp, bias=stat[:, c:c + 1],
                                              accum_out=stat[:, c + 4:c + 5]), key)
                if u >= 2:
                    h, br, i = UN[u - 2]
                    key = ("NT", u - 2)
                    b = take(act, key)
                    if h >= 2:
                        act.wait_ge(filled, J[("NO", h - 2)] + 1)
                    give(copy(ptN[h % 2][:, br, 0:i + 1, i * P:(i + 1) * P],
                              b[:, 0:(i + 1) * P].rearrange("p (k t) -> p k t", k=i + 1)), key)

            evacuated(act, ("NO", 7))
            act.wait_ge(S("R_rawzero"), 1)
            for s in range(13):
                key = ("R", s)
                b = take(act, key)
                if s >= 3:
                    act.wait_ge(S("R_mix"), s - 2)
                give(copy(raw[:, s % 3, 1:513], b[:, :]), key)
            tanhs([("C", 8, s) for s in range(4)], "R_tanh")
            act.wait_ge(S("R_mix"), 13)
            nc.scalar.activation(wdad[0:64, :], wdad[0:64, :], ACT.Tanh).then_inc(S("R_twd"), 1)
            act.wait_ge(S("R_half"), 1)
            for j in range(4):
                key = ("W", j)
                b = take(act, key)
                give(nc.scalar.activation(lw[:, j, :], b[:, :], ACT.Tanh, bias=stat[:, 576 + j:577 + j], scale=0.5), key)
            for j in range(4):
                key = ("A_", j)
                b = take(act, key)
                give(nc.scalar.activation(aF[:, j, :], b[:, :], ACT.Tanh, bias=stat[:, 580 + j:581 + j], scale=0.5), key)
            for j in range(4):
                act.wait_ge(S("R_kkraw"), j + 1)
                nc.scalar.activation(sq[:, j, :], kk[:, j, :], ACT.Square).then_inc(S("R_sq"), 1)
            for j in range(4):
                act.wait_ge(S("R_cum"), j + 1)
                nc.scalar.activation(iP[:, j, :], cum[:, j, :], ACT.Exp, scale=-1.0).then_inc(S("R_P"), 1)
                nc.scalar.activation(lw[:, j, :], lw[:, j, :], ACT.Exp).then_inc(S("R_P"), 1)
                nc.scalar.activation(cum[:, j, :], cum[:, j, :], ACT.Exp).then_inc(S("R_P"), 1)

            def move(key, dst):
                b = take(act, key)
                give(copy(dst, b[:, :].rearrange("p (h t) -> p h t", h=4)), key)

            def moves(key, dst):
                for bt in range(2):
                    move(key + (bt,), dst[:, 4 * bt:4 * bt + 4, :])

            def As():
                return AE[:, :, 0, :]

            act.wait_ge(S("R_ops"), 4)
            for i in range(NT):
                key = ("tm", i, 0)
                b = take(act, key)
                give(copy(XG[:, :, 64:128], b[:, :].rearrange("p (h k) -> p h k", h=8)), key)
                for n, dst in ((1, btm), (2, ktm), (3, vtm)):
                    key = ("tm", i, n)
                    b = take(act, key)
                    give(copy(dst, b[:, :]), key)
                moves(("D", i), Dm)
                key = ("X", i)
                b = take(act, key)
                give(copy(XG[:, :, 0:64], b[:, :].rearrange("p (h k) -> p h k", h=8)), key)
                moves(("A2", i), A2)
                moves(("A4", i), As())
                moves(("D4", i), Dm)
                moves(("D8", i), D2)
                moves(("QT", i), A2)
                moves(("KT", i), Dm)
                moves(("K2", i), D2)
                moves(("HG", i), HG)
                for c in range(2):
                    key = ("Bm", i, c)
                    b = take(act, key)
                    if i >= 1:
                        act.wait_ge(S("R_state"), 2 * i + 1)
                    give(copy(Bm[:, c, :], b[:, 0:256]), key)
                key = ("Y1", i)
                b = take(act, key)
                give(copy(yF[:, :, i * P:(i + 1) * P], b[:, :].rearrange("p (j t) -> p j t", j=4)), key)
            for j in range(4):
                act.wait_ge(S("R_centred"), j + 1)
                nc.scalar.activation(sq[:, j, :], yF[:, j, :], ACT.Square).then_inc(S("R_gsq"), 1)
            squares("out", lambda i: evacuated(act, ("CO", 1, i)), 24)

        @block.vector
        def _(dve):
            chain = [0]

            def link(ins):
                chain[0] += 1
                ins.then_inc(s_v, 1)
                dve.wait_ge(s_v, chain[0])

            TT, TS, STT = nc.vector.tensor_tensor, nc.vector.tensor_scalar, nc.vector.scalar_tensor_tensor

            def rsqrt(y, v, t):
                link(TS(y.bitcast(I32), v.bitcast(I32), 1, None, ALU.arith_shift_right))
                link(TS(y.bitcast(I32), y.bitcast(I32), -1.0, RSQRT_MAGIC, ALU.mult, ALU.add))
                for _ in range(3):
                    link(STT(t, y, -0.5, y, ALU.mult, ALU.mult))
                    link(TT(t, t, v, ALU.mult))
                    link(STT(y, t, 1.5, y, ALU.add, ALU.mult))

            def rstd_tile(tag, col, i):
                dve.wait_ge(S("ss_" + tag), i + 1)
                v, y = stat[:, col + i:col + i + 1], stat[:, 32 + i:33 + i]
                link(TS(v, v, 1.0 / D, EPS, ALU.mult, ALU.add))
                rsqrt(y, v, stat[:, 36 + i:37 + i])
                return y

            def scale_tile(tag, col, i):
                y = rstd_tile(tag, col, i)
                if i >= 2:
                    dve.wait_ge(filled, J[(tag, i - 2, 1)] + 1)
                TS(xn[:, i % 2, :], x[:, i, :], y, None, ALU.mult).then_inc(S("xn_" + tag), 1)

            def gain_tile(tag, i):
                g = vcol(tag, 0, 8)
                dst = low[tag].rearrange("p (k t) -> p k t", k=KB)
                for hf in range(2):
                    key = (tag, i, hf)
                    b = take(dve, key)
                    give(TT(dst[:, 4 * hf:4 * hf + 4, i * P:(i + 1) * P], b[:, :].rearrange("p (k t) -> p k t", k=4),
                            ap(g, [(1, 4), (0, P)], 4 * hf), ALU.mult), key)

            def low_tile3(tag):
                dst = low[tag].rearrange("p (k t) -> p k t", k=KB)
                for hf in range(2):
                    dve.wait_ge(S("hi_" + tag), 6 + hf + 1)
                    v = dst[:, 4 * hf:4 * hf + 4, 3 * P:T]
                    TT(rounded(v), v, read_back(hT[:, 4 * hf:4 * hf + 4, 3 * P:T]), ALU.subtract).then_inc(S("lo3_" + tag), 1)

            def norm_after(tag, col, last):
                for i in range(NT):
                    if i == 3:
                        gain_tile(tag, 0)
                    last(i)
                    if i >= 1:
                        scale_tile(tag, col, i - 1)
                gain_tile(tag, 1)
                scale_tile(tag, col, 3)

            def rstd(tag, col, width=D, eps=EPS):
                dve.wait_ge(S("ss_" + tag), NT)
                v = stat[:, col:col + NT]
                link(TS(v, v, 1.0 / width, eps, ALU.mult, ALU.add))
                y = stat[:, 32:32 + NT]
                rsqrt(y, v, stat[:, 36:36 + NT])
                return y

            def norm(tag, col, natural=False):
                y = rstd(tag, col)
                g = vcol(tag, 0, 8)

                def evac(i):
                    for hf in range(2):
                        key = (tag, i, hf)
                        b = take(dve, key)
                        if natural:
                            o = ap(hT[:, 4 * hf, :], [(T, 4), (1, CT), (GW, GR)], CT * i)
                            s = b[:, :].rearrange("p (k c r) -> p k c r", k=4, r=GR)
                            w = ap(g, [(1, 4), (0, CT), (0, GR)], 4 * hf)
                        else:
                            o = hT[:, 4 * hf:4 * hf + 4, i * P:(i + 1) * P]
                            s = b[:, :].rearrange("p (k t) -> p k t", k=4)
                            w = ap(g, [(1, 4), (0, P)], 4 * hf)
                        give(TT(o, s, w, ALU.mult), key)

                for i in range(NT):
                    if i >= 2:
                        dve.wait_ge(filled, J[(tag, i - 2, 1)] + 1)
                    TS(xn[:, i % 2, :], x[:, i, :], y[:, i:i + 1], None, ALU.mult).then_inc(S("xn_" + tag), 1)
                    if i >= 1:
                        evac(i - 1)
                evac(NT - 1)

            nc.vector.memset(vrow[64:P, :], 0.0).then_inc(S("vrow_zero"), 1)
            nc.vector.memset(rrev, 0.0).then_inc(s_rpbr, 1)
            dve.wait_ge(s_rpb, 16)
            dve.wait_ge(s_rpbr, 1)
            nc.vector.tensor_copy(ap(rrev, [(-64, 15), (-1, 31)], 1007), rpb_in[0:16, 0:465].rearrange(
                "p (a b) -> p a b", a=15)).then_inc(s_rpbr, 1)
            dve.wait_ge(s_cst, 16)
            nc.vector.tensor_copy(identb[:, :], ident).then_inc(S("bf16_constants"), 1)
            nc.vector.tensor_copy(causalb[:, :], C("causal")).then_inc(S("bf16_constants"), 1)
            evacuated(dve, "vec")
            norm_after("norm0", 0, lambda i: None)
            gain_tile("norm0", 2)
            gain_tile("norm0", 3)
            low_tile3("norm0")

            def gates(keys, name, dst):
                for k, key in enumerate(keys):
                    b = take(dve, key)
                    dve.wait_ge(S(name), k + 1)
                    give(STT(dst[:, k, :], th[:, k % 2, :], 1.0, b[:, :], ALU.add, ALU.mult), key)

            gates([("A", 12 + k // 2, k % 2) for k in range(8)], "A_tanh", G)

            dve.wait_ge(S("bias_edge"), 2)

            def frontA(h):
                dve.wait_ge(s_bias, 3 * h + 3)
                for hf in range(2):
                    key = ("AS", h, hf)
                    b = take(dve, key)
                    if h >= 2:
                        dve.wait_ge(S("A_exp"), 2 * (h - 2) + hf + 1)
                    s = sA[:, h % 2, 512 * hf:512 * hf + 512]
                    w = ap(bias[:, h % 2, :], [(0, 2), (1, 256)]) if hf == 0 else \
                        bias[:, h % 2, :].rearrange("p (m n) -> p m n", m=2)
                    ins = TT(s.rearrange("p (m n) -> p m n", m=2), b[:, :].rearrange("p (m n) -> p m n", m=2), w, ALU.add)
                    give(ins, key)
                    evacuated(dve, key)
                    c = 64 + 8 * (h % 2) + 2 * hf
                    ins = nc.vector.tensor_reduce(stat[:, c:c + 2], s.rearrange("p (m n) -> p m n", m=2), X,
                                                  ALU.max, negate=True)
                    ins.then_inc(S("A_max"), 1)

            def probsA(h):
                for hf in range(2):
                    dve.wait_ge(S("A_exp"), 2 * h + hf + 1)
                    c = 64 + 8 * (h % 2) + 2 * hf
                    link(nc.vector.reciprocal(stat[:, c + 32:c + 34], stat[:, c + 16:c + 18]))
                    for m in range(2):
                        o = 512 * hf + 256 * m
                        ins = TS(pA[:, h % 2, o:o + 256], pA[:, h % 2, o:o + 256], stat[:, c + 32 + m:c + 33 + m],
                                 None, ALU.mult)
                    ins.then_inc(S("A_probs"), 1)

            def outA(h):
                e, j = 64 * (h % 2), h // 2
                key = ("AO_", h)
                b = take(dve, key)
                g = G[e:e + 64, j, :]
                o = hT[e:e + 64, j, :]
                s = b[e:e + 64, :]
                STT(o[:, 64:512], s[:, 0:448], 0.5, g[:, 64:512], ALU.mult, ALU.mult).then_inc(S("A_o_mid"), 1)
                give(STT(o[:, 0:64], s[:, 448:512], 0.5, g[:, 0:64], ALU.mult, ALU.mult), key)

            for h in range(16 + 3):
                if h < 16:
                    frontA(h)
                if 1 <= h < 17:
                    probsA(h - 1)
                if h >= 3:
                    outA(h - 3)
            def add_proj(tag, n, i, w):
                key = (tag, n, i)
                b = take(dve, key)
                xs = x[:, i, w * n:w * n + w]
                give(TT(xs, xs, b[:, 0:w], ALU.add), key)
                evacuated(dve, key)

            def ple(l, tag, col, after):
                for i in range(NT):
                    add_proj(tag, 0, i, 256)
                for k in range(2):
                    key = ("pT", l, k)
                    b = take(dve, key)
                    dve.wait_ge(S("p_high"), 2 * l + k + 1)
                    give(TT(rounded(p_lo[:, k, :]), b[:, :], read_back(p_T[:, k, :]), ALU.subtract), key)
                for n in (1, 2):
                    for i in range(NT):
                        add_proj(tag, n, i, 256)
                norm_after(f"ple{l}", col, lambda i: add_proj(tag, 3, i, 256))

                def add(n, i):
                    key = ("PP", l, n, i)
                    u = 4 * n + i
                    b = take(dve, key)
                    evacuated(dve, ("PG", l, n, i))
                    give(STT(tp[:, u % 2, :], thp[:, u % 4, :], 1.0, b[:, 0:256], ALU.add, ALU.mult), key)
                    evacuated(dve, key)
                    xs = x[:, i, 256 * n:256 * n + 256]
                    STT(xs, tp[:, u % 2, :], 0.5, xs, ALU.mult, ALU.add).then_inc(S("x_ple"), 1)

                add(0, 0)
                gain_tile(f"ple{l}", 2)
                add(0, 1)
                gain_tile(f"ple{l}", 3)
                low_tile3(f"ple{l}")
                add(0, 2)
                add(0, 3)
                for n in (1, 2):
                    for i in range(NT):
                        add(n, i)
                after(lambda i: add(3, i))

            ple(0, "AO", 4, lambda last: norm_after("norm1", 8, last))
            gain_tile("norm1", 2)
            gain_tile("norm1", 3)
            low_tile3("norm1")

            dve.wait_ge(S("gqk_loaded"), 32)
            cb, sbn = CAT["ropeb"][0], CAT["ropeb"][0] + NT * HD
            tab = cst[:, cb:cb + 2 * NT * HD]
            for n, (dst, sc) in enumerate(((tabq, 0.125), (tabk, 1.0))):
                g = gqk[:, 64 * n:64 * n + 64]
                o = ap(dst[:, 0, :], [(64, 4), (1, 64)])
                STT(o, ap(tab, [(64, 4), (1, 64)]), sc, ap(g, [(0, 4), (1, 64)]), ALU.mult, ALU.mult)
                for hf in range(2):
                    for s in range(2):
                        a = 32 * s + 16 * hf
                        STT(ap(dst[:, 1, :], [(64, 4), (1, 16)], a), ap(tab, [(64, 4), (1, 16)], NT * HD + a), sc,
                            ap(g, [(0, 4), (1, 16)], 32 * s + 16 * (1 - hf)), ALU.mult, ALU.mult)\
                            .then_inc(S("B_tab"), 1)
            dve.wait_ge(S("B_tab"), 8)
            ssq = stat[:, 160:240].rearrange("p (i h) -> p i h", i=NT)
            for n in range(5):
                for i in range(NT):
                    u = 4 * n + i
                    dve.wait_ge(S("B_sq"), u + 1)
                    nc.vector.tensor_reduce(ssq[:, i, 4 * n:4 * n + 4],
                                            sqB[:, u % 2, :].rearrange("p (h d) -> p h d", d=64), X, ALU.add)\
                        .then_inc(S("B_sq_read"), 1)
            dve.wait_ge(S("B_sq_read"), 20)
            link(TS(stat[:, 160:240], stat[:, 160:240], 1.0 / HD, EPS, ALU.mult, ALU.add))
            rsqrt(stat[:, 240:320], stat[:, 160:240], stat[:, 320:400])
            evacuated(dve, ("B", 4, 3))

            def rope(src, nh, col, tabs, i, a, b, last):
                v = ap(src, [(64, nh), (1, 64)])
                link(TT(v, v, ap(stat[:, col:col + nh], [(1, nh), (0, 64)]), ALU.mult))
                TT(ap(a, [(64, nh), (1, 64)]), v, ap(tabs[:, 0, :], [(0, nh), (1, 64)], 64 * i), ALU.mult)\
                    .then_inc(S("B_rope_t"), 1)
                for hf in range(2):
                    TT(ap(b, [(64, nh), (32, 2), (1, 16)], 16 * hf), ap(src, [(64, nh), (32, 2), (1, 16)], 16 * (1 - hf)),
                       ap(tabs[:, 1, :], [(0, nh), (32, 2), (1, 16)], 64 * i + 16 * hf), ALU.mult)\
                        .then_inc(S("B_rope_t"), 1)
                rope_n[0] += 3
                dve.wait_ge(S("B_rope_t"), rope_n[0])
                if last:
                    TT(src, a[:, 0:64 * nh], b[:, 0:64 * nh], ALU.add).then_inc(S("B_rope"), 1)
                else:
                    TT(ap(kD[:, i, :], [(128, nh), (64, 2), (1, 64)]), ap(a, [(64, nh), (0, 2), (1, 64)]),
                       ap(b, [(64, nh), (0, 2), (1, 64)]), ALU.add).then_inc(S("B_rope_k"), 1)

            def gates_B(k):
                key = ("B", 6 + k // 2, k % 2)
                b = take(dve, key)
                dve.wait_ge(S("B_tanh"), k + 1)
                give(STT(G[:, k, :], th[:, k % 2, :], 1.0, b[:, :], ALU.add, ALU.mult), key)

            rope_n = [0]
            for i in range(NT):
                rope(kB[:, i, :], 4, 240 + 20 * i + 16, tabk, i, tkB[:, 0:256], tkB[:, 256:512], False)
                rope(qB[:, i, :], 16, 240 + 20 * i, tabq, i, t1B, t2B, True)
                dve.wait_ge(S("B_rope"), i + 1)
                gates_B(2 * i)
                gates_B(2 * i + 1)

            NB_ = 16 * NT

            def outB(h):
                e = 64 * (h % 2)
                key = ("BO_", h)
                b = take(dve, key)
                give(STT(hT[e:e + 64, h // 2, :], b[e:e + 64, :], 0.5, G[e:e + 64, h // 2, :], ALU.mult, ALU.mult), key)

            for u in range(NB_ + 1):
                if u < NB_:
                    b = take(dve, ("BS", u))
                    if u >= 4:
                        evacuated(dve, ("BS", u - 4))
                    nc.vector.tensor_reduce(stat[:, 128 + u % 4:129 + u % 4], b[:, :], X, ALU.max, negate=True)\
                        .then_inc(S("B_max"), 1)
                if u >= 1:
                    v = u - 1
                    evacuated(dve, ("BS", v))
                    c = 136 + v % 4
                    link(nc.vector.reciprocal(stat[:, c:c + 1], stat[:, c - 4:c - 3]))
                    TS(pB[:, v % 3, :], pB[:, v % 3, :], stat[:, c:c + 1], None, ALU.mult).then_inc(S("B_probs"), 1)
                if u >= 8 and u % 4 == 0:
                    outB(u // 4 - 2)
            outB(15)

            def final_norm(last):
                for i in range(NT):
                    last(i)
                    if i >= 1:
                        final_tile(i - 1)
                final_tile(NT - 1)

            def final_tile(i):
                y = rstd_tile("fin", 16, i)
                if i == 0:
                    dve.wait_ge(s_gb[0], 16)
                STT(x[:, i, :], x[:, i, :], y, gb[:, :], ALU.mult, ALU.mult).then_inc(S("x_fin"), 1)

            ple(1, "BO", 12, final_norm)
            dve.wait_ge(S("x_fin"), NT)
            norm("norm2", 20, natural=True)
            nc.vector.memset(fl[:, :, :], 0.0).then_inc(S("C_flz"), 1)
            dve.wait_ge(S("C_flz"), 1)
            for n in range(2):
                key = ("kvc", n)
                b = take(dve, key)
                m = 0
                for g in range(2):
                    for par in range(2):
                        for hi in range(2):
                            src = ap(b[64 * g:64 * g + 64, :], [(2, 8), (16, 31)], 16 * hi + par)
                            dst = ap(fl[64 * par:64 * par + 64, n, :], [(64, 8), (1, 31)], 8 * hi * 64 + 32 * g)
                            ins = nc.vector.tensor_copy(dst, src)
                            m += 1
                            if m < 8:
                                ins.then_inc(S("C_flcopy"), 1)
                give(ins, key)
                dve.wait_ge(S("C_flcopy"), 7 * (n + 1))
                evacuated(dve, key)
                pos = vcol("posk" if n == 0 else "posv", 0, 16)
                f = ap(fl[:, n, :], [(64, 16), (1, 64)])
                TT(f, f, ap(pos, [(1, 16), (0, 64)]), ALU.add).then_inc(S("C_flat"), 1)

            def gatesC(keys, name, dst):
                for k, key in enumerate(keys):
                    b = take(dve, key)
                    dve.wait_ge(S(name), k + 1)
                    give(STT(dst[:, k, :], thC[:, k % 2, :], 1.0, b[:, :], ALU.add, ALU.mult), key)

            gatesC([("C", 3, s) for s in range(4)], "C_tanh", Gn)
            dve.wait_ge(S("C_gates"), NT)
            link(TS(gt[:, :, :], gt[:, :, :], 0.5, 0.5, ALU.mult, ALU.add))
            evacuated(dve, ("C", 2, NT - 1))
            evacuated(dve, ("C", 0, NT - 1))
            for n, (src, dst) in enumerate(((q2, q2r), (kd, kd))):
                src, dst = src[:, 0], dst[:, 0]

                def part(v, o):
                    return ap(v, [(512, NT), (64, 8), (1, 8)], o)

                def tabs(name):
                    return ap(C(name), [(8, NT), (0, 8), (1, 8)])

                r4 = [ap(rt[:, k, :], [(64, NT), (8, 8), (1, 8)]) for k in range(4)]
                TT(r4[0], part(src, 0), tabs("cos2"), ALU.mult).then_inc(S("C_rt"), 1)
                TT(r4[1], part(src, 8), tabs("sin2"), ALU.mult).then_inc(S("C_rt"), 1)
                TT(r4[2], part(src, 8), tabs("cos2"), ALU.mult).then_inc(S("C_rt"), 1)
                TT(r4[3], part(src, 0), tabs("sin2"), ALU.mult).then_inc(S("C_rt"), 1)
                dve.wait_ge(S("C_rt"), 4 * n + 4)
                TT(part(dst, 0), r4[0], r4[1], ALU.subtract).then_inc(S("C_rope"), 1)
                TT(part(dst, 8), r4[2], r4[3], ALU.add).then_inc(S("C_rope"), 1)
                dve.wait_ge(S("C_rope"), 2 * n + 2)
            for n in range(2):
                key = ("hid", n)
                b = take(dve, key)
                dve.wait_ge(S("C_thh"), n + 1)
                give(STT(hid[:, n, :], thh, 1.0, b[:, 0:128], ALU.add, ALU.mult), key)
            dve.wait_ge(S("C_clear"), 3)
            b = take(dve, "kcmp")
            for e in range(2):
                ins = TS(kcz[64 * e:64 * e + 64, :, e, :], b[0:64, 0:64].rearrange("p (g c) -> p g c", g=2), 0.5, None,
                         ALU.mult)
                if e == 0:
                    ins.then_inc(S("C_cmp"), 1)
            give(ins, "kcmp")
            evacuated(dve, "kcmp")
            b = take(dve, "vcmp")
            for g in range(2):
                for r in range(4):
                    ins = TS(vcz[32 * r:32 * r + 32, g, r, :], b[0:32, g * 64:g * 64 + 64], 0.5, None, ALU.mult)
                    if (g, r) != (1, 3):
                        ins.then_inc(S("C_cmp"), 1)
            give(ins, "vcmp")
            evacuated(dve, "vcmp")
            dve.sem_inc(S("C_cmp"), 4)

            def heads8(i):
                return smC[:, i % 2, :].rearrange("p (h c) -> p h c", h=8)

            for i in range(NT):
                if i >= 2:
                    dve.wait_ge(filled, J[("ct", i - 2)] + 1)
                s = heads8(i)
                key = ("cs", i)
                b = take(dve, key)
                give(TT(s, b[:, 0:256].rearrange("p (h c) -> p h c", h=8),
                        ap(C("cmpneg"), [(0, 8), (1, 32)], 32 * i), ALU.add), key)
                evacuated(dve, key)
                mx, sm, sc = stat[:, 416:424], stat[:, 424:432], stat[:, 432:440]
                link(nc.vector.tensor_reduce(mx, s, X, ALU.max))
                TT(s, s, ap(mx, [(1, 8), (0, 32)]), ALU.subtract).then_inc(S("C_cs"), 1)
                dve.wait_ge(S("C_ce"), i + 1)
                link(nc.vector.tensor_reduce(sm, s, X, ALU.add))
                link(nc.vector.reciprocal(sm, sm))
                link(TT(sc, sm, ap(gt[:, i, :], [(3, 8)]), ALU.mult))
                link(TT(s, s, ap(C("cmpok"), [(0, 8), (1, 32)], 32 * i), ALU.mult))
                TT(s, s, ap(sc, [(1, 8), (0, 32)]), ALU.mult).then_inc(S("C_pc"), 1)

            def outN(h):
                e, j = 64 * (h % 2), h // 2
                key = ("NO", h)
                b = take(dve, key)
                give(STT(ap(mixA[e:e + 64, j, :], [(1, GR), (GR, GW)]), b[e:e + 64, :].rearrange("p (r c) -> p r c", r=GR),
                         0.5, Gn[e:e + 64, j, :].rearrange("p (r c) -> p r c", r=GR), ALU.mult, ALU.mult), key)

            for u in range(len(UN) + 4):
                if u < len(UN):
                    nk = (UN[u][2] + 1) * P
                    b = take(dve, ("NS", u))
                    if u >= 4:
                        evacuated(dve, ("NS", u - 4))
                    nc.vector.tensor_reduce(stat[:, 400 + u % 4:401 + u % 4], b[:, 0:nk], X, ALU.max, negate=True)\
                        .then_inc(S("N_max"), 1)
                if 1 <= u < len(UN) + 1:
                    v = u - 1
                    h, br, i = UN[v]
                    nk = (i + 1) * P
                    evacuated(dve, ("NS", v))
                    c = 408 + v % 4
                    link(nc.vector.reciprocal(stat[:, c:c + 1], stat[:, c - 4:c - 3]))
                    TS(pN[:, v % 3, 0:nk], pN[:, v % 3, 0:nk], stat[:, c:c + 1], gt[:, i, 3 * h + 1 + br:3 * h + 2 + br],
                       ALU.mult, ALU.mult).then_inc(S("N_probs"), 1)
                if u >= 12 and (u - 12) % 8 == 0:
                    outN((u - 12) // 8)
            outN(7)

            nc.vector.memset(ap(raw[:, 0, :], [(513, 3)]), 0.0).then_inc(S("R_rawzero"), 1)
            dsts = [rF[:, j, :] for j in range(4)] + [kF[:, j, :] for j in range(4)] + [vF[:, j, :] for j in range(4)] + [wdad]
            for s in range(13):
                dve.wait_ge(S("R_dif"), s + 1)
                STT(dsts[s], dif[:, s % 2, :], vcol("mu", s), raw[:, s % 3, 1:513], ALU.mult, ALU.add).then_inc(S("R_mix"), 1)
            TS(stat[:, 576:584], vec[:, V0["w0"]:V0["w0"] + 8], 0.5, None, ALU.mult).then_inc(S("R_half"), 1)
            gatesC([("C", 8, s) for s in range(4)], "R_tanh", Gr)
            dve.wait_ge(S("R_mix"), 13)
            for j in range(4):
                TS(kk[:, j, :], kF[:, j, :], vcol("kk", j), None, ALU.mult).then_inc(S("R_kkraw"), 1)
            for j in range(4):
                evacuated(dve, ("W", j))
                link(TS(lw[:, j, :], lw[:, j, :], -LOGC / 2, -LOGC / 2, ALU.mult, ALU.add))
                link(nc.vector.tensor_tensor_scan(cum[:, j, :], C("chunk"), lw[:, j, :], 0.0, ALU.mult, ALU.add))
                TT(lw[:, j, :], cum[:, j, :], lw[:, j, :], ALU.subtract).then_inc(S("R_cum"), 1)
            for j in range(4):
                evacuated(dve, ("A_", j))
                link(TS(aF[:, j, :], aF[:, j, :], 0.5, 0.5, ALU.mult, ALU.add))
                link(TS(dif[:, 0, :], aF[:, j, :], -1.0, vcol("ka", j), ALU.add, ALU.mult))
                link(STT(kF[:, j, :], dif[:, 0, :], 1.0, kF[:, j, :], ALU.add, ALU.mult))
            b = take(dve, "ks")
            give(TS(stat[:, 448:480], b[:, 0:32], 1e-24, None, ALU.max), "ks")
            evacuated(dve, "ks")
            rsqrt(stat[:, 480:512], stat[:, 448:480], stat[:, 512:544])
            bx3 = bx.rearrange("p (s d) -> p s d", d=64)
            nc.vector.tensor_copy(bx3, ap(stat[:, 480:512], [(1, 32), (0, 64)])).then_inc(S("R_kx"), 1)
            for j in range(4):
                key = ("kb", j)
                b = take(dve, key)
                give(TT(kk[:, j, :], kk[:, j, :], b[:, :], ALU.mult), key)
            evacuated(dve, ("kb", 3))
            dve.wait_ge(S("R_P"), 12)
            for j in range(4):
                def tiles(v):
                    return v.rearrange("p (i t) -> p i t", i=NT)

                STT(AR[:, j, :, 0, :], tiles(kk[:, j, :]), -1.0, tiles(lw[:, j, :]), ALU.mult, ALU.mult).then_inc(S("R_ar"), 1)
                link(TT(aF[:, j, :], aF[:, j, :], kk[:, j, :], ALU.mult))
                link(TT(aF[:, j, :], aF[:, j, :], iP[:, j, :], ALU.mult))
                TT(AR[:, j, :, 1, :], tiles(rF[:, j, :]), tiles(cum[:, j, :]), ALU.mult).then_inc(S("R_ar"), 1)
                STT(sq[:, j, :], rF[:, j, :], vcol("rk", j), kF[:, j, :], ALU.mult, ALU.mult).then_inc(S("R_rk"), 1)
                nc.vector.tensor_copy(PC[:, j, :], ap(cum[:, j, :], [(CH, 8)], CH - 1)).then_inc(S("R_ar"), 1)
                TT(iP[:, j, :], kF[:, j, :], iP[:, j, :], ALU.mult).then_inc(S("R_kap"), 1)
                dve.wait_ge(S("R_kap"), j + 1)
                dve.wait_ge(S("R_ar"), 3 * j + 3)
                dve.sem_inc(S("R_ops"), 1)
            b = take(dve, "bs")
            give(nc.vector.tensor_copy(bx3, ap(b[:, 0:32], [(1, 32), (0, 64)])), "bs")
            evacuated(dve, "bs")
            dve.sem_inc(S("R_bx"), 1)
            for j in range(4):
                key = ("bb", j)
                b = take(dve, key)
                give(TT(rF[:, j, :], vF[:, j, :], b[:, :], ALU.mult), key)
            nc.vector.memset(Sst[:, 0, :], 0.0).then_inc(S("R_state"), 1)

            def plus(key, dst, src):
                for bt in range(2):
                    b = take(dve, key + (bt,))
                    hs = slice(4 * bt, 4 * bt + 4)
                    give(TT(dst[:, hs, :], b[:, :].rearrange("p (h t) -> p h t", h=4), src[:, hs, :], ALU.add), key + (bt,))
                evacuated(dve, key + (1,))

            def moves(key, dst):
                for bt in range(2):
                    b = take(dve, key + (bt,))
                    give(nc.vector.tensor_copy(dst[:, 4 * bt:4 * bt + 4, :], b[:, :].rearrange("p (h t) -> p h t", h=4)),
                         key + (bt,))

            for i in range(NT):
                for h in range(8):
                    key = ("gr", i, h)
                    b = take(dve, key)
                    TT(AE[:, h, :, :], ap(b[:, 0:P], [(0, 2), (1, P)]), ap(C("a16"), [(P, 2), (1, P)]), ALU.mult)\
                        .then_inc(S("R_gram"), 1)
                    give(TT(B3[:, h, :, :].rearrange("p m t -> p (m t)"), b[:, P:512], C("gram"), ALU.mult), key)
                dve.wait_ge(S("R_gram"), 8 * i + 8)
                TT(Qa[:, :, :], AE[:, :, 0, :], ap(ident, [(0, 8), (1, P)]), ALU.add).then_inc(S("R_q1"), 1)
                moves(("D2", i), D2)
                dve.wait_ge(S("R_q1"), i + 1)
                plus(("Q2", i), Qb, Qa)
                plus(("Q3", i), Qa, Qb)
                plus(("Q4", i), Qb, Qa)
                moves(("K", i), AE[:, :, 0, :])
                plus(("Q5", i), Qa, Qb)
                plus(("RR", i), Qb, Qa)
                key = ("rho", i)
                b = take(dve, key)
                give(TT(RHO.rearrange("p (j t) -> p j t", j=4), b[:, :].rearrange("p (j t) -> p j t", j=4),
                        AR[:, :, i, 1, :], ALU.add), key)
                for c in range(2):
                    key = ("M", i, c)
                    b = take(dve, key)
                    give(TT(MT[:, c, :, :], b[:, 0:256].rearrange("p (j k) -> p j k", j=4),
                            ap(C("ident64"), [(0, 4), (1, 64)]), ALU.add), key)
                for c in range(2):
                    k = 2 * i + c
                    key = ("St", k)
                    b = take(dve, key)
                    evacuated(dve, ("Bm", i, c))
                    nx = Sst[:, (k + 1) % 4, :]
                    give(TT(nx, b[:, 0:256], Bm[:, c, :], ALU.add), key)
                    evacuated(dve, key)
                    nv = nx.rearrange("p (j v) -> p j v", j=4)
                    TT(nv, nv, ap(PC[:, :, k], [(8, 4), (0, 64)]), ALU.mult).then_inc(S("R_state"), 1)
                    dve.wait_ge(S("R_state"), k + 2)
                key = ("Y2", i)
                b = take(dve, key)
                evacuated(dve, ("Y1", i))
                yi = yF[:, :, i * P:(i + 1) * P]
                give(TT(yi, yi, b[:, :].rearrange("p (j t) -> p j t", j=4), ALU.add), key)

            b = take(dve, "gn1")
            give(TS(bx3, ap(b[:, 0:32], [(1, 32), (0, 64)]), 1.0 / HD, None, ALU.mult), "gn1")
            evacuated(dve, "gn1")
            dve.sem_inc(S("R_gx"), 1)
            for j in range(4):
                key = ("gb1", j)
                b = take(dve, key)
                give(TT(yF[:, j, :], yF[:, j, :], b[:, :], ALU.subtract), key)
                evacuated(dve, key)
                if j == 3:
                    dve.sem_inc(S("R_centred"), 4)
            b = take(dve, "gn2")
            give(TS(stat[:, 448:480], b[:, 0:32], 1.0 / HD, GN_EPS, ALU.mult, ALU.add), "gn2")
            evacuated(dve, "gn2")
            rsqrt(stat[:, 480:512], stat[:, 448:480], stat[:, 512:544])
            nc.vector.tensor_copy(bx3, ap(stat[:, 480:512], [(1, 32), (0, 64)])).then_inc(S("R_gx"), 1)
            for j in range(4):
                key = ("gb2", j)
                b = take(dve, key)
                y = yF[:, j, :]
                give(TT(y, y, b[:, :], ALU.mult), key)
                evacuated(dve, key)
                link(TS(y, y, vcol("gnw", j), vcol("gnb", j), ALU.mult, ALU.add))
                link(TT(y, y, rF[:, j, :], ALU.add))
                STT(ap(mixB[:, j, :], [(1, GR), (GR, GW)]), y.rearrange("p (r c) -> p r c", r=GR), 0.5,
                    Gr[:, j, :].rearrange("p (r c) -> p r c", r=GR), ALU.mult, ALU.mult).then_inc(S("R_done"), 1)
            for n in range(2):
                for i in range(NT):
                    add_proj("CO", n, i, 512)

            y = rstd("out", 24)
            dve.wait_ge(s_gb[1], 16)
            for i in range(NT):
                STT(xo[:, i, :], x[:, i, :], y[:, i:i + 1], gb2[:, :], ALU.mult, ALU.mult).then_inc(S("out_ready"), 1)

        @block.gpsimd
        def _(pool):
            pool.dma_start(cst[:, :], A["cst"]).then_inc(s_cst, 16)
            pool.dma_start(rpb_in[0:16, 0:465], A["a_rpb"][0].rearrange("h a b -> h (a b)")).then_inc(s_rpb, 16)
            pool.wait_ge(S("vrow_zero"), 1)
            c = 0
            for src, n in rows:
                pool.dma_start(vrow[c:c + n, :], src).then_inc(s_vrow, 16)
                c += n
            pool.wait_ge(s_rpbr, 2)
            pool.dma_start(scratch, rrev).then_inc(s_scr, 16)
            pool.wait_ge(s_scr, 16)
            pool.dma_start(w2[:, 0, :, :], A["cmp_w2_k_2"][0].rearrange("(b p) d -> p b d", p=P)).then_inc(s_small, 16)
            pool.dma_start(w2[:, 1, :, :], A["cmp_w2_v_2"][0].rearrange("(b p) d -> p b d", p=P)).then_inc(s_small, 16)
            pool.dma_start(wa[0:64, :], A["decay_up_2"][0]).then_inc(s_small, 16)
            pool.dma_start(wa[64:128, :], A["iclr_up_2"][0]).then_inc(s_small, 16)

            def load_bias(h):
                src = bass.AP(scratch.tensor, h * 1024 + 49, [[1, 16], [64, 8], [1, 512]])
                pool.dma_start(ext[:, h % 2, :], src).then_inc(s_ext[h % 2], 16)

            def lower(n0, n1=None):
                for n in range(n0, (n0 if n1 is None else n1) + 1):
                    if n < len(halves):
                        pool.wait_ge(s_whi, n + 1)
                        r = raw_slot(n)
                        nc.gpsimd.tensor_tensor(rounded(r), r, read_back(high_slot(n)), ALU.subtract).then_inc(s_wlo, 1)

            def low_tiles(tag):
                dst = low[tag].rearrange("p (k t) -> p k t", k=KB)
                for i in range(3):
                    for hf in range(2):
                        pool.wait_ge(S("hi_" + tag), 2 * i + hf + 1)
                        ks, ts = slice(4 * hf, 4 * hf + 4), slice(i * P, (i + 1) * P)
                        nc.gpsimd.tensor_tensor(rounded(dst[:, ks, ts]), dst[:, ks, ts], read_back(hT[:, ks, ts]), ALU.subtract)\
                            .then_inc(S("lo_" + tag), 1)

            def low_pair(l, j):
                pool.wait_ge(S("o_high"), 8 * l + j + 1)
                nc.gpsimd.tensor_tensor(rounded(hT[:, j, :]), hT[:, j, :], read_back(o_high[:, T * j:T * j + T]), ALU.subtract)\
                    .then_inc(S("o_low"), 1)

            def low_embedding(l):
                pool.wait_ge(S("pw_high"), l + 1)
                nc.gpsimd.tensor_tensor(rounded(pw_lo), pw_lo, read_back(pw_hi), ALU.subtract).then_inc(S("pw_low"), 1)

            for i in range(2):
                nc.gpsimd.memset(bias[0:64, i, 256:384], NEG).then_inc(S("bias_edge"), 1)
            load_bias(0)
            load_bias(1)
            lower(0)
            low_tiles("norm0")
            lower(1, HI[("A", 12)])
            pool.wait_ge(s_cst, 16)
            mask = C("nbr")
            for h in range(16):
                if h == 2:
                    lower(HI[("A", 12)] + 1, HI[("AO", 1)])
                pool.wait_ge(s_ext[h % 2], 16 * (h // 2 + 1))
                if h >= 2:
                    evacuated(pool, ("AS", h - 2, 1))
                e_ = ext[:, h % 2, :]
                o = bias[:, h % 2, :]

                def rev(lo, hi, jj):
                    return ap(ext[lo:hi, h % 2, :], [(-1, 32), (-64, 8)], 511 - jj)

                def jk(v, c):
                    return v[:, c:c + 256].rearrange("p (j k) -> p j k", k=8)

                nc.gpsimd.tensor_tensor(jk(o, 0), rev(0, 128, 8), jk(mask, 0), ALU.add).then_inc(s_bias, 1)
                pool.wait_ge(s_bias, 3 * h + 1)
                nc.gpsimd.tensor_tensor(o[0:64, 384:512].rearrange("p (j k) -> p j k", k=8),
                                        ap(ext[0:64, h % 2, :], [(-1, 16), (-64, 8)], 511 - 8),
                                        mask[0:64, 384:512].rearrange("p (j k) -> p j k", k=8), ALU.add).then_inc(s_bias, 1)
                pool.wait_ge(s_bias, 3 * h + 2)
                nc.gpsimd.tensor_tensor(jk(o[64:128], 256), rev(64, 128, 24), jk(mask[64:128], 256), ALU.add)\
                    .then_inc(s_bias, 1)
                pool.wait_ge(s_bias, 3 * h + 3)
                if h + 2 < 16:
                    load_bias(h + 2)
                if h >= 7 and h % 2:
                    low_pair(0, (h - 7) // 2)
            for l in range(2):
                for j in range(5 if l == 0 else 0, 7):
                    low_pair(l, j)
                evacuated(pool, ("AO_" if l == 0 else "BO_", 15))
                src = A["p"][l, 0].rearrange("(r c) d -> c r d", r=GR)
                for i in range(NT):
                    pool.dma_start(p_tm[:, i, :], src[CT * i:CT * i + CT]).then_inc(s_p[l], 16)
                low_pair(l, 7)
                if l == 0:
                    for n, name in enumerate(("b_q_norm", "b_k_norm")):
                        pool.dma_start(gqk[:, 64 * n:64 * n + 64], bass.AP(A[name].tensor, 0, [[0, P], [1, 64]]))\
                            .then_inc(S("gqk_loaded"), 16)
                else:
                    pool.dma_start(gb[:, :], bass.AP(A["final_norm_g"].tensor, 0, [[0, P], [1, D]]))\
                        .then_inc(s_gb[0], 16)
                low_embedding(l)
                a = HI[("AO" if l == 0 else "BO", 2)]
                lower(a, HI[("PG", l, 0)])
                low_tiles(f"ple{l}")
                if l == 0:
                    lower(HI[("PG", 0, 1)], HI[("B", 0)])
                    low_tiles("norm1")
                    lower(HI[("B", 1)], HI[("BO", 1)])
                else:
                    lower(HI[("PG", 1, 1)], HI[("PG", 1, 3)])
            evacuated(pool, ("norm2", NT - 1, 1))
            nc.gpsimd.memset(kcz[:, :, :, :], 0.0).then_inc(S("C_clear"), 1)
            nc.gpsimd.memset(vcz[:, :, :, :], 0.0).then_inc(S("C_clear"), 1)
            nc.gpsimd.memset(kz[:, :, :, :, :], 0.0).then_inc(S("C_clear"), 1)
            for s in range(13):
                evacuated(pool, ("R", s))
                if s >= 2:
                    pool.wait_ge(S("R_mix"), s - 1)
                nc.gpsimd.tensor_tensor(dif[:, s % 2, :], raw[:, s % 3, 0:512], raw[:, s % 3, 1:513], ALU.subtract)\
                    .then_inc(S("R_dif"), 1)
            pool.wait_ge(S("R_done"), 4)
            pool.dma_start(gb2[:, :], bass.AP(A["final_g_2"].tensor, 0, [[0, P], [1, D]])).then_inc(s_gb[1], 16)

        @block.sync
        def _(sp):
            for n, src in enumerate(halves):
                if n >= NRAW:
                    sp.wait_ge(filled, half_last[n - NRAW] + 1)
                sp.dma_start(raw_slot(n).rearrange("p (k m) -> p k m", k=KB), src).then_inc(raw_loaded[n % NRAW], 16)
                for l, tag in enumerate(("AO", "BO")):
                    if n == HI[(tag, 3)]:
                        evacuated(sp, (tag + "_", 15))
                        sp.dma_start(pw_lo.rearrange("p (k m) -> p k m", k=2), cols(A["ple_w_proj"][l], 0, D))\
                            .then_inc(s_pp[l], 16)
            for n, (src, (k, m)) in enumerate(chunks):
                if n < NSLOT:
                    sp.wait_ge(filled, half_last[len(halves) - (3 if n == 0 else 1)] + 1)
                else:
                    sp.wait_ge(filled, chunk_last[n - NSLOT] + 1)
                dst = slot(n)[:, 0:k * m].rearrange("p (k m) -> p k m", k=k)
                sp.dma_start(dst, src).then_inc(weights[n % NSLOT], 16)
            o = out[0].rearrange("(r c) d -> c r d", r=GR)
            for i in range(NT):
                sp.wait_ge(S("out_ready"), i + 1)
                sp.dma_start(o[CT * i:CT * i + CT], xo[:, i, :]).then_inc(s_out, 16)
            sp.wait_ge(s_out, 16 * NT)


NAMES = ("x p norm_g a_w_in a_rpb a_w_out b_w_in b_q_norm b_k_norm b_w_out ple_norm_g ple_w_gate ple_w_proj "
         "final_norm_g norm_g_2 w_in_2 cmp_pos_k_2 cmp_w1_k_2 cmp_w2_k_2 cmp_pos_v_2 cmp_w1_v_2 cmp_w2_v_2 "
         "shift_mu_2 decay_w0_2 decay_up_2 iclr_a0_2 iclr_up_2 k_k_2 k_a_2 r_k_2 gn_w_2 gn_b_2 w_out_2 "
         "final_g_2").split()


def kernel(**inputs):
    import numpy as _np
    import concourse.bacc as _bacc
    from concourse import mybir as _mybir
    from concourse.bass_utils import run_bass_kernel_spmd as _run

    nc = _bacc.Bacc("TRN2", target_bir_lowering=False, num_devices=1)
    arrays, aps = {}, {}
    for name in NAMES:
        a = _np.ascontiguousarray(inputs[name])
        arrays[f"in_{name}"] = a
        aps[name] = nc.dram_tensor(f"in_{name}", a.shape, _mybir.dt.from_np(a.dtype), kind="ExternalInput").ap()
    arrays["in_cst"] = CST
    aps["cst"] = nc.dram_tensor("in_cst", CST.shape, _mybir.dt.float32, kind="ExternalInput").ap()
    out = nc.dram_tensor("out_0", (1, T, D), _mybir.dt.float32, kind="ExternalOutput").ap()
    program(nc, aps, out)
    r = _run(nc, [arrays], core_ids=[0])
    return r.results[0]["out_0"]
```

```python
import math
from contextlib import ExitStack

import numpy as np

import concourse.bass as bass
from concourse import mybir

F32 = mybir.dt.float32
F32R = mybir.dt.float32r
BF16 = mybir.dt.bfloat16
I32 = mybir.dt.int32
ALU = mybir.AluOpType
ACT = mybir.ActivationFunctionType
X = mybir.AxisListType.X

P = 128
D = 1024
T = 512
NT = T // P
KB = D // P
HD = 64
GW, GR = 64, 8
CT = GW // NT
NEG = -1e30
EPS = 1e-6
GN_EPS = 64e-5
NBANK = 8
HALF = 2048
NRAW, NHI = 4, 2
CH = 64
LOGC = math.exp(-0.5)
RSQRT_MAGIC = float(0x5F3759DF)


def constants():
    parts, at, n = [], {}, 0

    def add(name, a):
        nonlocal n
        a = np.asarray(a, np.float64).reshape(P, -1).astype(np.float32)
        at[name] = (n, a.shape[1])
        n += a.shape[1]
        parts.append(a)

    p = np.arange(P)
    cq, r = p // GR, p % GR
    add("ident", np.eye(P))
    j = np.repeat(np.arange(32), GR)
    mid = (j[None] >= cq[:, None]) & (j[None] <= cq[:, None] + 15)
    edge = np.where(cq[:, None] < 8, j[None] >= 16, j[None] < 16)
    add("nbr", np.concatenate([np.where(mid, 0, NEG), np.where(edge, 0, NEG)], 1))
    inv = 10000.0 ** (-np.arange(16) * 2.0 / 32)
    cos, sin = np.zeros((P, NT, 2, 2, 16)), np.zeros((P, NT, 2, 2, 16))
    for i in range(NT):
        for s, pos in ((0, r), (1, CT * i + cq)):
            ang = pos[:, None] * inv[None]
            for hf in range(2):
                cos[:, i, s, hf] = np.cos(ang)
                sin[:, i, s, hf] = np.sin(ang) * (-1 if hf == 0 else 1)
    add("ropeb", np.concatenate([cos.reshape(P, NT * HD), sin.reshape(P, NT * HD)], 1))
    inv2 = 500000.0 ** (-np.arange(8) / 8.0)
    pos = (np.arange(NT)[None] * P + p[:, None])[..., None] * inv2
    add("cos2", np.cos(pos))
    add("sin2", np.sin(pos))
    c = np.arange(32)
    ok = (c[None, None] * 16 + 31 <= (np.arange(NT)[None] * P + p[:, None])[..., None]) & (c < 31)
    add("cmpneg", np.where(ok, 0, NEG))
    add("cmpok", ok)
    add("causal", np.where(p[None] > p[:, None], NEG, 0))
    s, t = p[:, None], p[None]
    same, same16 = s // CH == t // CH, s // 16 == t // 16
    add("a16", (s < t) & same16)
    add("e16", (s < t) & same & ~same16)
    add("gram", np.concatenate([(s <= t) & same, (s < t) & same, (s <= t) & same], 1))
    add("chunk", np.tile((np.arange(T) % CH != 0), (P, 1)))
    add("heads", np.stack([p < HD, p >= HD], 1))
    add("headmean", (s // HD == t // HD) / HD)
    add("ident64", np.tile(np.eye(HD), (2, 1)))
    return np.concatenate(parts, 1), at


CST, CAT = constants()


def program(nc, A, out):
    ctx = ExitStack()
    with ctx:
        def sb(name, shape, dt=F32):
            return ctx.enter_context(nc.sbuf_tensor(name, shape, dt))

        second = {}

        def sb2(name, shape, *spans):
            at = -(-nc.sbuf_base // 32) * 32
            plain = sb(name, shape)
            second[name] = [(o, n, nc.alloc_sbuf_tensor_at(f"{name}_parts{o}", [P, n], F32R, offset=at + 4 * o))
                            for o, n in spans]
            return plain

        def sem(name):
            return ctx.enter_context(nc.semaphore(name))

        x = sb2("x", [P, NT, D], (0, NT * D))
        hT = sb2("hT", [P, KB, T], (0, KB * T))
        ring = sb2("ring", [P, (NRAW + NHI) * HALF], (0, (NRAW + NHI) * HALF))
        cst = sb("cst", [P, CST.shape[1]])
        vrow = sb("vrow", [P, P])
        vec = sb("vec", [P, P])
        stat = sb("stat", [P, 640])
        identb = sb("identb", [P, P], BF16)
        causalb = sb("causalb", [P, P], BF16)
        w2 = sb("w2", [P, 2, 2, HD])
        wa = sb("wa", [P, 512])
        NARENA = 27968
        arena = sb2("arena", [P, NARENA], (0, 12288), (19456, 6144))
        bank = [ctx.enter_context(nc.psum_tensor(f"bank{b}", [P, 512], F32)) for b in range(NBANK)]
        x_kept = nc.dram_tensor("x_kept", [NT, P, D], F32, kind="Internal").ap()
        scratch = nc.dram_tensor("rpb_rows", [16, 1024], F32, kind="Internal").ap()

        def C(name):
            o, n = CAT[name]
            return cst[:, o:o + n]

        def ap(base, dims, off=0):
            return bass.AP(base.tensor, base.offset + off, [list(base.ap[0])] + [list(d) for d in dims])

        def area(o, n):
            assert o + n <= NARENA
            return arena[:, o:o + n]

        ident = C("ident")

        def tile_of(base, tag, i, hf):
            if tag == "norm2":
                return ap(base, [(T, 4), (1, CT), (GW, GR)], 4 * hf * T + CT * i)
            return ap(base, [(T, 4), (1, P)], 4 * hf * T + P * i)

        rows, V0 = [], {}
        for name, src in (("norm0", A["norm_g"][0:1]), ("norm1", A["norm_g"][1:2]),
                          ("ple0", A["ple_norm_g"][0:1]), ("ple1", A["ple_norm_g"][1:2]),
                          ("norm2", A["norm_g_2"]), ("mu", A["shift_mu_2"]), ("w0", A["decay_w0_2"]),
                          ("a0", A["iclr_a0_2"]), ("kk", A["k_k_2"]), ("ka", A["k_a_2"]), ("rk", A["r_k_2"]),
                          ("gnw", A["gn_w_2"]), ("gnb", A["gn_b_2"]),
                          ("posk", A["cmp_pos_k_2"].rearrange("a b c -> a (b c)")),
                          ("posv", A["cmp_pos_v_2"].rearrange("a b c -> a (b c)"))):
            n = src.shape[1] // P
            V0[name] = sum(m for _, m in rows)
            rows.append((src.rearrange("a (j p) -> (a j) p", p=P), n))
        NV = sum(m for _, m in rows)
        assert NV <= P

        def vcol(name, j=0, n=1):
            return vec[:, V0[name] + j:V0[name] + j + n]

        halves, HI, splits = [], {}, []

        def cols(w, a, b):
            return w.rearrange("(k p) n -> p k n", p=P)[:, :, a:b]

        def load(name, src, shape, split=True):
            HI[name] = len(halves)
            if split:
                splits.append(len(halves))
            halves.append((src, shape))

        def half(name, w, n):
            load(name, cols(w, 256 * n, 256 * n + 256), (KB, 256))

        AORD = list(range(8, 12)) + list(range(8)) + list(range(12, 16))
        for n in AORD:
            half(("A", n), A["a_w_in"][0], n)
        for n in range(4):
            half(("AO", n), A["a_w_out"][0], n)
        for n in range(4):
            half(("PG", 0, n), A["ple_w_gate"][0], n)
        for n in range(10):
            half(("B", n), A["b_w_in"][0], n)
        for n in range(4):
            half(("BO", n), A["b_w_out"][0], n)
        for n in range(4):
            half(("PG", 1, n), A["ple_w_gate"][1], n)

        w_in2 = A["w_in_2"][0]
        for name, a, b in (("Ckv", 512, 768), ("Csel", 768, 1024), (("Cq", 0), 0, 256), (("Cq", 1), 256, 512),
                           ("Cwin", 1024, 1280), ("Cbg", 1280, 1408)):
            load(name, cols(w_in2, a, b), (KB, b - a))
        for name, w in (("W1K", A["cmp_w1_k_2"][0]), ("W1V", A["cmp_w1_v_2"][0])):
            for n in range(2):
                load((name, n), w[1024 * n:1024 * n + 1024].rearrange("(k p) n -> p k n", p=P), (8, 256), False)
        for n in range(2):
            load(("Cog", n), cols(w_in2, 1304 + 256 * n, 1560 + 256 * n), (KB, 256))
        load(("R", 6), cols(w_in2, 3352, 3480), (KB, P))
        for n in (2, 3, 0, 1, 4, 5):
            load(("R", n), cols(w_in2, 1816 + 256 * n, 2072 + 256 * n), (KB, 256))
        for n in range(2):
            load(("Rg", n), cols(w_in2, 3480 + 256 * n, 3736 + 256 * n), (KB, 256))
        for part in range(2):
            for n in range(2):
                w = A["w_out_2"][0][512 * part:512 * part + 512, 512 * n:512 * n + 512]
                load(("CO", part, n), w.rearrange("(k p) n -> p k n", p=P), (4, 512), False)

        def raw_slot(n):
            return ring[:, HALF * (n % NRAW):HALF * (n % NRAW) + HALF]

        def high_slot(n):
            o = HALF * (NRAW + splits.index(n) % NHI)
            return ring[:, o:o + HALF]

        def W(name):
            n = HI[name]
            k, m = halves[n][1]
            return raw_slot(n)[:, 0:k * m].rearrange("p (k m) -> p k m", k=k)

        def rounded(v):
            last = v.offset + sum(step * (count - 1) for step, count in list(v.ap)[1:])
            for o, n, t in second[v.tensor.name]:
                if o <= v.offset and last < o + n:
                    return bass.AP(t, v.offset - o, [[n, P]] + [list(d) for d in list(v.ap)[1:]])
            raise ValueError("no rounded parts here")

        def read_back(v):
            return rounded(v).bitcast(F32)

        def parts(high, low, k):
            return tuple(rounded(v.rearrange("p (k m) -> p k m", k=k)) for v in (high, low))

        def W3(name):
            n = HI[name]
            k, m = halves[n][1]
            return parts(high_slot(n)[:, 0:k * m], raw_slot(n)[:, 0:k * m], k)

        filled = sem("filled")
        drained = {"a": sem("drained_by_scalar"), "v": sem("drained_by_vector")}
        raw_loaded = [sem(f"raw_loaded{i}") for i in range(NRAW)]
        s_whi = sem("weight_high_parts")
        s_wlo = sem("weight_low_parts")
        s_pp = [sem(f"embedding_weights_loaded{l}") for l in range(2)]
        s_kept = [sem(f"x_written_out{i}") for i in range(2)]
        s_x = [sem(f"x_loaded{i}") for i in range(NT)]
        s_ident = sem("identity_loaded")
        s_cst = sem("constants_loaded")
        s_vrow = sem("vectors_loaded")
        s_small = sem("small_weights_loaded")
        s_p = [sem(f"p_loaded{l}") for l in range(2)]
        s_gb = [sem(f"gain_rows_loaded{l}") for l in range(3)]
        s_rpb = sem("rpb_loaded")
        s_rpbr = sem("rpb_reversed")
        s_scr = sem("rpb_scratch_written")
        s_ext = [sem(f"bias_rows_loaded{i}") for i in range(2)]
        s_bias = sem("bias_ready")
        s_v = sem("vector_chain")
        s_out = sem("out_written")
        made = {}

        def S(name):
            if name not in made:
                made[name] = sem(name)
            return made[name]

        order, J, who, nth, count = [], {}, {}, {}, {"a": 0, "v": 0}

        def take(eng, key):
            eng.wait_ge(filled, J[key] + 1)
            return bank[J[key] % NBANK]

        given = {"a": 0, "v": 0}

        def give(ins, key):
            given[who[key]] += 1
            assert nth[key] == given[who[key]], (key, nth[key], given)
            ins.then_inc(drained[who[key]], 1)

        def evacuated(eng, key):
            eng.wait_ge(drained[who[key]], nth[key])

        qT = area(0, 4096).rearrange("p (j t) -> p j t", j=8)
        kT = area(4096, 4096).rearrange("p (j t) -> p j t", j=8)
        va = area(8192, 4096).rearrange("p (i n) -> p i n", i=NT)
        G = area(12288, 4096).rearrange("p (j t) -> p j t", j=8)
        xn = area(16384, 2048).rearrange("p (b d) -> p b d", b=2)
        th = area(18432, 1024).rearrange("p (b d) -> p b d", b=2)
        ext = area(19456, 1024).rearrange("p (b d) -> p b d", b=2)
        bias = area(20480, 1024).rearrange("p (b d) -> p b d", b=2)
        sA = area(21504, 2048).rearrange("p (b d) -> p b d", b=2)
        pA = area(23552, 3072).rearrange("p (b d) -> p b d", b=3)
        ptA = area(16384, 3072).rearrange("p (b h d) -> p b h d", b=3, h=2)
        rpb_in = area(27136, 480)
        rrev = area(19456, 1024)[0:16, :]
        junk = area(26112, 1024)
        hTf = hT[:, :, :].rearrange("p k t -> p (k t)")
        low = {"norm0": area(21504, 4096), "ple0": area(4096, 4096), "norm1": area(0, 4096), "ple1": area(4096, 4096),
               "norm2": x[:, :, :].rearrange("p i d -> p (i d)")}
        o_high = area(0, 4096)
        p_tm = area(20480, 1024).rearrange("p (i n) -> p i n", i=NT)
        p_T = area(21504, 1024).rearrange("p (k t) -> p k t", k=2)
        p_lo = area(19456, 1024).rearrange("p (k t) -> p k t", k=2)
        thp = area(22528, 1024).rearrange("p (b d) -> p b d", b=4)
        tp = area(24576, 512).rearrange("p (b d) -> p b d", b=2)
        pw_lo, pw_hi = area(8192, 2048), area(10240, 2048)
        kTB = area(4096, 2048).rearrange("p (g t) -> p g t", g=4)
        vB = area(6144, 1024).rearrange("p (i n) -> p i n", i=NT)
        tabq = area(7168, 512).rearrange("p (s n) -> p s n", s=2)
        tabk = area(7680, 512).rearrange("p (s n) -> p s n", s=2)
        gqk = area(27616, 128)
        kB = area(8320, 1024).rearrange("p (i n) -> p i n", i=NT)
        qB = area(19456, 4096).rearrange("p (i n) -> p i n", i=NT)
        t1B = area(23552, 1024)
        t2B = area(24576, 1024)
        sqB = area(25600, 512).rearrange("p (b d) -> p b d", b=2)
        tkB = area(9344, 512)
        kD = area(9856, 2048).rearrange("p (i n) -> p i n", i=NT)
        ptB = area(19456, 4096).rearrange("p (b k t) -> p b k t", b=2, k=4)
        pB = area(23552, 2048).rearrange("p (b d) -> p b d", b=4)
        gb = area(12288, 1024)
        xo = area(0, 4096).rearrange("p (i d) -> p i d", i=NT)
        gb2 = area(4096, 1024)
        xn4 = area(16384, 4096).rearrange("p (i d) -> p i d", i=NT)
        q2 = area(0, 2048).rearrange("p (i n) -> p i n", i=NT)
        q2r = area(2048, 2048).rearrange("p (i n) -> p i n", i=NT)
        qTp = area(4096, 2048).rearrange("p (j t) -> p j t", j=4)
        qTr = area(6144, 2048).rearrange("p (j t) -> p j t", j=4)
        kz = area(8192, 4096).rearrange("p (b g e t) -> p b g e t", b=2, g=2, e=2)
        vS = area(12288, 1024).rearrange("p (i b n) -> p i b n", i=NT, b=2)
        gt = area(14432, 96).rearrange("p (i n) -> p i n", i=NT)
        pTc = area(14528, 1024).rearrange("p (g t) -> p g t", g=2)
        fl = area(15552, 2048).rearrange("p (b n) -> p b n", b=2)
        hid = area(17600, 256).rearrange("p (b n) -> p b n", b=2)
        hid_t = area(24256, 512)[0:64, :].rearrange("p (b n) -> p b n", b=2)
        thh = area(27328, 512)[0:64, :].rearrange("p (b n) -> p b n", b=2)
        kcz = area(17984, 128).rearrange("p (g e c) -> p g e c", g=2, e=2)
        vcz = area(18112, 512).rearrange("p (g r d) -> p g r d", g=2, r=4)
        pN = [area(18624, 512), area(19136, 512), area(19648, 512), area(24256, 512)]
        ptN = [area(20160, 4096).rearrange("p (b k t) -> p b k t", b=2, k=4),
               area(0, 4096).rearrange("p (b k t) -> p b k t", b=2, k=4)]
        rt = area(20160, 1024).rearrange("p (b n) -> p b n", b=4)
        kd = area(21184, 2048).rearrange("p (i b n) -> p i b n", i=NT, b=2)
        smC = area(24256, 512).rearrange("p (b n) -> p b n", b=2)
        Gn = area(24768, 2048).rearrange("p (j t) -> p j t", j=4)
        thC = area(26816, 1024).rearrange("p (b n) -> p b n", b=2)
        mixA = area(15552, 2048).rearrange("p (j t) -> p j t", j=4)
        def four(o):
            return area(o, 2048).rearrange("p (j t) -> p j t", j=4)

        rF, kF, vF, Gr = four(0), four(2048), four(4096), four(6144)
        raw = area(8192, 1539).rearrange("p (b n) -> p b n", b=3)
        wdad = area(9732, 512)
        dif = area(10244, 1024).rearrange("p (b n) -> p b n", b=2)
        yF = four(11268)
        lw, cum, iP, aF, kk = four(13316), four(17600), four(19648), four(21696), four(23744)
        sq = yF
        bx = area(11268, 2048)
        RORD = [12, 4, 5, 6, 7, 0, 1, 2, 3, 8, 9, 10, 11]
        ka = area(27328, 512)
        bxg, sqg = area(26816, 512), area(27328, 512)
        AR = hT[:, :, :].rearrange("p (j i) t -> p (j i t)", j=4).rearrange("p (j i a t) -> p j i a t", j=4, i=4, a=2)
        wslot = ring[:, NRAW * HALF:(NRAW + NHI) * HALF]
        B3 = wslot[:, 0:3072].rearrange("p (h m t) -> p h m t", h=8, m=3)
        Dm = wslot[:, 3072:4096].rearrange("p (h t) -> p h t", h=8)
        AE = area(2048, 2048).rearrange("p (h m t) -> p h m t", h=8, m=2)
        A2 = area(13316, 1024).rearrange("p (h t) -> p h t", h=8)
        D2 = area(14340, 1024).rearrange("p (h t) -> p h t", h=8)
        Qa = area(17600, 1024).rearrange("p (h t) -> p h t", h=8)
        Qb = area(18624, 1024).rearrange("p (h t) -> p h t", h=8)
        XG = area(23744, 1024).rearrange("p (h t) -> p h t", h=8)
        HG = area(24768, 1024).rearrange("p (h t) -> p h t", h=8)
        btm, ktm, vtm = area(8192, 512), area(8704, 512), area(9216, 512)
        MT = area(9728, 512).rearrange("p (c j k) -> p c j k", c=2, j=4)
        Bm = area(10240, 512).rearrange("p (c n) -> p c n", c=2)
        RHO = area(10752, 512)
        Sst = area(25792, 1024).rearrange("p (b n) -> p b n", b=4)
        mixB = hT[:, :, :].rearrange("p (j h) t -> p j h t", h=2)[:, :, 0, :]
        PC = stat[:, 544:576].rearrange("p (j c) -> p j c", j=4)

        UN = [(h, br, i) for h in range(8) for br in range(2) for i in range(NT)]

        block = ctx.enter_context(nc.Block())
        half_last = {}

        @block.tensor
        def _(pe):
            def begin(key, consumer):
                n = len(order)
                if n >= NBANK:
                    evacuated(pe, order[n - NBANK])
                order.append(key)
                J[key], who[key] = n, consumer
                count[consumer] += 1
                nth[key] = count[consumer]
                return bank[n % NBANK]

            def end(ins):
                ins.then_inc(filled, 1)

            def mm(o, l, r, start, stop):
                return nc.tensor.matmul(o, l, r, start=start, stop=stop)

            def need(name):
                n = HI[name]
                pe.wait_ge(raw_loaded[n % NRAW], 16 * (n // NRAW + 1))

            def turn_half(tag, i, hf, src):
                b = begin((tag, i, hf), "v")
                for q in range(4):
                    o = (4 * hf + q) * P
                    ins = nc.tensor.transpose(b[:, q * P:(q + 1) * P], src[:, o:o + P], ident)
                end(ins)

            def turn(tag, i):
                pe.wait_ge(S("xn_" + tag), i + 1)
                for hf in range(2):
                    turn_half(tag, i, hf, xn[:, i % 2, :])

            def need3(name):
                pe.wait_ge(s_wlo, splits.index(HI[name]) + 1)

            def used3(name):
                half_last[HI[name]] = len(order) - 1

            def three(o, left, right, start, stop):
                mm(o, left[0], right[0], start, False)
                mm(o, left[0], right[1], False, False)
                return mm(o, left[1], right[0], False, stop)

            def fm3(key, consumer, name, c0, act, ready=None):
                b = begin(key, consumer)
                w = W3(name)
                for k in range(KB):
                    if ready:
                        ready(k)
                    ins = three(b[:, :], [v[:, k, c0:c0 + P] for v in w], [v[:, k, :] for v in act], k == 0, k == KB - 1)
                end(ins)

            def tm3(key, consumer, w, i, c0, act, nk=KB, ready=None, m=256):
                b = begin(key, consumer)
                for k in range(nk):
                    if ready:
                        ready(k)
                    ins = three(b[:, 0:m], [v[:, k, i * P:(i + 1) * P] for v in act], [v[:, k, c0:c0 + m] for v in w],
                                k == 0, k == nk - 1)
                end(ins)

            def tail(jobs, tag):
                for i in range(3):
                    jobs(i)
                turn(tag, 0)
                jobs(3)
                turn(tag, 1)

            def head(tag, jobs):
                for i in range(NT):
                    def ready(k):
                        if k % 4 == 0 and i < 3:
                            pe.wait_ge(S("lo_" + tag), 2 * i + k // 4 + 1)
                        elif k % 4 == 0:
                            pe.wait_ge(S("lo3_" + tag), k // 4 + 1)

                    jobs(i, ready)
                    if i < 2:
                        turn(tag, i + 2)

            def act3(tag):
                return parts(hTf, low[tag], KB)

            def out_proj(tag, l):
                act = parts(o_high, hTf, KB)

                def ready(k):
                    pe.wait_ge(S("o_low"), 8 * l + k + 1)

                for n in range(4):
                    need3((tag, n))

                    def jobs(i):
                        tm3((tag, n, i), "v", W3((tag, n)), i, 0, act, ready=ready if (n, i) == (0, 0) else None)

                    if n < 3:
                        for i in range(NT):
                            jobs(i)
                    else:
                        tail(jobs, f"ple{l}")
                    used3((tag, n))
                    if n == 0:
                        pe.wait_ge(s_p[l], 16 * NT)
                        for k in range(2):
                            b = begin(("pT", l, k), "v")
                            for i in range(NT):
                                ins = nc.tensor.transpose(b[:, i * P:(i + 1) * P], p_tm[:, i, k * P:(k + 1) * P], ident)
                            end(ins)

            def ple(l, after):
                act = act3(f"ple{l}")
                pw = parts(pw_hi, pw_lo, 2)
                pT = tuple(rounded(v[:, :, :]) for v in (p_T, p_lo))
                for n in range(4):
                    need3(("PG", l, n))
                    if n == 0:
                        evacuated(pe, ("pT", l, 1))
                        pe.wait_ge(S("pw_low"), l + 1)

                    def jobs(i, ready=None):
                        tm3(("PG", l, n, i), "a", W3(("PG", l, n)), i, 0, act, ready=ready)
                        tm3(("PP", l, n, i), "v", pw, i, 256 * n, pT, nk=2)

                    if n == 0:
                        head(f"ple{l}", jobs)
                    elif n == 3 and after:
                        tail(jobs, after)
                    else:
                        for i in range(NT):
                            jobs(i)
                    used3(("PG", l, n))

            pe.wait_ge(s_ident, 16)
            pe.wait_ge(S("vrow_zero"), 1)
            pe.wait_ge(s_vrow, 16 * len(rows))
            b = begin("vec", "a")
            end(nc.tensor.transpose(b[:, 0:P], vrow[:, :], ident))

            turn("norm0", 0)
            turn("norm0", 1)
            act = act3("norm0")
            for n in AORD:
                need3(("A", n))
                if n == AORD[0]:
                    head("norm0", lambda i, ready: tm3(("Av", n, i), "a", W3(("A", n)), i, 0, act, ready=ready))
                elif n in range(8, 12):
                    for i in range(NT):
                        tm3(("Av", n, i), "a", W3(("A", n)), i, 0, act)
                else:
                    for s in range(2):
                        fm3(("A", n, s), "a" if n < 8 else "v", ("A", n), s * P, act)
                used3(("A", n))

            def scoresA(h):
                e, j = 64 * (h % 2), h // 2
                q = qT[e:e + 64, j, :]
                k = kT[e:e + 64, j, :]
                for hf in range(2):
                    b = begin(("AS", h, hf), "v")
                    for m in range(2):
                        t = 2 * hf + m
                        l = q[:, P * t:P * t + P]
                        r = k[:, P * t:P * t + 256] if t < 3 else ap(k, [(384, 2), (1, P)])
                        ins = mm(b[:, m * 256:(m + 1) * 256], l, r, True, True)
                    end(ins)

            def transA(h):
                for hf in range(2):
                    pe.wait_ge(S("A_probs"), 2 * h + hf + 1)
                    b = begin(("AT", h, hf), "a")
                    for m in range(2):
                        for c in range(2):
                            o = (2 * m + c) * P
                            ins = nc.tensor.transpose(b[:, o:o + P], pA[:, h % 3, 512 * hf + o:512 * hf + o + P], ident)
                    end(ins)

            def pvA(h):
                e = 64 * (h % 2)
                evacuated(pe, ("AT", h, 1))
                b = begin(("AO_", h), "v")
                for t in range(4):
                    for c in range(2):
                        kt = (t + c) if t < 3 else 3 * c
                        o = (2 * (t % 2) + c) * P
                        ins = mm(b[e:e + 64, t * P:(t + 1) * P], va[:, kt, h * 64:h * 64 + 64],
                                 ptA[:, h % 3, t // 2, o:o + P], c == 0, c == 1)
                end(ins)

            evacuated(pe, ("A", 7, 1))
            evacuated(pe, ("Av", 11, 3))
            for h in range(16 + 4):
                if h < 16:
                    scoresA(h)
                if h >= 4:
                    pvA(h - 4)
                if 2 <= h < 18:
                    transA(h - 2)
            out_proj("AO", 0)
            ple(0, "norm1")

            act = act3("norm1")
            for n in range(10):
                need3(("B", n))
                if n == 0:
                    head("norm1", lambda i, ready: tm3(("B", 0, i), "a", W3(("B", 0)), i, 0, act, ready=ready))
                elif n < 6:
                    for i in range(NT):
                        tm3(("B", n, i), "a", W3(("B", n)), i, 0, act)
                else:
                    for s in range(2):
                        fm3(("B", n, s), "v", ("B", n), s * P, act)
                used3(("B", n))
            for i in range(NT):
                pe.wait_ge(S("B_rope"), i + 1)
                pe.wait_ge(S("B_rope_k"), i + 1)
                for hf in range(2):
                    b = begin(("BqT", i, hf), "a")
                    for q in range(4):
                        o = (4 * hf + q) * P
                        ins = nc.tensor.transpose(b[:, q * P:(q + 1) * P], qB[:, i, o:o + P], ident)
                    end(ins)
                b = begin(("BkT", i), "a")
                for g in range(4):
                    ins = nc.tensor.transpose(b[:, g * P:(g + 1) * P], kD[:, i, g * P:(g + 1) * P], ident)
                end(ins)
            evacuated(pe, ("BkT", NT - 1))

            NB_ = 16 * NT

            def scoresB(u):
                h, i = divmod(u, NT)
                e = 64 * (h % 2)
                b = begin(("BS", u), "a")
                end(mm(b[:, :], qT[e:e + 64, h // 2, i * P:(i + 1) * P], kTB[e:e + 64, h // 4, :], True, True))

            def transB(u):
                pe.wait_ge(S("B_probs"), u + 1)
                b = begin(("BT", u), "a")
                for k in range(4):
                    ins = nc.tensor.transpose(b[:, k * P:(k + 1) * P], pB[:, u % 4, k * P:(k + 1) * P], ident)
                end(ins)

            def pvB(h):
                e = 64 * (h % 2)
                evacuated(pe, ("BT", NT * h + 3))
                b = begin(("BO_", h), "v")
                for k in range(4):
                    ins = mm(b[e:e + 64, :], vB[:, k, (h // 4) * 64:(h // 4) * 64 + 64], ptB[:, h % 2, k, :],
                             k == 0, k == 3)
                end(ins)

            for u in range(NB_ + 5):
                if u < NB_:
                    scoresB(u)
                if 3 <= u < NB_ + 3:
                    transB(u - 3)
                if u >= 8 and u % 4 == 0:
                    pvB((u - 8) // 4)
            out_proj("BO", 1)
            ple(1, None)

            for hf in range(2):
                for i in range(NT):
                    pe.wait_ge(S("xn_norm2"), i + 1)
                    turn_half("norm2", i, hf, xn4[:, i, :])

            def ready2(k):
                if k % 4 == 0:
                    pe.wait_ge(S("lo_norm2"), (2, 3)[k // 4])
                    pe.wait_ge(S("lo3_norm2"), (2, 5)[k // 4])

            act2 = act3("norm2")
            need3("Ckv")
            for n in range(2):
                fm3(("kvc", n), "v", "Ckv", n * P, act2, ready2 if n == 0 else None)
            used3("Ckv")

            def tokens(name, key):
                need3(name)
                for i in range(NT):
                    tm3((key, i), "a", W3(name), i, 0, act2)
                used3(name)

            tokens("Csel", "sel")
            tokens(("Cq", 0), "q0")
            tokens(("Cq", 1), "q1")
            tokens("Cwin", "win")
            need3("Cbg")
            fm3("bg", "a", "Cbg", 0, act2)
            used3("Cbg")

            for n, name in enumerate(("W1K", "W1V")):
                need((name, 0))
                need((name, 1))
                pe.wait_ge(S("C_flat"), n + 1)
                b = begin(("hid", n), "v")
                for ii in range(16):
                    ins = mm(b[0:64, 0:256], fl[:, n, ii * 64:ii * 64 + 64], W((name, ii // 8))[:, ii % 8, :],
                             ii == 0, ii == 15)
                end(ins)
                used3((name, 0))
                used3((name, 1))
                if n == 0:
                    evacuated(pe, "bg")
                    b = begin("bgT", "a")
                    for i in range(NT):
                        ins = nc.tensor.transpose(b[:, i * 24:i * 24 + 24], thC[0:24, 0, i * P:(i + 1) * P],
                                                  ident[0:24, 0:24])
                    end(ins)
            pe.wait_ge(S("C_rope"), 4)
            for i in range(NT):
                for name, src in (("qp", q2), ("qr", q2r)):
                    b = begin((name, i), "a")
                    for j in range(4):
                        ins = nc.tensor.transpose(b[:, j * P:(j + 1) * P], src[:, i, j * P:(j + 1) * P], ident)
                    end(ins)
                b = begin(("kz", i), "a")
                for m in range(4):
                    ins = nc.tensor.transpose(b[:, m * P:(m + 1) * P], kd[:, i, m // 2, (m % 2) * P:(m % 2) * P + P], ident)
                end(ins)
            evacuated(pe, ("hid", 1))
            b = begin("hidT", "a")
            for m in range(4):
                ins = nc.tensor.transpose(b[:, m * 64:m * 64 + 64], hid_t[:, m // 2, (m % 2) * P:(m % 2) * P + P],
                                          ident[0:64, 0:64])
            end(ins)

            def scores_c(i):
                b = begin(("cs", i), "v")
                for h in range(8):
                    ins = mm(b[:, h * 32:h * 32 + 32], qTp[:, h // 2, i * P:(i + 1) * P], kcz[:, h // 4, h % 2, :],
                             True, True)
                end(ins)

            def trans_c(i):
                pe.wait_ge(S("C_pc"), i + 1)
                b = begin(("ct", i), "a")
                for g in range(2):
                    ins = nc.tensor.transpose(b[:, g * P:(g + 1) * P], smC[:, i % 2, g * P:(g + 1) * P], ident)
                end(ins)

            def gate_c(s):
                if s % 2 == 0:
                    need3(("Cog", s // 2))
                fm3(("og", s), "v", ("Cog", s // 2), (s % 2) * P, act2)
                if s % 2:
                    used3(("Cog", s // 2))

            gate_c(0)
            pe.wait_ge(s_small, 64)
            evacuated(pe, "hidT")
            b = begin("kcmp", "v")
            for blk in range(2):
                ins = mm(b[0:64, 0:64], w2[:, 0, blk, :], hid[:, 0, blk * 64:blk * 64 + 64], blk == 0, blk == 1)
            end(ins)
            b = begin("vcmp", "v")
            for g in range(2):
                for blk in range(2):
                    ins = mm(b[0:32, g * 64:g * 64 + 64], hid[:, 1, blk * 64 + g * 32:blk * 64 + g * 32 + 32],
                             w2[:, 1, blk, :], blk == 0, blk == 1)
            end(ins)
            gate_c(1)
            evacuated(pe, ("kz", NT - 1))
            pe.wait_ge(S("C_cmp"), 12)
            scores_c(0)
            scores_c(1)
            gate_c(2)
            trans_c(0)
            trans_c(1)
            scores_c(2)
            scores_c(3)
            gate_c(3)
            trans_c(2)
            trans_c(3)

            def scoresN(u):
                h, br, i = UN[u]
                q = qTr[:, h // 2, i * P:(i + 1) * P]
                k = kz[:, br, h // 4, h % 2, :]
                b = begin(("NS", u), "a")
                if i:
                    mm(b[:, 0:i * P], q, k[:, 0:i * P], True, True)
                d = b[:, i * P:(i + 1) * P]
                mm(d, q, k[:, i * P:(i + 1) * P], True, False)
                end(mm(d, identb[:, :], causalb[:, :], False, True))

            def transN(u):
                h, br, i = UN[u]
                pe.wait_ge(S("N_probs"), u + 1)
                b = begin(("NT", u), "a")
                for k in range(i + 1):
                    ins = nc.tensor.transpose(b[:, k * P:(k + 1) * P], pN[u % 4][:, k * P:(k + 1) * P], ident)
                end(ins)

            def pvN(h):
                e, g = 64 * (h % 2), h // 4
                evacuated(pe, ("NT", 8 * h + 7))
                b = begin(("NO", h), "v")
                mm(b[e:e + 64, :], vcz[:, g, h % 4, :], pTc[:, g, :], True, False)
                for br in range(2):
                    for k in (3, 2, 1, 0):
                        ins = mm(b[e:e + 64, k * P:T], vS[:, k, br, g * 64:g * 64 + 64],
                                 ptN[h % 2][:, br, k, k * P:T], False, br == 1 and k == 0)
                end(ins)

            pe.wait_ge(S("bf16_constants"), 2)
            for u in range(len(UN) + 5):
                if u < len(UN):
                    scoresN(u)
                if 3 <= u < len(UN) + 3:
                    transN(u - 3)
                if u >= 12 and (u - 12) % 8 == 0:
                    pvN((u - 12) // 8)

            def project(ss):
                for s in ss:
                    name = ("R", s // 2)
                    if s % 2 == 0:
                        need3(name)
                    fm3(("R", s), "a", name, (s % 2) * P, act2)
                    if s % 2 or s == 12:
                        used3(name)

            def head_sums(key, src):
                b = begin(key, "v")
                for i in range(NT):
                    for j in range(4):
                        c = (4 * i + j) * 2
                        ins = mm(b[:, c:c + 2], src[:, j, i * P:(i + 1) * P], C("heads"), True, True)
                end(ins)

            def spread(key, j):
                b = begin((key, j), "v")
                for i in range(NT):
                    o = (4 * i + j) * P
                    ins = nc.tensor.transpose(b[:, i * P:(i + 1) * P], bx[:, o:o + P], ident)
                end(ins)

            project([12, 4, 5])
            pe.wait_ge(S("R_twd"), 1)
            for j in range(4):
                b = begin(("W", j), "a")
                end(mm(b[:, :], wa[0:64, j * P:(j + 1) * P], wdad[0:64, :], True, True))
            for j in range(4):
                b = begin(("A_", j), "a")
                end(mm(b[:, :], wa[64:128, j * P:(j + 1) * P], wdad[64:128, :], True, True))
            project([6, 7, 0, 1])
            pe.wait_ge(S("R_sq"), 4)
            head_sums("ks", sq)
            project([2, 3])
            pe.wait_ge(S("R_kx"), 1)
            for j in range(4):
                spread("kb", j)
            project([8, 9, 10, 11])
            for s in range(4):
                if s % 2 == 0:
                    need3(("Rg", s // 2))
                fm3(("rg", s), "v", ("Rg", s // 2), (s % 2) * P, act2)
                if s % 2:
                    used3(("Rg", s // 2))
                if s == 1:
                    pe.wait_ge(S("R_rk"), 4)
                    head_sums("bs", sq)
            pe.wait_ge(S("R_bx"), 1)
            for j in range(4):
                spread("bb", j)

            def four_heads(key, consumer, left, right, after=()):
                for bt in range(2):
                    for k in after:
                        evacuated(pe, (k, key[1], bt))
                    b = begin(key + (bt,), consumer)
                    for q in range(4):
                        h = 4 * bt + q
                        ins = mm(b[:, q * P:(q + 1) * P], left(h), right(h), True, True)
                    end(ins)

            def turned(key, consumer, src, after=()):
                for bt in range(2):
                    for k in after:
                        evacuated(pe, (k, key[1], bt if k != "gr" else 4 * bt + 3))
                    b = begin(key + (bt,), consumer)
                    for q in range(4):
                        ins = nc.tensor.transpose(b[:, q * P:(q + 1) * P], src(4 * bt + q), ident)
                    end(ins)

            mA, mE, mD = (lambda h: AE[:, h, 0, :]), (lambda h: AE[:, h, 1, :]), (lambda h: Dm[:, h, :])
            mA2, mD2 = (lambda h: A2[:, h, :]), (lambda h: D2[:, h, :])
            mQa, mQb = (lambda h: Qa[:, h, :]), (lambda h: Qb[:, h, :])
            def out_part(half, n, i):
                b = begin(("CO", half, n, i), "v")
                w = W(("CO", half, n))
                need(("CO", half, n))
                src = (mixA, mixB)[half]
                for k in range(4):
                    ins = mm(b[:, :], src[:, k, i * P:(i + 1) * P], w[:, k, :], k == 0, k == 3)
                end(ins)

            def mean_job(i):
                evacuated(pe, ("Y2", i))
                b = begin(("gm", i), "v")
                end(mm(b[:, :].rearrange("p (j t) -> p j t", j=4), C("headmean"), yF[:, :, i * P:(i + 1) * P], True, True))

            def square_job(i):
                pe.wait_ge(S("R_gsq"), i + 1)
                b = begin(("gs", i), "v")
                for j in range(4):
                    ins = mm(b[:, 2 * j:2 * j + 2], sqg[:, j * P:(j + 1) * P], C("heads"), True, True)
                end(ins)

            def spread_job(i):
                pe.wait_ge(S("R_gx"), i + 1)
                b = begin(("gb", i), "v")
                for j in range(4):
                    ins = nc.tensor.transpose(b[:, j * P:(j + 1) * P], bxg[:, j * P:(j + 1) * P], ident)
                end(ins)

            for i in range(NT):
                ti = slice(i * P, (i + 1) * P)
                for h in range(8):
                    e, j = 64 * (h % 2), h // 2
                    if i == 0:
                        pe.wait_ge(S("R_ops"), j + 1)
                    b = begin(("gr", i, h), "v")
                    mm(b[:, 0:256], aF[e:e + 64, j, ti], AR[e:e + 64, j, i, :, :], True, True)
                    end(mm(b[:, 256:512], iP[e:e + 64, j, ti], AR[e:e + 64, j, i, :, :], True, True))
                for n, src in enumerate((lambda j: AR[:, j, i, 0, :], lambda j: aF[:, j, ti], lambda j: iP[:, j, ti],
                                         lambda j: vF[:, j, ti])):
                    b = begin(("tm", i, n), "a")
                    for j in range(4):
                        ins = nc.tensor.transpose(b[:, j * P:(j + 1) * P], src(j), ident)
                    end(ins)
                if i:
                    mean_job(i - 1)
                turned(("D", i), "a", mA, ("gr",))
                b = begin(("X", i), "a")
                evacuated(pe, ("tm", i, 3))
                for h in range(8):
                    ins = mm(b[:, h * 64:h * 64 + 64], B3[:, h, 1, :], vtm[:, h * 64:h * 64 + 64], True, True)
                end(ins)
                four_heads(("A2", i), "a", mD, mA, ("D",))
                four_heads(("D2", i), "v", mA, mD)
                if i:
                    square_job(i - 1)
                four_heads(("Q2", i), "v", mD2, mQa, ("D2",))
                four_heads(("A4", i), "a", mD2, mA2, ("A2",))
                four_heads(("D4", i), "a", mA2, mD2)
                if i:
                    spread_job(i - 1)
                four_heads(("Q3", i), "v", mD, mQb, ("D4", "Q2"))
                four_heads(("D8", i), "a", mA, mD)
                four_heads(("Q4", i), "v", mD2, mQa, ("D8", "Q3"))
                turned(("QT", i), "a", mQb, ("Q4",))
                if i < NT - 1:
                    out_part(0, 0, i)
                four_heads(("KT", i), "a", mE, mA2, ("QT",))
                four_heads(("K", i), "v", mA2, mE)
                four_heads(("K2", i), "a", mA, mD, ("KT", "K"))
                four_heads(("Q5", i), "v", mD2, mQb, ("K2",))
                if i < NT - 1:
                    out_part(0, 1, i)
                four_heads(("RR", i), "v", mD, mQa, ("Q5",))
                evacuated(pe, ("X", i))
                four_heads(("HG", i), "a", mQb, lambda h: XG[:, h, :], ("RR",))
                evacuated(pe, ("HG", i, 1))
                b = begin(("rho", i), "v")
                for h in range(8):
                    e, j = 64 * (h % 2), h // 2
                    ins = mm(b[e:e + 64, j * P:(j + 1) * P], HG[:, h, 64:128], B3[:, h, 0, :], True, True)
                end(ins)
                for c in range(2):
                    cs = slice(64 * c, 64 * c + 64)
                    b = begin(("M", i, c), "v")
                    for h in range(8):
                        e, j = 64 * (h % 2), h // 2
                        ins = mm(b[e:e + 64, j * 64:j * 64 + 64], HG[cs, h, 64:128], btm[cs, h * 64:h * 64 + 64], True, True)
                    end(ins)
                for c in range(2):
                    cs = slice(64 * c, 64 * c + 64)
                    b = begin(("Bm", i, c), "a")
                    for h in range(8):
                        e, j = 64 * (h % 2), h // 2
                        o = b[e:e + 64, j * 64:j * 64 + 64]
                        mm(o, btm[cs, h * 64:h * 64 + 64], HG[cs, h, 0:64], True, False)
                        ins = mm(o, ktm[cs, h * 64:h * 64 + 64], vtm[cs, h * 64:h * 64 + 64], False, True)
                    end(ins)
                for c in range(2):
                    k = 2 * i + c
                    evacuated(pe, ("M", i, c))
                    pe.wait_ge(S("R_state"), k + 1)
                    b = begin(("St", k), "v")
                    for h in range(8):
                        e, j = 64 * (h % 2), h // 2
                        ins = mm(b[e:e + 64, j * 64:j * 64 + 64], MT[e:e + 64, c, j, :],
                                 Sst[e:e + 64, k % 4, j * 64:j * 64 + 64], True, True)
                    end(ins)
                    if c == 0:
                        b = begin(("Y1", i), "a")
                        for h in range(8):
                            e, j = 64 * (h % 2), h // 2
                            o = b[e:e + 64, j * P:(j + 1) * P]
                            mm(o, HG[:, h, 0:64], B3[:, h, 0, :], True, False)
                            ins = mm(o, vtm[:, h * 64:h * 64 + 64], B3[:, h, 2, :], False, True)
                        end(ins)
                evacuated(pe, ("rho", i))
                b = begin(("Y2", i), "v")
                for c in range(2):
                    for h in range(8):
                        e, j = 64 * (h % 2), h // 2
                        o = j * P + 64 * c
                        ins = mm(b[e:e + 64, o:o + 64], Sst[e:e + 64, (2 * i + c) % 4, j * 64:j * 64 + 64],
                                 RHO[e:e + 64, o:o + 64], True, True)
                end(ins)

            mean_job(NT - 1)
            out_part(0, 0, NT - 1)
            square_job(NT - 1)
            out_part(0, 1, NT - 1)
            spread_job(NT - 1)
            pe.wait_ge(S("R_done"), 4 * NT)
            for n in range(2):
                for i in range(NT):
                    out_part(1, n, i)

        @block.scalar
        def _(act):
            xin = A["x"][0].rearrange("(r c) d -> c r d", r=GR)
            act.dma_start(x[:, 0, :], xin[0:CT]).then_inc(s_x[0], 16)

            act.wait_ge(S("vrow_zero"), 1)
            c = 0
            for src, n in rows:
                act.dma_start(vrow[c:c + n, :], src).then_inc(s_vrow, 16)
                c += n
            act.dma_start(x[:, 3, :], xin[3 * CT:]).then_inc(s_x[3], 16)

            def copy(o, i, scale=1.0):
                return nc.scalar.activation(o, i, ACT.Copy, scale=scale)

            nsq = [0]

            def square(tag, i, col):
                if nsq[0]:
                    act.wait_ge(S("squares_done"), nsq[0])
                nsq[0] += 1
                nc.scalar.activation(junk, x[:, i, :], ACT.Square, accum_out=stat[:, col + i:col + i + 1])\
                  .then_inc(S("squares_done"), 1)
                act.wait_ge(S("squares_done"), nsq[0])
                act.sem_inc(S("ss_" + tag), 1)

            def squares(tag, ready, col):
                for i in range(NT):
                    ready(i)
                    square(tag, i, col)

            split = [0]

            def high(upto):
                while split[0] < len(splits) and splits[split[0]] <= upto:
                    n = splits[split[0]]
                    act.wait_ge(raw_loaded[n % NRAW], 16 * (n // NRAW + 1))
                    if split[0] >= NHI:
                        act.wait_ge(filled, half_last[splits[split[0] - NHI]] + 1)
                    m = halves[n][1][0] * halves[n][1][1]
                    nc.scalar.activation(rounded(high_slot(n)[:, 0:m]), raw_slot(n)[:, 0:m], ACT.Copy).then_inc(s_whi, 1)
                    split[0] += 1

            def high_half(tag, i, hf):
                evacuated(act, (tag, i, hf))
                nc.scalar.activation(rounded(tile_of(hTf, tag, i, hf)), tile_of(low[tag], tag, i, hf), ACT.Copy)\
                  .then_inc(S("hi_" + tag), 1)

            def high_tile(tag, i):
                for hf in range(2):
                    high_half(tag, i, hf)

            def head(tag, first, drain):
                if tag == "norm0":
                    high_tile(tag, 0)
                high_tile(tag, 1)
                drain(0)
                high_tile(tag, 2)
                high(first + 1)
                drain(1)
                high_tile(tag, 3)
                drain(2)
                drain(3)

            def high_pair(j):
                nc.scalar.activation(rounded(o_high[:, T * j:T * j + T]), hT[:, j, :], ACT.Copy)\
                    .then_inc(S("o_high"), 1)

            def loaded(i):
                act.wait_ge(s_x[i], 16)

            loaded(0)
            square("norm0", 0, 0)
            high(0)
            loaded(1)
            square("norm0", 1, 0)
            key = "vec"
            b = take(act, key)
            give(copy(vec[:, :], b[:, 0:P]), key)
            loaded(2)
            square("norm0", 2, 0)
            loaded(3)
            square("norm0", 3, 0)

            def drain_v(n, i):
                key = ("Av", n, i)
                b = take(act, key)
                give(copy(va[:, i, 256 * (n - 8):256 * (n - 7)], b[:, 0:256]), key)

            head("norm0", 0, lambda i: drain_v(AORD[0], i))
            for n in AORD[1:]:
                high(HI[("A", n)] + 1)
                if n in range(8, 12):
                    for i in range(NT):
                        drain_v(n, i)
                elif n < 8:
                    for s in range(2):
                        key = ("A", n, s)
                        b = take(act, key)
                        j = (2 * n + s) % 8
                        if n < 4:
                            copy(qT[:, j, 0:448], b[:, 64:512], 0.125)
                            give(copy(qT[:, j, 448:512], b[:, 0:64], 0.125), key)
                        else:
                            give(copy(kT[:, j, :], b[:, :]), key)
                else:
                    for s in range(2):
                        k = 2 * (n - 12) + s
                        b = take(act, ("A", n, s))
                        if k >= 2:
                            act.wait_ge(drained["v"], nth[("A", 12 + (k - 2) // 2, (k - 2) % 2)])
                        nc.scalar.activation(th[:, k % 2, :], b[:, :], ACT.Tanh, scale=0.5).then_inc(S("A_tanh"), 1)
            high(HI[("AO", 1)])

            def expA(h):
                for hf in range(2):
                    act.wait_ge(S("A_max"), 2 * h + hf + 1)
                    if h >= 3:
                        act.wait_ge(filled, J[("AT", h - 3, hf)] + 1)
                    for m in range(2):
                        c = 64 + 8 * (h % 2) + 2 * hf + m
                        o = 512 * hf + 256 * m
                        ins = nc.scalar.activation(pA[:, h % 3, o:o + 256], sA[:, h % 2, o:o + 256], ACT.Exp,
                                                   bias=stat[:, c:c + 1], accum_out=stat[:, c + 16:c + 17])
                    ins.then_inc(S("A_exp"), 1)

            def ptA_copy(h):
                for hf in range(2):
                    key = ("AT", h, hf)
                    b = take(act, key)
                    if h >= 3:
                        act.wait_ge(filled, J[("AO_", h - 3)] + 1)
                    give(copy(ptA[:, h % 3, hf, :], b[:, :]), key)

            for h in range(16 + 2):
                if h < 16:
                    expA(h)
                if h >= 2:
                    ptA_copy(h - 2)
                if h >= 6 and h % 2 == 0:
                    evacuated(act, ("AO_", h - 5))
                    act.wait_ge(S("A_o_mid"), h - 4)
                    high_pair((h - 6) // 2)
            for h in (13, 15):
                evacuated(act, ("AO_", h))
                act.wait_ge(S("A_o_mid"), h + 1)
                high_pair(h // 2)

            def ple(l, tag, col, after):
                act.wait_ge(s_pp[l], 16)
                nc.scalar.activation(rounded(pw_hi), pw_lo, ACT.Copy).then_inc(S("pw_high"), 1)
                for k in range(2):
                    b = take(act, ("pT", l, k))
                    nc.scalar.activation(rounded(p_T[:, k, :]), b[:, :], ACT.Copy).then_inc(S("p_high"), 1)
                for n in (1, 2, 3):
                    high(HI[(tag, n)] + 1)
                for i in range(NT):
                    evacuated(act, (tag, 3, i))
                    if i == 3:
                        high_tile(f"ple{l}", 0)
                    square(f"ple{l}", i, col)

                def drain(n, i):
                    key = ("PG", l, n, i)
                    u = 4 * n + i
                    b = take(act, key)
                    if u >= 4:
                        act.wait_ge(drained["v"], nth[("PP", l, (u - 4) // 4, (u - 4) % 4)])
                    give(nc.scalar.activation(thp[:, u % 4, :], b[:, 0:256], ACT.Tanh, scale=0.5), key)

                head(f"ple{l}", HI[("PG", l, 0)], lambda i: drain(0, i))
                for n in (1, 2, 3):
                    high(HI[("PG", l, n)] + 1)
                    for i in range(NT):
                        drain(n, i)
                        if n == 3 and i >= 1:
                            after(i - 1)
                if l == 0:
                    high_tile("norm1", 0)
                after(NT - 1)

            def finished(l, i):
                act.wait_ge(S("x_ple"), 16 * l + 12 + i + 1)

            def square1(i):
                finished(0, i)
                square("norm1", i, 8)

            ple(0, "AO", 4, square1)

            def drain_B(n, i):
                key = ("B", n, i)
                b = take(act, key)
                u = 4 * n + i
                if n < 5:
                    if u >= 2:
                        act.wait_ge(S("B_sq_read"), u - 1)
                    nc.scalar.activation(sqB[:, u % 2, :], b[:, 0:256], ACT.Square).then_inc(S("B_sq"), 1)
                if n < 4:
                    give(copy(qB[:, i, 256 * n:256 * n + 256], b[:, 0:256]), key)
                else:
                    give(copy((kB if n == 4 else vB)[:, i, :], b[:, 0:256]), key)

            head("norm1", HI[("B", 0)], lambda i: drain_B(0, i))
            for n in range(1, 10):
                high(HI[("B", n)] + 1)
                if n < 6:
                    for i in range(NT):
                        drain_B(n, i)
                else:
                    for s in range(2):
                        k = 2 * (n - 6) + s
                        b = take(act, ("B", n, s))
                        if k >= 2:
                            act.wait_ge(drained["v"], nth[("B", 6 + (k - 2) // 2, (k - 2) % 2)])
                        nc.scalar.activation(th[:, k % 2, :], b[:, :], ACT.Tanh, scale=0.5).then_inc(S("B_tanh"), 1)
            high(HI[("BO", 1)])
            for i in range(NT):
                for hf in range(2):
                    key = ("BqT", i, hf)
                    b = take(act, key)
                    give(copy(qT[:, 4 * hf:4 * hf + 4, i * P:(i + 1) * P], b[:, :].rearrange("p (j t) -> p j t", j=4)), key)
                key = ("BkT", i)
                b = take(act, key)
                give(copy(kTB[:, :, i * P:(i + 1) * P], b[:, :].rearrange("p (j t) -> p j t", j=4)), key)

            NB_ = 16 * NT
            for u in range(NB_ + 3):
                if u < NB_:
                    key = ("BS", u)
                    b = take(act, key)
                    act.wait_ge(S("B_max"), u + 1)
                    if u >= 4:
                        act.wait_ge(filled, J[("BT", u - 4)] + 1)
                    c = 128 + u % 4
                    give(nc.scalar.activation(pB[:, u % 4, :], b[:, :], ACT.Exp, bias=stat[:, c:c + 1],
                                              accum_out=stat[:, c + 4:c + 5]), key)
                if u >= 3:
                    v = u - 3
                    h, i = divmod(v, NT)
                    key = ("BT", v)
                    b = take(act, key)
                    if h >= 2:
                        act.wait_ge(filled, J[("BO_", h - 2)] + 1)
                    give(copy(ptB[:, h % 2, :, i * P:(i + 1) * P], b[:, :].rearrange("p (k t) -> p k t", k=4)), key)
                if u >= 18 and u % 8 == 2:
                    j = u // 8 - 2
                    evacuated(act, ("BO_", 2 * j + 1))
                    high_pair(j)
            evacuated(act, ("BO_", 15))
            high_pair(7)

            def square2(i):
                finished(1, i)
                square("fin", i, 16)
                if i:
                    act.wait_ge(S("x_gain"), i)
                    square("norm2", i - 1, 20)

            ple(1, "BO", 12, square2)
            act.wait_ge(S("x_gain"), NT)
            square("norm2", NT - 1, 20)
            act.wait_ge(S("fin_rstd"), 1)
            for i in range(NT):
                nc.scalar.activation(x[:, i, :], x[:, i, :], ACT.Copy, scale=stat[:, 32 + i:33 + i])\
                  .then_inc(S("x_fin"), 1)
            def tanhs(keys, name, first=0):
                for k, key in enumerate(keys, first):
                    b = take(act, key)
                    if k >= 2:
                        evacuated(act, (key[0], k - 2))
                    nc.scalar.activation(thC[:, k % 2, :], b[:, :], ACT.Tanh, scale=0.5).then_inc(S(name), 1)

            for hf in range(2):
                for i in range(NT):
                    high_half("norm2", i, hf)
            high(HI["Csel"])

            def keys_values(n, key):
                for i in range(NT):
                    b = take(act, (key, i))
                    copy(ap(kd[:, i, n, :], [(P, 2), (64, 2), (1, 64)]), ap(b[:, 0:P], [(64, 2), (0, 2), (1, 64)]))
                    give(copy(vS[:, i, n, :], b[:, P:256]), (key, i))

            high(HI[("Cq", 0)])
            keys_values(0, "sel")
            for n in range(2):
                high(HI[("Cq", n)] + 1)
                for i in range(NT):
                    key = (f"q{n}", i)
                    b = take(act, key)
                    copy(q2[:, i, 256 * n:256 * n + 256], b[:, 0:256])
                    give(copy(q2r[:, i, 256 * n:256 * n + 256], b[:, 0:256]), key)
            high(HI["Cbg"])
            keys_values(1, "win")
            b = take(act, "bg")
            give(nc.scalar.activation(thC[0:24, 0, :], b[0:24, :], ACT.Tanh, scale=0.5), "bg")
            for n in range(2):
                b = take(act, ("hid", n))
                nc.scalar.activation(thh[:, n, :], b[0:64, 0:256], ACT.Tanh, scale=0.5).then_inc(S("C_thh"), 1)
                if n == 0:
                    b = take(act, "bgT")
                    give(copy(gt[:, :, :], b[:, 0:96].rearrange("p (i n) -> p i n", i=NT)), "bgT")
            high(HI[("Cog", 0)])
            act.wait_ge(S("C_clear"), 3)
            for i in range(NT):
                for name, dst in (("qp", qTp), ("qr", qTr)):
                    key = (name, i)
                    b = take(act, key)
                    give(copy(dst[:, :, i * P:(i + 1) * P], b[:, :].rearrange("p (j t) -> p j t", j=4), 0.125), key)
                key = ("kz", i)
                b = take(act, key)
                for e in range(2):
                    es = slice(64 * e, 64 * e + 64)
                    ins = copy(ap(kz[es, 0, 0, e, :], [(1024, 4), (1, P)], i * P), b[es, :].rearrange("p (j t) -> p j t", j=4))
                give(ins, key)
            b = take(act, "hidT")
            give(copy(hid[:, :, :], b[:, 0:256].rearrange("p (b n) -> p b n", b=2)), "hidT")
            high(HI[("Cog", 1)])

            def exp_c(i):
                act.wait_ge(S("C_cs"), i + 1)
                nc.scalar.activation(smC[:, i % 2, :], smC[:, i % 2, :], ACT.Exp).then_inc(S("C_ce"), 1)

            def pTc_copy(i):
                key = ("ct", i)
                b = take(act, key)
                give(copy(pTc[:, :, i * P:(i + 1) * P], b[:, 0:256].rearrange("p (g t) -> p g t", g=2)), key)

            tanhs([("og", 0), ("og", 1)], "C_tanh")
            exp_c(0)
            exp_c(1)
            tanhs([("og", 2)], "C_tanh", 2)
            pTc_copy(0)
            pTc_copy(1)
            exp_c(2)
            exp_c(3)
            tanhs([("og", 3)], "C_tanh", 3)
            pTc_copy(2)
            pTc_copy(3)
            high(HI[("R", 2)])

            for u in range(len(UN) + 3):
                if u < len(UN):
                    nk = (UN[u][2] + 1) * P
                    key = ("NS", u)
                    b = take(act, key)
                    act.wait_ge(S("N_max"), u + 1)
                    if u >= 4:
                        act.wait_ge(filled, J[("NT", u - 4)] + 1)
                    c = 400 + u % 4
                    give(nc.scalar.activation(pN[u % 4][:, 0:nk], b[:, 0:nk], ACT.Exp, bias=stat[:, c:c + 1],
                                              accum_out=stat[:, c + 4:c + 5]), key)
                if u >= 3:
                    h, br, i = UN[u - 3]
                    key = ("NT", u - 3)
                    b = take(act, key)
                    if h >= 2:
                        act.wait_ge(filled, J[("NO", h - 2)] + 1)
                    give(copy(ptN[h % 2][:, br, 0:i + 1, i * P:(i + 1) * P],
                              b[:, 0:(i + 1) * P].rearrange("p (k t) -> p k t", k=i + 1)), key)

            evacuated(act, ("NO", 7))
            act.wait_ge(S("R_rawzero"), 1)
            def fetch(ss):
                for s in ss:
                    key = ("R", s)
                    b = take(act, key)
                    m = RORD.index(s)
                    if s % 2 == 0:
                        high(HI[("R", s // 2)] + 1)
                    if m >= 3:
                        act.wait_ge(S("R_mix"), m - 2)
                    give(copy(raw[:, m % 3, 1:513], b[:, :]), key)

            fetch([12])
            act.wait_ge(S("R_mix"), 1)
            nc.scalar.activation(wdad[0:64, :], wdad[0:64, :], ACT.Tanh).then_inc(S("R_twd"), 1)
            fetch([4, 5])
            act.wait_ge(S("R_half"), 1)
            for j in range(4):
                key = ("W", j)
                b = take(act, key)
                give(nc.scalar.activation(lw[:, j, :], b[:, :], ACT.Tanh, bias=stat[:, 576 + j:577 + j], scale=0.5), key)
            for j in range(4):
                key = ("A_", j)
                b = take(act, key)
                give(nc.scalar.activation(aF[:, j, :], b[:, :], ACT.Tanh, bias=stat[:, 580 + j:581 + j], scale=0.5), key)
            fetch([6, 7])
            for j in range(4):
                act.wait_ge(S("R_kkraw"), j + 1)
                nc.scalar.activation(sq[:, j, :], kk[:, j, :], ACT.Square).then_inc(S("R_sq"), 1)
            fetch([0, 1])
            for j in range(4):
                act.wait_ge(S("R_cum"), j + 1)
                nc.scalar.activation(iP[:, j, :], cum[:, j, :], ACT.Exp, scale=-1.0).then_inc(S("R_P"), 1)
                nc.scalar.activation(lw[:, j, :], lw[:, j, :], ACT.Exp).then_inc(S("R_P"), 1)
                nc.scalar.activation(cum[:, j, :], cum[:, j, :], ACT.Exp).then_inc(S("R_P"), 1)
            fetch([2, 3, 8, 9, 10, 11])
            high(HI[("Rg", 1)])
            tanhs([("rg", 0), ("rg", 1)], "R_tanh")
            tanhs([("rg", 2), ("rg", 3)], "R_tanh", 2)

            def move(key, dst):
                b = take(act, key)
                give(copy(dst, b[:, :].rearrange("p (h t) -> p h t", h=4)), key)

            def moves(key, dst):
                for bt in range(2):
                    move(key + (bt,), dst[:, 4 * bt:4 * bt + 4, :])

            def As():
                return AE[:, :, 0, :]

            def square_tile(i):
                act.wait_ge(S("R_centred"), i + 1)
                nc.scalar.activation(sqg.rearrange("p (j t) -> p j t", j=4), yF[:, :, i * P:(i + 1) * P], ACT.Square)\
                    .then_inc(S("R_gsq"), 1)

            for i in range(NT):
                key = ("tm", i, 0)
                b = take(act, key)
                give(copy(XG[:, :, 64:128], b[:, :].rearrange("p (h k) -> p h k", h=8)), key)
                for n, dst in ((1, btm), (2, ktm), (3, vtm)):
                    key = ("tm", i, n)
                    b = take(act, key)
                    give(copy(dst, b[:, :]), key)
                moves(("D", i), Dm)
                if i:
                    square_tile(i - 1)
                key = ("X", i)
                b = take(act, key)
                give(copy(XG[:, :, 0:64], b[:, :].rearrange("p (h k) -> p h k", h=8)), key)
                moves(("A2", i), A2)
                moves(("A4", i), As())
                moves(("D4", i), Dm)
                moves(("D8", i), D2)
                moves(("QT", i), A2)
                moves(("KT", i), Dm)
                moves(("K2", i), D2)
                moves(("HG", i), HG)
                for c in range(2):
                    key = ("Bm", i, c)
                    b = take(act, key)
                    if i >= 1:
                        act.wait_ge(S("R_state"), 2 * i + 1)
                    give(copy(Bm[:, c, :], b[:, 0:256]), key)
                key = ("Y1", i)
                b = take(act, key)
                give(copy(yF[:, :, i * P:(i + 1) * P], b[:, :].rearrange("p (j t) -> p j t", j=4)), key)
            square_tile(NT - 1)
            squares("out", lambda i: evacuated(act, ("CO", 1, 1, i)), 24)

        @block.vector
        def _(dve):
            chain = [0]

            def link(ins):
                chain[0] += 1
                ins.then_inc(s_v, 1)
                dve.wait_ge(s_v, chain[0])

            TT, TS, STT = nc.vector.tensor_tensor, nc.vector.tensor_scalar, nc.vector.scalar_tensor_tensor

            def rsqrt(y, v, t):
                link(TS(y.bitcast(I32), v.bitcast(I32), 1, None, ALU.arith_shift_right))
                link(TS(y.bitcast(I32), y.bitcast(I32), -1.0, RSQRT_MAGIC, ALU.mult, ALU.add))
                for _ in range(3):
                    link(STT(t, y, -0.5, y, ALU.mult, ALU.mult))
                    link(TT(t, t, v, ALU.mult))
                    link(STT(y, t, 1.5, y, ALU.add, ALU.mult))

            def rstd_tile(tag, col, i):
                dve.wait_ge(S("ss_" + tag), i + 1)
                v, y = stat[:, col + i:col + i + 1], stat[:, 32 + i:33 + i]
                t, h = stat[:, 36 + i:37 + i], stat[:, 40 + i:41 + i]
                TS(h, v, -0.5 / D, -0.5 * EPS, ALU.mult, ALU.add).then_inc(S("half_variance"), 1)
                halves_made[0] += 1
                link(TS(v, v, 1.0 / D, EPS, ALU.mult, ALU.add))
                link(TS(y.bitcast(I32), v.bitcast(I32), 1, None, ALU.arith_shift_right))
                link(TS(y.bitcast(I32), y.bitcast(I32), -1.0, RSQRT_MAGIC, ALU.mult, ALU.add))
                dve.wait_ge(S("half_variance"), halves_made[0])
                for _ in range(3):
                    link(STT(t, y, h, y, ALU.mult, ALU.mult))
                    link(STT(y, t, 1.5, y, ALU.add, ALU.mult))
                return y

            halves_made = [0]

            def scale_tile(tag, col, i):
                y = rstd_tile(tag, col, i)
                if i >= 2:
                    dve.wait_ge(filled, J[(tag, i - 2, 1)] + 1)
                TS(xn[:, i % 2, :], x[:, i, :], y, None, ALU.mult).then_inc(S("xn_" + tag), 1)

            def gain_half(tag, i, hf):
                g = vcol(tag, 0, 8)
                key = (tag, i, hf)
                b = take(dve, key)
                dst = tile_of(low[tag], tag, i, hf)
                if tag == "norm2":
                    give(TT(dst, b[:, :].rearrange("p (k c r) -> p k c r", k=4, r=GR),
                            ap(g, [(1, 4), (0, CT), (0, GR)], 4 * hf), ALU.mult), key)
                else:
                    give(TT(dst, b[:, :].rearrange("p (k t) -> p k t", k=4), ap(g, [(1, 4), (0, P)], 4 * hf),
                            ALU.mult), key)

            def gain_tile(tag, i):
                for hf in range(2):
                    gain_half(tag, i, hf)

            def low_half(tag, i, hf, n):
                dve.wait_ge(S("hi_" + tag), n)
                v = tile_of(low[tag], tag, i, hf)
                TT(rounded(v), v, read_back(tile_of(hTf, tag, i, hf)), ALU.subtract).then_inc(S("lo3_" + tag), 1)

            def low_tile3(tag):
                for hf in range(2):
                    low_half(tag, 3, hf, 6 + hf + 1)

            def norm_after(tag, col, last):
                last(0)
                last(1)
                scale_tile(tag, col, 0)
                last(2)
                scale_tile(tag, col, 1)
                gain_tile(tag, 0)
                last(3)
                gain_tile(tag, 1)
                scale_tile(tag, col, 2)
                scale_tile(tag, col, 3)

            nc.vector.memset(vrow[64:P, :], 0.0).then_inc(S("vrow_zero"), 1)
            nc.vector.memset(rrev, 0.0).then_inc(s_rpbr, 1)
            dve.wait_ge(s_rpb, 16)
            dve.wait_ge(s_rpbr, 1)
            nc.vector.tensor_copy(ap(rrev, [(-64, 15), (-1, 31)], 1007), rpb_in[0:16, 0:465].rearrange(
                "p (a b) -> p a b", a=15)).then_inc(s_rpbr, 1)
            norm_after("norm0", 0, lambda i: evacuated(dve, "vec") if i == 2 else None)
            gain_tile("norm0", 2)
            gain_tile("norm0", 3)
            low_tile3("norm0")

            def gates(keys, name, dst):
                for k, key in enumerate(keys):
                    b = take(dve, key)
                    dve.wait_ge(S(name), k + 1)
                    give(STT(dst[:, k, :], th[:, k % 2, :], 1.0, b[:, :], ALU.add, ALU.mult), key)

            gates([("A", 12 + k // 2, k % 2) for k in range(8)], "A_tanh", G)
            dve.wait_ge(s_ident, 16)
            dve.wait_ge(s_cst, 16)
            nc.vector.tensor_copy(identb[:, :], ident).then_inc(S("bf16_constants"), 1)
            nc.vector.tensor_copy(causalb[:, :], C("causal")).then_inc(S("bf16_constants"), 1)

            dve.wait_ge(S("bias_edge"), 2)

            def frontA(h):
                dve.wait_ge(s_bias, 3 * h + 3)
                for hf in range(2):
                    key = ("AS", h, hf)
                    b = take(dve, key)
                    if h >= 2:
                        dve.wait_ge(S("A_exp"), 2 * (h - 2) + hf + 1)
                    s = sA[:, h % 2, 512 * hf:512 * hf + 512]
                    w = ap(bias[:, h % 2, :], [(0, 2), (1, 256)]) if hf == 0 else \
                        bias[:, h % 2, :].rearrange("p (m n) -> p m n", m=2)
                    ins = TT(s.rearrange("p (m n) -> p m n", m=2), b[:, :].rearrange("p (m n) -> p m n", m=2), w, ALU.add)
                    give(ins, key)
                    evacuated(dve, key)
                    c = 64 + 8 * (h % 2) + 2 * hf
                    ins = nc.vector.tensor_reduce(stat[:, c:c + 2], s.rearrange("p (m n) -> p m n", m=2), X,
                                                  ALU.max, negate=True)
                    ins.then_inc(S("A_max"), 1)

            def probsA(h):
                for hf in range(2):
                    dve.wait_ge(S("A_exp"), 2 * h + hf + 1)
                    c = 64 + 8 * (h % 2) + 2 * hf
                    link(nc.vector.reciprocal(stat[:, c + 32:c + 34], stat[:, c + 16:c + 18]))
                    for m in range(2):
                        o = 512 * hf + 256 * m
                        ins = TS(pA[:, h % 3, o:o + 256], pA[:, h % 3, o:o + 256], stat[:, c + 32 + m:c + 33 + m],
                                 None, ALU.mult)
                    ins.then_inc(S("A_probs"), 1)

            def outA(h):
                e, j = 64 * (h % 2), h // 2
                key = ("AO_", h)
                b = take(dve, key)
                g = G[e:e + 64, j, :]
                o = hT[e:e + 64, j, :]
                s = b[e:e + 64, :]
                STT(o[:, 64:512], s[:, 0:448], 0.5, g[:, 64:512], ALU.mult, ALU.mult).then_inc(S("A_o_mid"), 1)
                give(STT(o[:, 0:64], s[:, 448:512], 0.5, g[:, 0:64], ALU.mult, ALU.mult), key)

            for h in range(16 + 5):
                if h >= 5:
                    outA(h - 5)
                if h < 16:
                    frontA(h)
                if 1 <= h < 17:
                    probsA(h - 1)
            def add_proj(tag, n, i, w):
                key = (tag, n, i)
                b = take(dve, key)
                xs = x[:, i, w * n:w * n + w]
                give(TT(xs, xs, b[:, 0:w], ALU.add), key)
                evacuated(dve, key)

            def ple(l, tag, col, after):
                for i in range(NT):
                    add_proj(tag, 0, i, 256)
                for k in range(2):
                    key = ("pT", l, k)
                    b = take(dve, key)
                    dve.wait_ge(S("p_high"), 2 * l + k + 1)
                    give(TT(rounded(p_lo[:, k, :]), b[:, :], read_back(p_T[:, k, :]), ALU.subtract), key)
                for n in (1, 2):
                    for i in range(NT):
                        add_proj(tag, n, i, 256)
                norm_after(f"ple{l}", col, lambda i: add_proj(tag, 3, i, 256))

                def add(n, i):
                    key = ("PP", l, n, i)
                    u = 4 * n + i
                    b = take(dve, key)
                    evacuated(dve, ("PG", l, n, i))
                    give(STT(tp[:, u % 2, :], thp[:, u % 4, :], 1.0, b[:, 0:256], ALU.add, ALU.mult), key)
                    evacuated(dve, key)
                    xs = x[:, i, 256 * n:256 * n + 256]
                    STT(xs, tp[:, u % 2, :], 0.5, xs, ALU.mult, ALU.add).then_inc(S("x_ple"), 1)

                add(0, 0)
                gain_tile(f"ple{l}", 2)
                add(0, 1)
                gain_tile(f"ple{l}", 3)
                low_tile3(f"ple{l}")
                add(0, 2)
                add(0, 3)
                for n in (1, 2):
                    for i in range(NT):
                        add(n, i)
                after(lambda i: add(3, i))

            ple(0, "AO", 4, lambda last: norm_after("norm1", 8, last))
            gain_tile("norm1", 2)
            gain_tile("norm1", 3)
            low_tile3("norm1")

            dve.wait_ge(S("gqk_loaded"), 32)
            cb = CAT["ropeb"][0]
            tab = cst[:, cb:cb + 2 * NT * HD]
            for n, (dst, sc) in enumerate(((tabq, 0.125), (tabk, 1.0))):
                g = gqk[:, 64 * n:64 * n + 64]
                o = ap(dst[:, 0, :], [(64, 4), (1, 64)])
                STT(o, ap(tab, [(64, 4), (1, 64)]), sc, ap(g, [(0, 4), (1, 64)]), ALU.mult, ALU.mult)
                for hf in range(2):
                    for s in range(2):
                        a = 32 * s + 16 * hf
                        STT(ap(dst[:, 1, :], [(64, 4), (1, 16)], a), ap(tab, [(64, 4), (1, 16)], NT * HD + a), sc,
                            ap(g, [(0, 4), (1, 16)], 32 * s + 16 * (1 - hf)), ALU.mult, ALU.mult)\
                            .then_inc(S("B_tab"), 1)
            dve.wait_ge(S("B_tab"), 8)
            ssq = stat[:, 160:240].rearrange("p (i h) -> p i h", i=NT)
            for n in range(5):
                for i in range(NT):
                    u = 4 * n + i
                    dve.wait_ge(S("B_sq"), u + 1)
                    nc.vector.tensor_reduce(ssq[:, i, 4 * n:4 * n + 4],
                                            sqB[:, u % 2, :].rearrange("p (h d) -> p h d", d=64), X, ALU.add)\
                        .then_inc(S("B_sq_read"), 1)
            dve.wait_ge(S("B_sq_read"), 20)
            link(TS(stat[:, 160:240], stat[:, 160:240], 1.0 / HD, EPS, ALU.mult, ALU.add))
            rsqrt(stat[:, 240:320], stat[:, 160:240], stat[:, 320:400])
            evacuated(dve, ("B", 4, 3))

            def rope(src, nh, col, tabs, i, a, b, last):
                v = ap(src, [(64, nh), (1, 64)])
                link(TT(v, v, ap(stat[:, col:col + nh], [(1, nh), (0, 64)]), ALU.mult))
                TT(ap(a, [(64, nh), (1, 64)]), v, ap(tabs[:, 0, :], [(0, nh), (1, 64)], 64 * i), ALU.mult)\
                    .then_inc(S("B_rope_t"), 1)
                for hf in range(2):
                    TT(ap(b, [(64, nh), (32, 2), (1, 16)], 16 * hf), ap(src, [(64, nh), (32, 2), (1, 16)], 16 * (1 - hf)),
                       ap(tabs[:, 1, :], [(0, nh), (32, 2), (1, 16)], 64 * i + 16 * hf), ALU.mult)\
                        .then_inc(S("B_rope_t"), 1)
                rope_n[0] += 3
                dve.wait_ge(S("B_rope_t"), rope_n[0])
                if last:
                    TT(src, a[:, 0:64 * nh], b[:, 0:64 * nh], ALU.add).then_inc(S("B_rope"), 1)
                else:
                    TT(ap(kD[:, i, :], [(128, nh), (64, 2), (1, 64)]), ap(a, [(64, nh), (0, 2), (1, 64)]),
                       ap(b, [(64, nh), (0, 2), (1, 64)]), ALU.add).then_inc(S("B_rope_k"), 1)

            def gates_B(k):
                key = ("B", 6 + k // 2, k % 2)
                b = take(dve, key)
                dve.wait_ge(S("B_tanh"), k + 1)
                give(STT(G[:, k, :], th[:, k % 2, :], 1.0, b[:, :], ALU.add, ALU.mult), key)

            rope_n = [0]
            for i in range(NT):
                rope(kB[:, i, :], 4, 240 + 20 * i + 16, tabk, i, tkB[:, 0:256], tkB[:, 256:512], False)
                rope(qB[:, i, :], 16, 240 + 20 * i, tabq, i, t1B, t2B, True)
                dve.wait_ge(S("B_rope"), i + 1)
                gates_B(2 * i)
                gates_B(2 * i + 1)

            NB_ = 16 * NT

            def outB(h):
                e = 64 * (h % 2)
                key = ("BO_", h)
                b = take(dve, key)
                give(STT(hT[e:e + 64, h // 2, :], b[e:e + 64, :], 0.5, G[e:e + 64, h // 2, :], ALU.mult, ALU.mult), key)

            for u in range(NB_ + 1):
                if u >= 9 and u % 4 == 1:
                    outB((u - 9) // 4)
                if u < NB_:
                    b = take(dve, ("BS", u))
                    if u >= 4:
                        evacuated(dve, ("BS", u - 4))
                    nc.vector.tensor_reduce(stat[:, 128 + u % 4:129 + u % 4], b[:, :], X, ALU.max, negate=True)\
                        .then_inc(S("B_max"), 1)
                if u >= 1:
                    v = u - 1
                    evacuated(dve, ("BS", v))
                    c = 136 + v % 4
                    link(nc.vector.reciprocal(stat[:, c:c + 1], stat[:, c - 4:c - 3]))
                    TS(pB[:, v % 4, :], pB[:, v % 4, :], stat[:, c:c + 1], None, ALU.mult).then_inc(S("B_probs"), 1)
            outB(14)
            outB(15)

            def final_norm(last):
                dve.wait_ge(s_gb[0], 16)
                for i in range(NT):
                    last(i)
                    if i:
                        times_gain(i - 1)
                times_gain(NT - 1)
                v, y, t = stat[:, 16:20], stat[:, 32:36], stat[:, 36:40]
                link(TS(v, v, 1.0 / D, EPS, ALU.mult, ALU.add))
                rsqrt(y, v, t)
                dve.sem_inc(S("fin_rstd"), 1)
                dve.wait_ge(S("ss_norm2"), NT)
                v2, y2 = stat[:, 20:24], stat[:, 44:48]
                link(TT(v2, v2, y, ALU.mult))
                link(TT(v2, v2, y, ALU.mult))
                link(TS(v2, v2, 1.0 / D, EPS, ALU.mult, ALU.add))
                rsqrt(y2, v2, stat[:, 48:52])
                for i in range(NT):
                    dve.wait_ge(S("x_fin"), i + 1)
                    TS(xn4[:, i, :], x[:, i, :], y2[:, i:i + 1], None, ALU.mult).then_inc(S("xn_norm2"), 1)

            def times_gain(i):
                dve.wait_ge(S("ss_fin"), i + 1)
                TT(x[:, i, :], x[:, i, :], gb[:, :], ALU.mult).then_inc(S("x_gain"), 1)

            ple(1, "BO", 12, final_norm)
            dve.wait_ge(S("xn_norm2"), NT)
            for hf in range(2):
                dve.wait_ge(s_kept[0], 16 * 2)
                if hf:
                    dve.wait_ge(s_kept[1], 16 * 2)
                for i in range(NT):
                    gain_half("norm2", i, hf)
                for i in ((1, 2), (1, 2, 3))[hf]:
                    low_half("norm2", i, hf, 4 * hf + i + 1)
            nc.vector.memset(fl[:, :, :], 0.0).then_inc(S("C_flz"), 1)
            dve.wait_ge(S("C_flz"), 1)
            for n in range(2):
                key = ("kvc", n)
                b = take(dve, key)
                m = 0
                for g in range(2):
                    for par in range(2):
                        for hi in range(2):
                            src = ap(b[64 * g:64 * g + 64, :], [(2, 8), (16, 31)], 16 * hi + par)
                            dst = ap(fl[64 * par:64 * par + 64, n, :], [(64, 8), (1, 31)], 8 * hi * 64 + 32 * g)
                            ins = nc.vector.tensor_copy(dst, src)
                            m += 1
                            if m < 8:
                                ins.then_inc(S("C_flcopy"), 1)
                give(ins, key)
                dve.wait_ge(S("C_flcopy"), 7 * (n + 1))
                evacuated(dve, key)
                pos = vcol("posk" if n == 0 else "posv", 0, 16)
                f = ap(fl[:, n, :], [(64, 16), (1, 64)])
                TT(f, f, ap(pos, [(1, 16), (0, 64)]), ALU.add).then_inc(S("C_flat"), 1)

            def gatesC(keys, name, dst, first=0):
                for k, key in enumerate(keys, first):
                    b = take(dve, key)
                    dve.wait_ge(S(name), k + 1)
                    give(STT(dst[:, k, :], thC[:, k % 2, :], 1.0, b[:, :], ALU.add, ALU.mult), key)

            evacuated(dve, ("win", NT - 1))
            for n, (src, dst) in enumerate(((q2, q2r), (kd, kd))):
                src, dst = src[:, 0], dst[:, 0]

                def part(v, o):
                    return ap(v, [(512, NT), (64, 8), (1, 8)], o)

                def tabs(name):
                    return ap(C(name), [(8, NT), (0, 8), (1, 8)])

                r4 = [ap(rt[:, k, :], [(64, NT), (8, 8), (1, 8)]) for k in range(4)]
                TT(r4[0], part(src, 0), tabs("cos2"), ALU.mult).then_inc(S("C_rt"), 1)
                TT(r4[1], part(src, 8), tabs("sin2"), ALU.mult).then_inc(S("C_rt"), 1)
                TT(r4[2], part(src, 8), tabs("cos2"), ALU.mult).then_inc(S("C_rt"), 1)
                TT(r4[3], part(src, 0), tabs("sin2"), ALU.mult).then_inc(S("C_rt"), 1)
                dve.wait_ge(S("C_rt"), 4 * n + 4)
                TT(part(dst, 0), r4[0], r4[1], ALU.subtract).then_inc(S("C_rope"), 1)
                TT(part(dst, 8), r4[2], r4[3], ALU.add).then_inc(S("C_rope"), 1)
                dve.wait_ge(S("C_rope"), 2 * n + 2)
            evacuated(dve, "bgT")
            link(TS(gt[:, :, :], gt[:, :, :], 0.5, 0.5, ALU.mult, ALU.add))
            for n in range(2):
                key = ("hid", n)
                b = take(dve, key)
                dve.wait_ge(S("C_thh"), n + 1)
                give(STT(hid_t[:, n, :], thh[:, n, :], 1.0, b[0:64, 0:256], ALU.add, ALU.mult), key)
            gatesC([("og", 0)], "C_tanh", Gn)
            dve.wait_ge(S("C_clear"), 3)
            b = take(dve, "kcmp")
            for e in range(2):
                ins = TS(kcz[64 * e:64 * e + 64, :, e, :], b[0:64, 0:64].rearrange("p (g c) -> p g c", g=2), 0.5, None,
                         ALU.mult)
                if e == 0:
                    ins.then_inc(S("C_cmp"), 1)
            give(ins, "kcmp")
            evacuated(dve, "kcmp")
            b = take(dve, "vcmp")
            for g in range(2):
                for r in range(4):
                    ins = TS(vcz[32 * r:32 * r + 32, g, r, :], b[0:32, g * 64:g * 64 + 64], 0.5, None, ALU.mult)
                    if (g, r) != (1, 3):
                        ins.then_inc(S("C_cmp"), 1)
            give(ins, "vcmp")
            evacuated(dve, "vcmp")
            dve.sem_inc(S("C_cmp"), 4)
            gatesC([("og", 1)], "C_tanh", Gn, 1)

            def heads8(i):
                return smC[:, i % 2, :].rearrange("p (h c) -> p h c", h=8)

            def softmax_c(i):
                if i >= 2:
                    dve.wait_ge(filled, J[("ct", i - 2)] + 1)
                s = heads8(i)
                key = ("cs", i)
                b = take(dve, key)
                give(TT(s, b[:, 0:256].rearrange("p (h c) -> p h c", h=8),
                        ap(C("cmpneg"), [(0, 8), (1, 32)], 32 * i), ALU.add), key)
                evacuated(dve, key)
                mx, sm, sc = stat[:, 416:424], stat[:, 424:432], stat[:, 432:440]
                link(nc.vector.tensor_reduce(mx, s, X, ALU.max))
                TT(s, s, ap(mx, [(1, 8), (0, 32)]), ALU.subtract).then_inc(S("C_cs"), 1)
                dve.wait_ge(S("C_ce"), i + 1)
                link(nc.vector.tensor_reduce(sm, s, X, ALU.add))
                link(nc.vector.reciprocal(sm, sm))
                link(TT(sc, sm, ap(gt[:, i, :], [(3, 8)]), ALU.mult))
                link(TT(s, s, ap(C("cmpok"), [(0, 8), (1, 32)], 32 * i), ALU.mult))
                TT(s, s, ap(sc, [(1, 8), (0, 32)]), ALU.mult).then_inc(S("C_pc"), 1)

            softmax_c(0)
            softmax_c(1)
            gatesC([("og", 2)], "C_tanh", Gn, 2)
            softmax_c(2)
            softmax_c(3)
            gatesC([("og", 3)], "C_tanh", Gn, 3)

            def outN(h):
                e, j = 64 * (h % 2), h // 2
                key = ("NO", h)
                b = take(dve, key)
                give(STT(ap(mixA[e:e + 64, j, :], [(1, GR), (GR, GW)]), b[e:e + 64, :].rearrange("p (r c) -> p r c", r=GR),
                         0.5, Gn[e:e + 64, j, :].rearrange("p (r c) -> p r c", r=GR), ALU.mult, ALU.mult), key)

            for u in range(len(UN) + 4):
                if u >= 13 and (u - 13) % 8 == 0:
                    outN((u - 13) // 8)
                if u < len(UN):
                    nk = (UN[u][2] + 1) * P
                    b = take(dve, ("NS", u))
                    if u >= 4:
                        evacuated(dve, ("NS", u - 4))
                    nc.vector.tensor_reduce(stat[:, 400 + u % 4:401 + u % 4], b[:, 0:nk], X, ALU.max, negate=True)\
                        .then_inc(S("N_max"), 1)
                if 1 <= u < len(UN) + 1:
                    v = u - 1
                    h, br, i = UN[v]
                    nk = (i + 1) * P
                    evacuated(dve, ("NS", v))
                    c = 408 + v % 4
                    link(nc.vector.reciprocal(stat[:, c:c + 1], stat[:, c - 4:c - 3]))
                    TS(pN[v % 4][:, 0:nk], pN[v % 4][:, 0:nk], stat[:, c:c + 1], gt[:, i, 3 * h + 1 + br:3 * h + 2 + br],
                       ALU.mult, ALU.mult).then_inc(S("N_probs"), 1)
            outN(7)

            nc.vector.memset(ap(raw[:, 0, :], [(513, 3)]), 0.0).then_inc(S("R_rawzero"), 1)
            dsts = [rF[:, j, :] for j in range(4)] + [kF[:, j, :] for j in range(4)] + [vF[:, j, :] for j in range(4)] + [wdad]
            TS(stat[:, 576:584], vec[:, V0["w0"]:V0["w0"] + 8], 0.5, None, ALU.mult).then_inc(S("R_half"), 1)

            def mix(ss):
                for s in ss:
                    m = RORD.index(s)
                    dve.wait_ge(S("R_dif"), m + 1)
                    STT(dsts[s], dif[:, m % 2, :], vcol("mu", s), raw[:, m % 3, 1:513], ALU.mult, ALU.add)\
                        .then_inc(S("R_mix"), 1)

            mix([12, 4, 5])
            for j in range(4):
                evacuated(dve, ("W", j))
                link(TS(lw[:, j, :], lw[:, j, :], -LOGC / 2, -LOGC / 2, ALU.mult, ALU.add))
                link(nc.vector.tensor_tensor_scan(cum[:, j, :], C("chunk"), lw[:, j, :], 0.0, ALU.mult, ALU.add))
                TT(lw[:, j, :], cum[:, j, :], lw[:, j, :], ALU.subtract).then_inc(S("R_cum"), 1)
            mix([6, 7])
            dve.wait_ge(S("R_mix"), 5)
            for j in range(4):
                TS(kk[:, j, :], kF[:, j, :], vcol("kk", j), None, ALU.mult).then_inc(S("R_kkraw"), 1)
            dve.wait_ge(S("R_kkraw"), 4)
            mix([0, 1])
            for j in range(4):
                evacuated(dve, ("A_", j))
                link(TS(aF[:, j, :], aF[:, j, :], 0.5, 0.5, ALU.mult, ALU.add))
                link(TS(ka, aF[:, j, :], -1.0, vcol("ka", j), ALU.add, ALU.mult))
                link(STT(kF[:, j, :], ka, 1.0, kF[:, j, :], ALU.add, ALU.mult))
            b = take(dve, "ks")
            give(TS(stat[:, 448:480], b[:, 0:32], 1e-24, None, ALU.max), "ks")
            evacuated(dve, "ks")
            rsqrt(stat[:, 480:512], stat[:, 448:480], stat[:, 512:544])
            bx3 = bx.rearrange("p (s d) -> p s d", d=64)
            nc.vector.tensor_copy(bx3, ap(stat[:, 480:512], [(1, 32), (0, 64)])).then_inc(S("R_kx"), 1)
            mix([2, 3])
            for j in range(4):
                key = ("kb", j)
                b = take(dve, key)
                give(TT(kk[:, j, :], kk[:, j, :], b[:, :], ALU.mult), key)
            evacuated(dve, ("kb", 3))
            dve.wait_ge(S("R_P"), 12)
            dve.wait_ge(S("R_mix"), 9)
            for j in range(4):
                link(TT(aF[:, j, :], aF[:, j, :], kk[:, j, :], ALU.mult))
                TT(aF[:, j, :], aF[:, j, :], iP[:, j, :], ALU.mult).then_inc(S("R_ar"), 1)
                STT(sq[:, j, :], rF[:, j, :], vcol("rk", j), kF[:, j, :], ALU.mult, ALU.mult).then_inc(S("R_rk"), 1)
                nc.vector.tensor_copy(PC[:, j, :], ap(cum[:, j, :], [(CH, 8)], CH - 1)).then_inc(S("R_ar"), 1)
                dve.wait_ge(S("R_ar"), 2 * j + 2)
                TT(iP[:, j, :], kF[:, j, :], iP[:, j, :], ALU.mult).then_inc(S("R_kap"), 1)
                mix([8 + j])
            gatesC([("rg", 0), ("rg", 1)], "R_tanh", Gr)
            b = take(dve, "bs")
            give(nc.vector.tensor_copy(bx3, ap(b[:, 0:32], [(1, 32), (0, 64)])), "bs")
            evacuated(dve, "bs")
            dve.sem_inc(S("R_bx"), 1)
            gatesC([("rg", 2), ("rg", 3)], "R_tanh", Gr, 2)
            dve.wait_ge(S("R_kap"), 4)
            dve.wait_ge(filled, J[("rg", 3)] + 1)
            for j in range(4):
                def tiles(v):
                    return v.rearrange("p (i t) -> p i t", i=NT)

                STT(AR[:, j, :, 0, :], tiles(kk[:, j, :]), -1.0, tiles(lw[:, j, :]), ALU.mult, ALU.mult).then_inc(S("R_ar"), 1)
                TT(AR[:, j, :, 1, :], tiles(rF[:, j, :]), tiles(cum[:, j, :]), ALU.mult).then_inc(S("R_ar"), 1)
                dve.wait_ge(S("R_ar"), 8 + 2 * j + 2)
                dve.sem_inc(S("R_ops"), 1)
            nc.vector.memset(Sst[:, 0, :], 0.0).then_inc(S("R_state"), 1)
            dve.wait_ge(S("R_mix"), 13)
            for j in range(4):
                key = ("bb", j)
                b = take(dve, key)
                give(TT(rF[:, j, :], vF[:, j, :], b[:, :], ALU.mult), key)

            def plus(key, dst, src):
                for bt in range(2):
                    b = take(dve, key + (bt,))
                    hs = slice(4 * bt, 4 * bt + 4)
                    give(TT(dst[:, hs, :], b[:, :].rearrange("p (h t) -> p h t", h=4), src[:, hs, :], ALU.add), key + (bt,))
                evacuated(dve, key + (1,))

            def moves(key, dst):
                for bt in range(2):
                    b = take(dve, key + (bt,))
                    give(nc.vector.tensor_copy(dst[:, 4 * bt:4 * bt + 4, :], b[:, :].rearrange("p (h t) -> p h t", h=4)),
                         key + (bt,))

            def add_half(half, n, i):
                key = ("CO", half, n, i)
                b = take(dve, key)
                if half:
                    evacuated(dve, ("CO", 0, n, i))
                else:
                    dve.wait_ge(s_x[i], 32)
                xs = x[:, i, 512 * n:512 * n + 512]
                give(TT(xs, xs, b[:, :], ALU.add), key)

            def j4(v):
                return v.rearrange("p (j t) -> p j t", j=4)

            def centre(i):
                key = ("gm", i)
                b = take(dve, key)
                y = yF[:, :, i * P:(i + 1) * P]
                give(TT(y, y, j4(b[:, :]), ALU.subtract), key)
                evacuated(dve, key)
                dve.sem_inc(S("R_centred"), 1)

            def spread_of(i):
                key = ("gs", i)
                b = take(dve, key)
                give(TS(stat[:, 448:456], b[:, 0:8], 1.0 / HD, GN_EPS, ALU.mult, ALU.add), key)
                evacuated(dve, key)
                rsqrt(stat[:, 480:488], stat[:, 448:456], stat[:, 512:520])
                nc.vector.tensor_copy(bxg.rearrange("p (s d) -> p s d", d=64), ap(stat[:, 480:488], [(1, 8), (0, 64)]))\
                    .then_inc(S("R_gx"), 1)

            def finish(i):
                key = ("gb", i)
                b = take(dve, key)
                y = yF[:, :, i * P:(i + 1) * P]
                give(TT(y, y, j4(b[:, :]), ALU.mult), key)
                evacuated(dve, key)
                dve.wait_ge(S("R_bonus"), i + 1)
                for j in range(4):
                    ts = slice(i * P, (i + 1) * P)
                    STT(yF[:, j, ts], yF[:, j, ts], vcol("gnw", j), rF[:, j, ts], ALU.mult, ALU.add)\
                        .then_inc(S("R_y"), 1)

            def bonus(i):
                r = rF[:, :, i * P:(i + 1) * P]
                TT(r, r, ap(vcol("gnb", 0, 4), [(1, 4), (0, P)]), ALU.add).then_inc(S("R_bonus"), 1)

            def gate(i):
                dve.wait_ge(S("R_y"), 4 * i + 4)
                y = yF[:, :, i * P:(i + 1) * P]
                for j in range(4):
                    STT(ap(mixB[:, j, :], [(1, 2), (GR, GW)], 2 * i), y[:, j, :].rearrange("p (r c) -> p r c", r=2), 0.5,
                        Gr[:, j, i * P:(i + 1) * P].rearrange("p (r c) -> p r c", r=2), ALU.mult, ALU.mult)\
                        .then_inc(S("R_done"), 1)

            for i in range(NT):
                for h in range(8):
                    key = ("gr", i, h)
                    b = take(dve, key)
                    TT(AE[:, h, :, :], ap(b[:, 0:P], [(0, 2), (1, P)]), ap(C("a16"), [(P, 2), (1, P)]), ALU.mult)\
                        .then_inc(S("R_gram"), 1)
                    give(TT(B3[:, h, :, :].rearrange("p m t -> p (m t)"), b[:, P:512], C("gram"), ALU.mult), key)
                dve.wait_ge(S("R_gram"), 8 * i + 8)
                TT(Qa[:, :, :], AE[:, :, 0, :], ap(ident, [(0, 8), (1, P)]), ALU.add).then_inc(S("R_q1"), 1)
                if i:
                    centre(i - 1)
                moves(("D2", i), D2)
                if i:
                    spread_of(i - 1)
                dve.wait_ge(S("R_q1"), i + 1)
                plus(("Q2", i), Qb, Qa)
                if i:
                    finish(i - 1)
                plus(("Q3", i), Qa, Qb)
                plus(("Q4", i), Qb, Qa)
                if i < NT - 1:
                    add_half(0, 0, i)
                moves(("K", i), AE[:, :, 0, :])
                plus(("Q5", i), Qa, Qb)
                if i < NT - 1:
                    add_half(0, 1, i)
                if i == 2:
                    gate(0)
                    gate(1)
                if i == 3:
                    gate(2)
                plus(("RR", i), Qb, Qa)
                bonus(i)
                key = ("rho", i)
                b = take(dve, key)
                give(TT(RHO.rearrange("p (j t) -> p j t", j=4), b[:, :].rearrange("p (j t) -> p j t", j=4),
                        AR[:, :, i, 1, :], ALU.add), key)
                for c in range(2):
                    key = ("M", i, c)
                    b = take(dve, key)
                    give(TT(MT[:, c, :, :], b[:, 0:256].rearrange("p (j k) -> p j k", j=4),
                            ap(C("ident64"), [(0, 4), (1, 64)]), ALU.add), key)
                for c in range(2):
                    k = 2 * i + c
                    key = ("St", k)
                    b = take(dve, key)
                    evacuated(dve, ("Bm", i, c))
                    nx = Sst[:, (k + 1) % 4, :]
                    give(TT(nx, b[:, 0:256], Bm[:, c, :], ALU.add), key)
                    evacuated(dve, key)
                    nv = nx.rearrange("p (j v) -> p j v", j=4)
                    TT(nv, nv, ap(PC[:, :, k], [(8, 4), (0, 64)]), ALU.mult).then_inc(S("R_state"), 1)
                    dve.wait_ge(S("R_state"), k + 2)
                key = ("Y2", i)
                b = take(dve, key)
                evacuated(dve, ("Y1", i))
                yi = yF[:, :, i * P:(i + 1) * P]
                give(TT(yi, yi, b[:, :].rearrange("p (j t) -> p j t", j=4), ALU.add), key)

            centre(NT - 1)
            add_half(0, 0, NT - 1)
            spread_of(NT - 1)
            add_half(0, 1, NT - 1)
            finish(NT - 1)
            gate(NT - 1)
            for i in range(NT):
                add_half(1, 0, i)

            def norm_out(i):
                y = rstd_tile("out", 24, i)
                if i == 0:
                    dve.wait_ge(s_gb[1], 16)
                STT(xo[:, i, :], x[:, i, :], y, gb2[:, :], ALU.mult, ALU.mult).then_inc(S("out_ready"), 1)

            for i in range(NT):
                add_half(1, 1, i)
                if i:
                    norm_out(i - 1)
            norm_out(NT - 1)

        @block.gpsimd
        def _(pool):
            pool.dma_start(cst[:, 0:P], A["cst"][:, 0:P]).then_inc(s_ident, 16)
            pool.dma_start(rpb_in[0:16, 0:465], A["a_rpb"][0].rearrange("h a b -> h (a b)")).then_inc(s_rpb, 16)
            pool.wait_ge(s_rpbr, 2)
            pool.dma_start(scratch, rrev).then_inc(s_scr, 16)
            def load_bias(h):
                src = bass.AP(scratch.tensor, h * 1024 + 49, [[1, 16], [64, 8], [1, 512]])
                pool.dma_start(ext[:, h % 2, :], src).then_inc(s_ext[h % 2], 16)

            def lower(n0, n1=None):
                for n in range(n0, (n0 if n1 is None else n1) + 1):
                    if n in splits:
                        pool.wait_ge(s_whi, splits.index(n) + 1)
                        m = halves[n][1][0] * halves[n][1][1]
                        r = raw_slot(n)[:, 0:m]
                        nc.gpsimd.tensor_tensor(rounded(r), r, read_back(high_slot(n)[:, 0:m]), ALU.subtract)\
                            .then_inc(s_wlo, 1)

            def low_half(tag, i, hf, n):
                pool.wait_ge(S("hi_" + tag), n)
                v = tile_of(low[tag], tag, i, hf)
                nc.gpsimd.tensor_tensor(rounded(v), v, read_back(tile_of(hTf, tag, i, hf)), ALU.subtract)\
                    .then_inc(S("lo_" + tag), 1)

            def low_tiles(tag):
                for i in range(3):
                    for hf in range(2):
                        low_half(tag, i, hf, 2 * i + hf + 1)

            def low_pair(l, j):
                pool.wait_ge(S("o_high"), 8 * l + j + 1)
                nc.gpsimd.tensor_tensor(rounded(hT[:, j, :]), hT[:, j, :], read_back(o_high[:, T * j:T * j + T]), ALU.subtract)\
                    .then_inc(S("o_low"), 1)

            def low_embedding(l):
                pool.wait_ge(S("pw_high"), l + 1)
                nc.gpsimd.tensor_tensor(rounded(pw_lo), pw_lo, read_back(pw_hi), ALU.subtract).then_inc(S("pw_low"), 1)

            lower(0)
            low_tiles("norm0")
            for l in range(NT):
                pool.wait_ge(s_x[l], 16)
            pool.dma_start(cst[:, P:], A["cst"][:, P:]).then_inc(s_cst, 16)
            lower(1)
            pool.dma_start(w2[:, 0, :, :], A["cmp_w2_k_2"][0].rearrange("(b p) d -> p b d", p=P)).then_inc(s_small, 16)
            pool.dma_start(w2[:, 1, :, :], A["cmp_w2_v_2"][0].rearrange("(b p) d -> p b d", p=P)).then_inc(s_small, 16)
            pool.dma_start(wa[0:64, :], A["decay_up_2"][0]).then_inc(s_small, 16)
            pool.dma_start(wa[64:128, :], A["iclr_up_2"][0]).then_inc(s_small, 16)
            for i in range(2):
                nc.gpsimd.memset(bias[0:64, i, 256:384], NEG).then_inc(S("bias_edge"), 1)
            pool.wait_ge(s_scr, 16)
            load_bias(0)
            load_bias(1)
            lower(2, HI[("A", 12)])
            pool.wait_ge(s_cst, 16)
            mask = C("nbr")
            for h in range(16):
                if h == 2:
                    lower(HI[("A", 12)] + 1, HI[("AO", 1)])
                pool.wait_ge(s_ext[h % 2], 16 * (h // 2 + 1))
                if h >= 2:
                    evacuated(pool, ("AS", h - 2, 1))
                o = bias[:, h % 2, :]

                def rev(lo, hi, jj):
                    return ap(ext[lo:hi, h % 2, :], [(-1, 32), (-64, 8)], 511 - jj)

                def jk(v, c):
                    return v[:, c:c + 256].rearrange("p (j k) -> p j k", k=8)

                nc.gpsimd.tensor_tensor(jk(o, 0), rev(0, 128, 8), jk(mask, 0), ALU.add).then_inc(s_bias, 1)
                pool.wait_ge(s_bias, 3 * h + 1)
                nc.gpsimd.tensor_tensor(o[0:64, 384:512].rearrange("p (j k) -> p j k", k=8),
                                        ap(ext[0:64, h % 2, :], [(-1, 16), (-64, 8)], 511 - 8),
                                        mask[0:64, 384:512].rearrange("p (j k) -> p j k", k=8), ALU.add).then_inc(s_bias, 1)
                pool.wait_ge(s_bias, 3 * h + 2)
                nc.gpsimd.tensor_tensor(jk(o[64:128], 256), rev(64, 128, 24), jk(mask[64:128], 256), ALU.add)\
                    .then_inc(s_bias, 1)
                pool.wait_ge(s_bias, 3 * h + 3)
                if h + 2 < 16:
                    load_bias(h + 2)
                if h >= 9 and h % 2:
                    low_pair(0, (h - 9) // 2)
            for l in range(2):
                for j in range(4 if l == 0 else 0, 7):
                    low_pair(l, j)
                evacuated(pool, ("AO_" if l == 0 else "BO_", 15))
                src = A["p"][l, 0].rearrange("(r c) d -> c r d", r=GR)
                for i in range(NT):
                    pool.dma_start(p_tm[:, i, :], src[CT * i:CT * i + CT]).then_inc(s_p[l], 16)
                low_pair(l, 7)
                if l == 0:
                    for n, name in enumerate(("b_q_norm", "b_k_norm")):
                        pool.dma_start(gqk[:, 64 * n:64 * n + 64], bass.AP(A[name].tensor, 0, [[0, P], [1, 64]]))\
                            .then_inc(S("gqk_loaded"), 16)
                else:
                    pool.dma_start(gb[:, :], bass.AP(A["final_norm_g"].tensor, 0, [[0, P], [1, D]]))\
                        .then_inc(s_gb[0], 16)
                low_embedding(l)
                a = HI[("AO" if l == 0 else "BO", 2)]
                lower(a, HI[("PG", l, 0)])
                low_tiles(f"ple{l}")
                if l == 0:
                    lower(HI[("PG", 0, 1)], HI[("B", 0)])
                    low_tiles("norm1")
                    lower(HI[("B", 1)], HI[("BO", 1)])
                else:
                    lower(HI[("PG", 1, 1)], HI["Ckv"])
                    for hf, i in ((0, 0), (0, 3), (1, 0)):
                        low_half("norm2", i, hf, 4 * hf + i + 1)
                    lower(HI["Csel"])
            nc.gpsimd.memset(kcz[:, :, :, :], 0.0).then_inc(S("C_clear"), 1)
            nc.gpsimd.memset(vcz[:, :, :, :], 0.0).then_inc(S("C_clear"), 1)
            lower(HI[("Cq", 0)])
            nc.gpsimd.memset(kz[:, :, :, :, :], 0.0).then_inc(S("C_clear"), 1)
            lower(HI[("Cq", 1)], HI[("R", 2)])
            for m, s in enumerate(RORD):
                if s % 2 == 0 and s != 12:
                    lower(HI[("R", s // 2)] + 1)
                evacuated(pool, ("R", s))
                if m >= 2:
                    pool.wait_ge(S("R_mix"), m - 1)
                nc.gpsimd.tensor_tensor(dif[:, m % 2, :], raw[:, m % 3, 0:512], raw[:, m % 3, 1:513], ALU.subtract)\
                    .then_inc(S("R_dif"), 1)
            lower(HI[("Rg", 1)])
            pool.wait_ge(S("R_done"), 4 * NT)
            pool.dma_start(gb2[:, :], bass.AP(A["final_g_2"].tensor, 0, [[0, P], [1, D]])).then_inc(s_gb[1], 16)

        @block.sync
        def _(sp):
            for l in (1, 2):
                sp.dma_start(x[:, l, :], A["x"][0].rearrange("(r c) d -> c r d", r=GR)[CT * l:CT * l + CT])\
                  .then_inc(s_x[l], 16)
            for n, (src, (k, m)) in enumerate(halves):
                if n == 1:
                    for l in range(NT):
                        sp.wait_ge(s_x[l], 16)
                if n >= NRAW:
                    sp.wait_ge(filled, half_last[n - NRAW] + 1)
                dst = raw_slot(n)[:, 0:k * m].rearrange("p (k m) -> p k m", k=k)
                sp.dma_start(dst, src).then_inc(raw_loaded[n % NRAW], 16)
                if n == HI[("Cq", 1)]:
                    for i in range(NT):
                        sp.wait_ge(S("x_fin"), i + 1)
                        sp.dma_start(x_kept[i], x[:, i, :]).then_inc(s_kept[i // 2], 16)
                for l, tag in enumerate(("AO", "BO")):
                    if n == HI[(tag, 3)]:
                        evacuated(sp, (tag + "_", 15))
                        sp.dma_start(pw_lo.rearrange("p (k m) -> p k m", k=2), cols(A["ple_w_proj"][l], 0, D))\
                            .then_inc(s_pp[l], 16)
            sp.wait_ge(filled, half_last[HI[("Rg", 1)]] + 1)
            for i in range(2):
                sp.wait_ge(s_kept[i], 16 * 2)
            for i in range(NT):
                sp.dma_start(x[:, i, :], x_kept[i]).then_inc(s_x[i], 16)
            o = out[0].rearrange("(r c) d -> c r d", r=GR)
            for i in range(NT):
                sp.wait_ge(S("out_ready"), i + 1)
                sp.dma_start(o[CT * i:CT * i + CT], xo[:, i, :]).then_inc(s_out, 16)
            sp.wait_ge(s_out, 16 * NT)


NAMES = ("x p norm_g a_w_in a_rpb a_w_out b_w_in b_q_norm b_k_norm b_w_out ple_norm_g ple_w_gate ple_w_proj "
         "final_norm_g norm_g_2 w_in_2 cmp_pos_k_2 cmp_w1_k_2 cmp_w2_k_2 cmp_pos_v_2 cmp_w1_v_2 cmp_w2_v_2 "
         "shift_mu_2 decay_w0_2 decay_up_2 iclr_a0_2 iclr_up_2 k_k_2 k_a_2 r_k_2 gn_w_2 gn_b_2 w_out_2 "
         "final_g_2").split()


def kernel(**inputs):
    import numpy as _np
    import concourse.bacc as _bacc
    from concourse import mybir as _mybir
    from concourse.bass_utils import run_bass_kernel_spmd as _run

    nc = _bacc.Bacc("TRN2", target_bir_lowering=False, num_devices=1)
    arrays, aps = {}, {}
    for name in NAMES:
        a = _np.ascontiguousarray(inputs[name])
        arrays[f"in_{name}"] = a
        aps[name] = nc.dram_tensor(f"in_{name}", a.shape, _mybir.dt.from_np(a.dtype), kind="ExternalInput").ap()
    arrays["in_cst"] = CST
    aps["cst"] = nc.dram_tensor("in_cst", CST.shape, _mybir.dt.float32, kind="ExternalInput").ap()
    out = nc.dram_tensor("out_0", (1, T, D), _mybir.dt.float32, kind="ExternalOutput").ap()
    program(nc, aps, out)
    r = _run(nc, [arrays], core_ids=[0])
    return r.results[0]["out_0"]
```
